# Optimizing a Trainium2 kernel written in Bass

```python
import jax
import jax.numpy as jnp
from jax import lax
import numpy as np
import math
import jax, jax.numpy as jnp

D_MODEL = 2048
BATCH = 1
SEQ = 256
DEPTH = 1

MIX_WIDTH = D_MODEL
RWKV_WIDTH = MIX_WIDTH // 2
RWKV_HEAD = 64
RWKV_HEADS = RWKV_WIDTH // RWKV_HEAD
DECAY_LORA = 64
AAA_LORA = 64
GATE_LORA = 160
RWKV_LN_EPS = 64e-5
ATT_WIDTH = MIX_WIDTH - RWKV_WIDTH
ATT_HEAD = 128
ATT_HEADS = ATT_WIDTH // ATT_HEAD
ATT_KV_HEADS = 2
IDX_HEADS = 16
IDX_HEAD = 64
TOPK_MAX = 256
Q_BLOCK = 128
ROPE_THETA = 500000.0
N_MEM = 256
CROSS_HEADS = 4
CROSS_HEAD = 128
D_FF = 4 * D_MODEL
NORM_EPS = 1e-5

RWKV_SPLITS = (RWKV_WIDTH, RWKV_WIDTH, RWKV_WIDTH, DECAY_LORA, AAA_LORA, GATE_LORA)
ATT_SPLITS = (ATT_WIDTH, ATT_KV_HEADS * ATT_HEAD, ATT_KV_HEADS * ATT_HEAD,
              IDX_HEADS * IDX_HEAD, IDX_HEAD, IDX_HEADS)
RWKV_COLS = sum(RWKV_SPLITS)
ATT_COLS = sum(ATT_SPLITS)
IN_COLS = RWKV_COLS + ATT_COLS


def split_cols(t, sizes):
    out, start = [], 0
    for s in sizes:
        out.append(t[..., start:start + s])
        start += s
    return out

def rms_norm(x, g):
    xf = x.astype(jnp.float32)
    y = xf * lax.rsqrt(jnp.mean(xf * xf, axis=-1, keepdims=True) + NORM_EPS)
    return (y * g.astype(jnp.float32)).astype(x.dtype)

def partial_rope(x, pos):
    dh = x.shape[-1]
    rot = dh // 4
    half = rot // 2
    inv_freq = ROPE_THETA ** (-jnp.arange(half, dtype=jnp.float32) / half)
    ang = pos.astype(jnp.float32)[..., None] * inv_freq
    cos = jnp.cos(ang)[:, :, None, :]
    sin = jnp.sin(ang)[:, :, None, :]
    xr = x[..., :rot].astype(jnp.float32)
    x1, x2 = xr[..., :half], xr[..., half:]
    rotated = jnp.concatenate([x1 * cos - x2 * sin, x2 * cos + x1 * sin], axis=-1).astype(x.dtype)
    return jnp.concatenate([rotated, x[..., rot:]], axis=-1)

def rwkv7_group(p, mu, w0, w_decay_up, a0, a_up, g_up, k_k, k_a, r_k, lnx_w, lnx_b):
    B, S, _ = p.shape
    H, N = RWKV_HEADS, RWKV_HEAD
    f32 = jnp.float32
    prev = jnp.pad(p, ((0, 0), (1, 0), (0, 0)))[:, :-1]
    p = p + (prev - p) * mu
    r, k, v, xw, xa, xg = split_cols(p, RWKV_SPLITS)
    w = -jax.nn.softplus(-(w0 + jnp.tanh(xw) @ w_decay_up)) - 0.5
    decay = jnp.exp(-jnp.exp(w.astype(f32)))
    a = jax.nn.sigmoid(a0 + xa @ a_up)
    g = jax.nn.sigmoid(xg) @ g_up
    heads = lambda t: t.astype(f32).reshape(B, S, H, N)
    kk = heads(k * k_k)
    kk = kk / jnp.maximum(jnp.sqrt(jnp.sum(kk * kk, axis=-1, keepdims=True)), 1e-12)
    k = k * (1.0 + (a - 1.0) * k_a)
    r4, k4, v4, a4, w4 = heads(r), heads(k), heads(v), heads(a), decay.reshape(B, S, H, N)

    def step(state, inp):
        r_t, w_t, k_t, v_t, kk_t, a_t = inp
        sa = jnp.einsum('bhvk,bhk->bhv', state, -kk_t)
        state = (state * w_t[:, :, None, :]
                 + sa[..., None] * (kk_t * a_t)[:, :, None, :]
                 + v_t[..., None] * k_t[:, :, None, :])
        return state, jnp.einsum('bhvk,bhk->bhv', state, r_t)

    tm = lambda t: jnp.swapaxes(t, 0, 1)
    s0 = jnp.zeros((B, H, N, N), f32)
    _, y = lax.scan(step, s0, (tm(r4), tm(w4), tm(k4), tm(v4), tm(kk), tm(a4)))
    y = tm(y)
    mean = jnp.mean(y, axis=-1, keepdims=True)
    var = jnp.mean(jnp.square(y - mean), axis=-1, keepdims=True)
    yn = ((y - mean) * lax.rsqrt(var + RWKV_LN_EPS)).reshape(B, S, RWKV_WIDTH)
    yn = yn * lnx_w.astype(f32) + lnx_b.astype(f32)
    bonus = (jnp.sum(r4 * k4 * r_k.astype(f32), axis=-1, keepdims=True) * v4).reshape(B, S, RWKV_WIDTH)
    return ((yn + bonus) * g.astype(f32)).astype(p.dtype)

def dsa_group(p, pos):
    B, S, _ = p.shape
    f32 = jnp.float32
    G = ATT_HEADS // ATT_KV_HEADS
    q, k, v, qi, ki, wi = split_cols(p, ATT_SPLITS)
    q = partial_rope(q.reshape(B, S, ATT_HEADS, ATT_HEAD), pos)
    k = partial_rope(k.reshape(B, S, ATT_KV_HEADS, ATT_HEAD), pos)
    v = v.reshape(B, S, ATT_KV_HEADS, ATT_HEAD)
    qi = partial_rope(qi.reshape(B, S, IDX_HEADS, IDX_HEAD), pos)
    ki = partial_rope(ki.reshape(B, S, 1, IDX_HEAD), pos)[:, :, 0].astype(f32)
    wi = wi.astype(f32) * (IDX_HEADS ** -0.5 * IDX_HEAD ** -0.5)
    n_sel = min(TOPK_MAX, S // 4)
    nblk = S // Q_BLOCK
    key_pos = jnp.arange(S)
    gather = jax.vmap(lambda t, i: t[i])

    def to_blocks(t):
        return jnp.swapaxes(t.reshape((B, nblk, Q_BLOCK) + t.shape[2:]), 0, 1)

    def block(args):
        bi, qb, qib, wib = args
        q_pos = bi * Q_BLOCK + jnp.arange(Q_BLOCK)
        rel = jax.nn.relu(jnp.einsum('bqhd,bsd->bqhs', qib.astype(f32), ki))
        score = jnp.einsum('bqhs,bqh->bqs', rel, wib)
        causal = key_pos[None, :] <= q_pos[:, None]
        score = jnp.where(causal[None], score, -1e30)
        _, idx = lax.top_k(score, n_sel)
        valid = idx <= q_pos[None, :, None]
        kg = gather(k, idx)
        vg = gather(v, idx)
        qg = qb.reshape(B, Q_BLOCK, ATT_KV_HEADS, G, ATT_HEAD)
        s = jnp.einsum('bqhgd,bqkhd->bqhgk', qg, kg).astype(f32) * (ATT_HEAD ** -0.5)
        s = jnp.where(valid[:, :, None, None, :], s, -jnp.inf)
        prob = jax.nn.softmax(s, axis=-1).astype(vg.dtype)
        o = jnp.einsum('bqhgk,bqkhd->bqhgd', prob, vg)
        return o.reshape(B, Q_BLOCK, ATT_WIDTH)

    out = lax.map(block, (jnp.arange(nblk), to_blocks(q), to_blocks(qi), to_blocks(wi)))
    return jnp.swapaxes(out, 0, 1).reshape(B, S, ATT_WIDTH)

def memory_cross_attention(hn, mem_n, w_q, w_kv, w_o):
    B, S, _ = hn.shape
    M = mem_n.shape[1]
    q = (hn @ w_q).reshape(B, S, CROSS_HEADS, CROSS_HEAD)
    k, v = split_cols(mem_n @ w_kv, (CROSS_HEADS * CROSS_HEAD, CROSS_HEADS * CROSS_HEAD))
    k = k.reshape(B, M, CROSS_HEADS, CROSS_HEAD)
    v = v.reshape(B, M, CROSS_HEADS, CROSS_HEAD)
    s = jnp.einsum('bshd,bmhd->bhsm', q, k).astype(jnp.float32) * (CROSS_HEAD ** -0.5)
    prob = jax.nn.softmax(s, axis=-1).astype(v.dtype)
    o = jnp.einsum('bhsm,bmhd->bshd', prob, v).reshape(B, S, CROSS_HEADS * CROSS_HEAD)
    return o @ w_o

def first_inputs(seed: int = 0) -> dict:
    key = jax.random.key(seed)
    ks = jax.random.split(key, 32)
    f32 = jnp.float32
    L = DEPTH

    def dense(k, fan_in, shape):
        return jax.random.normal(k, shape, f32) * fan_in ** -0.5

    def gain(k, shape):
        return 1.0 + 0.02 * jax.random.normal(k, shape, f32)

    return {
        'x': jax.random.normal(ks[0], (BATCH, SEQ, D_MODEL), f32),
        'mem': jax.random.normal(ks[1], (BATCH, N_MEM, D_MODEL), f32),
        'positions': jnp.tile(jnp.arange(SEQ, dtype=jnp.int32)[None, :], (BATCH, 1)),
        'norm_mix': gain(ks[2], (L, D_MODEL)),
        'w_in': dense(ks[3], D_MODEL, (L, D_MODEL, IN_COLS)),
        'rwkv_mu': jax.random.uniform(ks[4], (L, RWKV_COLS), f32),
        'w_decay0': jax.random.uniform(ks[5], (L, RWKV_WIDTH), f32, -6.0, 1.0),
        'w_decay_up': dense(ks[6], DECAY_LORA, (L, DECAY_LORA, RWKV_WIDTH)),
        'a0': 0.1 * jax.random.normal(ks[7], (L, RWKV_WIDTH), f32),
        'a_up': dense(ks[8], AAA_LORA, (L, AAA_LORA, RWKV_WIDTH)),
        'g_up': dense(ks[9], GATE_LORA, (L, GATE_LORA, RWKV_WIDTH)),
        'k_k': 0.85 + 0.05 * jax.random.normal(ks[10], (L, RWKV_WIDTH), f32),
        'k_a': 1.0 + 0.05 * jax.random.normal(ks[11], (L, RWKV_WIDTH), f32),
        'r_k': 0.1 * jax.random.normal(ks[12], (L, RWKV_HEADS, RWKV_HEAD), f32),
        'lnx_w': gain(ks[13], (L, RWKV_WIDTH)),
        'lnx_b': 0.02 * jax.random.normal(ks[14], (L, RWKV_WIDTH), f32),
        'w_mix_out': dense(ks[15], MIX_WIDTH, (L, MIX_WIDTH, D_MODEL)),
        'norm_cross': gain(ks[16], (L, D_MODEL)),
        'norm_mem': gain(ks[17], (L, D_MODEL)),
        'w_q_cross': dense(ks[18], D_MODEL, (L, D_MODEL, CROSS_HEADS * CROSS_HEAD)),
        'w_kv_cross': dense(ks[19], D_MODEL, (L, D_MODEL, 2 * CROSS_HEADS * CROSS_HEAD)),
        'w_o_cross': dense(ks[20], CROSS_HEADS * CROSS_HEAD, (L, CROSS_HEADS * CROSS_HEAD, D_MODEL)),
        'norm_mlp': gain(ks[21], (L, D_MODEL)),
        'w_up': dense(ks[22], D_MODEL, (L, D_MODEL, D_FF)),
        'w_down': dense(ks[23], D_FF, (L, D_FF, D_MODEL)),
        'norm_final': gain(ks[24], (D_MODEL,)),
    }

def first_block(x, mem, positions, norm_mix, w_in, rwkv_mu, w_decay0, w_decay_up, a0, a_up, g_up,
              k_k, k_a, r_k, lnx_w, lnx_b, w_mix_out, norm_cross, norm_mem, w_q_cross,
              w_kv_cross, w_o_cross, norm_mlp, w_up, w_down, norm_final):
    h = x
    for l in range(DEPTH):
        p = rms_norm(h, norm_mix[l]) @ w_in[l]
        y_rwkv = rwkv7_group(p[..., :RWKV_COLS], rwkv_mu[l], w_decay0[l], w_decay_up[l], a0[l],
                             a_up[l], g_up[l], k_k[l], k_a[l], r_k[l], lnx_w[l], lnx_b[l])
        y_att = dsa_group(p[..., RWKV_COLS:], positions)
        h = h + jnp.concatenate([y_rwkv, y_att], axis=-1) @ w_mix_out[l]
        h = h + memory_cross_attention(rms_norm(h, norm_cross[l]), rms_norm(mem, norm_mem[l]),
                                       w_q_cross[l], w_kv_cross[l], w_o_cross[l])
        u = rms_norm(h, norm_mlp[l]) @ w_up[l]
        h = h + jnp.square(jax.nn.relu(u)) @ w_down[l]
    return rms_norm(h, norm_final)


CHUNK = 64
N_META = 16
HEAD_DIM = 128
SB_HEADS = 8
FOX_HEADS = 8
SB_WIDTH = SB_HEADS * HEAD_DIM
FOX_WIDTH = FOX_HEADS * HEAD_DIM
MIX_WIDTH_2 = SB_WIDTH + FOX_WIDTH
C_IN = 3 * SB_WIDTH + 4 * FOX_WIDTH + FOX_HEADS
PEER_HEADS = 8
PEER_TOPK = 16
N_KEYS = 128
N_EXPERTS = N_KEYS * N_KEYS
D_KEY = 256
PEER_BLOCK = 128
EPS = 1e-6


def rms_norm_2(x, gain):
    xf = x.astype(jnp.float32)
    y = xf * lax.rsqrt(jnp.mean(xf * xf, axis=-1, keepdims=True) + EPS)
    return y.astype(x.dtype) * gain

def to_query_blocks(a):
    b, l = a.shape[:2]
    return jnp.moveaxis(a.reshape((b, l // Q_BLOCK, Q_BLOCK) + a.shape[2:]), 1, 0)

def from_query_blocks(a):
    a = jnp.moveaxis(a, 0, 1)
    b, nb, qb = a.shape[:3]
    return a.reshape(b, nb * qb, -1)

def stick_breaking_attention(q, k, v):
    L = k.shape[1]
    k_pos = jnp.arange(L)
    scale = 1.0 / math.sqrt(HEAD_DIM)
    starts = jnp.arange(L // Q_BLOCK, dtype=jnp.int32) * Q_BLOCK

    def block(args):
        qb, start = args
        q_pos = start + jnp.arange(Q_BLOCK)
        z = jnp.einsum('bqhd,bkhd->bhqk', qb, k).astype(jnp.float32) * scale
        visible = k_pos[None, :] < q_pos[:, None]
        log_1mb = jnp.where(visible, jax.nn.log_sigmoid(-z), 0.0)
        after = lax.cumsum(log_1mb, axis=3, reverse=True) - log_1mb
        w = jnp.where(visible, jnp.exp(jax.nn.log_sigmoid(z) + after), 0.0)
        return jnp.einsum('bhqk,bkhd->bqhd', w.astype(v.dtype), v)

    out = lax.map(block, (to_query_blocks(q), starts))
    return from_query_blocks(out)

def forgetting_attention(q, k, v, log_f):
    L = k.shape[1]
    k_pos = jnp.arange(L)
    scale = 1.0 / math.sqrt(HEAD_DIM)
    cum_f = lax.cumsum(log_f, axis=1)
    cum_f_k = jnp.transpose(cum_f, (0, 2, 1))
    starts = jnp.arange(L // Q_BLOCK, dtype=jnp.int32) * Q_BLOCK

    def block(args):
        qb, fq, start = args
        q_pos = start + jnp.arange(Q_BLOCK)
        z = jnp.einsum('bqhd,bkhd->bhqk', qb, k).astype(jnp.float32) * scale
        logits = z + jnp.transpose(fq, (0, 2, 1))[..., None] - cum_f_k[:, :, None, :]
        visible = k_pos[None, :] <= q_pos[:, None]
        p = jax.nn.softmax(jnp.where(visible, logits, -jnp.inf), axis=-1)
        return jnp.einsum('bhqk,bkhd->bqhd', p.astype(v.dtype), v)

    out = lax.map(block, (to_query_blocks(q), to_query_blocks(cum_f), starts))
    return from_query_blocks(out)

def mixer_sublayer(h, w_in, b_forget, fox_q_gain, fox_k_gain, sb_out_gain, fox_out_gain, w_out):
    B, L, _ = h.shape
    proj = h @ w_in
    s3 = 3 * SB_WIDTH
    sb_q, sb_k, sb_v, fq, fk, fv, fgate, flogit = jnp.split(
        proj,
        [SB_WIDTH, 2 * SB_WIDTH, s3, s3 + FOX_WIDTH, s3 + 2 * FOX_WIDTH,
         s3 + 3 * FOX_WIDTH, s3 + 4 * FOX_WIDTH],
        axis=-1)

    def heads(a, n):
        return a.reshape(B, L, n, HEAD_DIM)

    sb = stick_breaking_attention(heads(sb_q, SB_HEADS), heads(sb_k, SB_HEADS), heads(sb_v, SB_HEADS))
    log_f = jax.nn.log_sigmoid((flogit + b_forget).astype(jnp.float32))
    fox = forgetting_attention(rms_norm_2(heads(fq, FOX_HEADS), fox_q_gain),
                               rms_norm_2(heads(fk, FOX_HEADS), fox_k_gain),
                               heads(fv, FOX_HEADS), log_f)
    merged = jnp.concatenate(
        [rms_norm_2(sb, sb_out_gain),
         rms_norm_2(fox, fox_out_gain) * jax.nn.sigmoid(fgate)], axis=-1)
    return merged @ w_out

def peer_sublayer(h, w_query, sub_keys, u, v):
    B, L, D = h.shape
    blocks = h.reshape(-1, PEER_BLOCK, D)

    def block(hb):
        q = (hb @ w_query).reshape(PEER_BLOCK, PEER_HEADS, 2, D_KEY // 2)
        s = jnp.einsum('thpc,hpnc->thpn', q, sub_keys).astype(jnp.float32)
        top_s, top_i = lax.top_k(s, PEER_TOPK)
        cand_s = (top_s[:, :, 0, :, None] + top_s[:, :, 1, None, :]).reshape(PEER_BLOCK, PEER_HEADS, -1)
        cand_i = (top_i[:, :, 0, :, None] * N_KEYS + top_i[:, :, 1, None, :]).reshape(PEER_BLOCK, PEER_HEADS, -1)
        best_s, best_j = lax.top_k(cand_s, PEER_TOPK)
        idx = jnp.take_along_axis(cand_i, best_j, axis=-1)
        g = jax.nn.softmax(best_s, axis=-1)
        u_sel = jnp.take(u, idx, axis=0)
        a = jax.nn.gelu(jnp.einsum('thkd,td->thk', u_sel, hb), approximate=False)
        v_sel = jnp.take(v, idx, axis=0)
        return jnp.einsum('thk,thkd->td', (g * a).astype(hb.dtype), v_sel)

    return lax.map(block, blocks).reshape(B, L, D)

def second_inputs(seed: int = 0) -> dict:
    key = jax.random.key(seed)
    ks = jax.random.split(key, 15)
    f32 = jnp.float32
    nrm = lambda k, shape, s: jax.random.normal(k, shape, f32) * s
    gain = lambda k, shape: 1.0 + 0.02 * jax.random.normal(k, shape, f32)
    return {
        "x": nrm(ks[0], (BATCH, SEQ, D_MODEL), 1.0),
        "meta_tokens": nrm(ks[1], (N_META, D_MODEL), 1.0),
        "norm_mix": gain(ks[2], (DEPTH, D_MODEL)),
        "w_in": nrm(ks[3], (DEPTH, D_MODEL, C_IN), D_MODEL ** -0.5),
        "b_forget": jax.random.uniform(ks[4], (DEPTH, FOX_HEADS), f32, 1.0, 4.0),
        "fox_q_gain": gain(ks[5], (DEPTH, HEAD_DIM)),
        "fox_k_gain": gain(ks[6], (DEPTH, HEAD_DIM)),
        "sb_out_gain": gain(ks[7], (DEPTH, SB_WIDTH)),
        "fox_out_gain": gain(ks[8], (DEPTH, FOX_WIDTH)),
        "w_out": nrm(ks[9], (DEPTH, MIX_WIDTH_2, D_MODEL), MIX_WIDTH_2 ** -0.5),
        "norm_ffn": gain(ks[10], (DEPTH, D_MODEL)),
        "peer_w_query": nrm(ks[11], (DEPTH, D_MODEL, PEER_HEADS * D_KEY), D_MODEL ** -0.5),
        "peer_sub_keys": nrm(ks[12], (DEPTH, PEER_HEADS, 2, N_KEYS, D_KEY // 2), (D_KEY // 2) ** -0.5),
        "peer_u": nrm(ks[13], (DEPTH, N_EXPERTS, D_MODEL), D_MODEL ** -0.5),
        "peer_v": nrm(ks[14], (DEPTH, N_EXPERTS, D_MODEL), PEER_HEADS ** -0.5),
    }

def second_block(x, meta_tokens, norm_mix, w_in, b_forget, fox_q_gain, fox_k_gain,
              sb_out_gain, fox_out_gain, w_out, norm_ffn, peer_w_query, peer_sub_keys,
              peer_u, peer_v):
    B, S, D = x.shape
    l_pad = ((S + N_META + Q_BLOCK - 1) // Q_BLOCK) * Q_BLOCK
    meta = jnp.broadcast_to(meta_tokens[None].astype(x.dtype), (B, N_META, D))
    pad = jnp.zeros((B, l_pad - S - N_META, D), x.dtype)
    h = jnp.concatenate([meta, x, pad], axis=1)
    for l in range(DEPTH):
        h = h + mixer_sublayer(rms_norm_2(h, norm_mix[l]), w_in[l], b_forget[l],
                               fox_q_gain[l], fox_k_gain[l], sb_out_gain[l],
                               fox_out_gain[l], w_out[l])
        h = h + peer_sublayer(rms_norm_2(h, norm_ffn[l]), peer_w_query[l],
                              peer_sub_keys[l], peer_u[l], peer_v[l])
    return h[:, N_META:N_META + S]


def setup_inputs(seed=0):
    out = dict(first_inputs(seed))
    for name, value in second_inputs(seed + 1).items():
        if name != "x":
            out[name + "_2"] = value
    return out


def reference(
    x, mem, positions, norm_mix, w_in, rwkv_mu, w_decay0, w_decay_up, a0, a_up, g_up, k_k, k_a,
    r_k, lnx_w, lnx_b, w_mix_out, norm_cross, norm_mem, w_q_cross, w_kv_cross, w_o_cross,
    norm_mlp, w_up, w_down, norm_final, meta_tokens_2, norm_mix_2, w_in_2, b_forget_2,
    fox_q_gain_2, fox_k_gain_2, sb_out_gain_2, fox_out_gain_2, w_out_2, norm_ffn_2,
    peer_w_query_2, peer_sub_keys_2, peer_u_2, peer_v_2,
):
    x = first_block(
        x, mem, positions, norm_mix, w_in, rwkv_mu, w_decay0, w_decay_up, a0, a_up, g_up, k_k,
        k_a, r_k, lnx_w, lnx_b, w_mix_out, norm_cross, norm_mem, w_q_cross, w_kv_cross,
        w_o_cross, norm_mlp, w_up, w_down, norm_final,
    )
    return second_block(
        x, meta_tokens_2, norm_mix_2, w_in_2, b_forget_2, fox_q_gain_2, fox_k_gain_2,
        sb_out_gain_2, fox_out_gain_2, w_out_2, norm_ffn_2, peer_w_query_2, peer_sub_keys_2,
        peer_u_2, peer_v_2,
    )


_drawn_inputs = setup_inputs


def setup_inputs(seed=0):
    import zlib

    import numpy as np

    out = dict(_drawn_inputs(seed))
    spreads = {}
    factors = {'lnx_w': 3.428,
     'lnx_b': 3.432,
     'norm_cross': 7.908,
     'norm_mem': 5.568,
     'fox_q_gain_2': 5.643,
     'fox_k_gain_2': 6.148,
     'sb_out_gain_2': 8.11,
     'fox_out_gain_2': 13.262,
     'norm_ffn_2': 7.985}
    for name, (base, spread) in spreads.items():
        noise = np.random.default_rng([zlib.crc32(name.encode()), seed]).standard_normal(out[name].shape)
        drawn = base * np.exp(spread * noise) if base else spread * noise
        out[name] = jnp.asarray(drawn.astype(out[name].dtype))
    for name, factor in factors.items():
        out[name] = (out[name] * factor).astype(out[name].dtype)
    return out
```

```python
import numpy as np
import concourse.bass as bass
from concourse import mybir
from concourse.alu_op_type import AluOpType as ALU
from contextlib import ExitStack

FP32 = mybir.dt.float32
I32 = mybir.dt.int32
U32 = mybir.dt.uint32
ACT = mybir.ActivationFunctionType
AX = mybir.AxisListType.X

P = 128
D = 2048
SEQ = 256
TILES = SEQ // P
META = 16
CTX = META + SEQ
SLABS = D // P
FF = 4 * D
R_W, R_HEAD = 1024, 64
R_HEADS = R_W // R_HEAD
LORA_W, LORA_A, LORA_G = 64, 64, 160
RWKV_COLS = 3 * R_W + LORA_W + LORA_A + LORA_G
A_W, A_HEAD, A_HEADS, A_KV = 1024, 128, 8, 2
I_HEADS, I_HEAD = 16, 64
IN_COLS = RWKV_COLS + A_W + 2 * A_KV * A_HEAD + I_HEADS * I_HEAD + I_HEAD + I_HEADS
TOPK = min(256, SEQ // 4)
C_HEADS, C_HEAD = 4, 128
C_W = C_HEADS * C_HEAD
HEADS2, HEAD2 = 8, 128
W2 = HEADS2 * HEAD2
C_IN = 7 * W2 + HEADS2
E_HEADS, E_TOP, N_KEYS = 8, 16, 128
N_EXPERTS = N_KEYS * N_KEYS
THETA = 500000.0
XW0 = 3 * R_W
XG0 = XW0 + LORA_W + LORA_A
Q0 = RWKV_COLS
K0 = Q0 + A_W
V0 = K0 + A_KV * A_HEAD
QI0 = V0 + A_KV * A_HEAD
KI0 = QI0 + I_HEADS * I_HEAD
WI0 = KI0 + I_HEAD

CHUNK = 512
SLOTS = 8
SLOT_SLABS = 2
NEG = -1.0e30
TAKEN = -3.0e38
E_HALF = 0.6065306597126334
TWO_PI_HI = 6.28125
TWO_PI_LO = 0.0019353071795864769
PI = 3.1415925


class Product:

    def __init__(self, name, w, k, col0, widths, tok, per_body, lo=META, hi=CTX):
        self.name, self.w, self.k, self.col0, self.widths, self.tok = name, w, k, col0, widths, tok
        self.per_body, self.bodies = per_body, len(widths) // per_body
        self.lo, self.hi = lo, hi
        self.tiles = k // (P * SLOT_SLABS)
        self.turns = self.tiles * per_body // SLOTS

    def uses(self, bank):
        if not self.tok:
            return self.per_body
        return sum(bank // 2 == c % 2 for c in range(self.per_body))

    def tile(self, c, j):
        t = c * self.tiles + j
        return t % SLOTS, t // SLOTS


def lay_out(products):
    turn, used = 0, [0] * 4
    for g in products:
        g.turn0, g.used0 = turn, list(used)
        turn += g.turns * g.bodies
        used = [u + g.uses(b) * g.bodies for b, u in enumerate(used)]


class Chain:

    def __init__(self, eng, sem):
        self.eng, self.sem, self.n = eng, sem, 0

    def __call__(self, ins):
        self.n += 1
        ins.then_inc(self.sem, 1)
        self.eng.wait_ge(self.sem, self.n)
        return self.n


def build(nc, A, out):
    with ExitStack() as ctx:
        sems = {}

        def sem(name):
            if name not in sems:
                sems[name] = ctx.enter_context(nc.semaphore(name))
            return sems[name]

        TOTAL = 53120
        arena = ctx.enter_context(nc.sbuf_tensor("arena", [P, TOTAL], FP32))
        ints = ctx.enter_context(nc.sbuf_tensor("ints", [P, 32], I32))
        acc = ctx.enter_context(nc.psum_tensor("acc", [P, 8, CHUNK], FP32))
        top = [0]

        def at(off, *shape):
            n = 1
            for s in shape:
                n *= s
            assert off + n <= TOTAL, (off, n)
            v = arena[:, off:off + n]
            if len(shape) == 2:
                v = v.rearrange("p (a b) -> p a b", a=shape[0])
            if len(shape) == 3:
                v = v.rearrange("p (a b c) -> p a b c", a=shape[0], b=shape[1])
            return v

        def take(*shape):
            n = 1
            for s in shape:
                n *= s
            v = at(top[0], *shape)
            top[0] += n
            return v

        ring = take(SLOTS, SLOT_SLABS, CHUNK)
        h = take(TILES, D)
        ident = take(P)
        tri = take(P)
        upper = take(P)
        upper16 = take(P)
        lower16 = take(P)
        lower_rest = take(P)
        halves = take(2)
        causal = take(TILES, CTX)
        strict = take(TILES, CTX)
        gains = take(7, SLABS)
        small = take(420)
        xT = take(SLABS, CTX)
        base = top[0]

        bank = lambda k: acc[:, k, :]
        ssum, var, rstd = small[:, 0:4], small[:, 4:8], small[:, 8:12]
        rmax, rsum, rinv = small[:, 12:20], small[:, 20:28], small[:, 28:36]
        invf = small[:, 36:52]
        posf = small[:, 52:54]
        posi = ints[:, 0:2]
        m8 = small[:, 54:62]
        kss = small[:, 62:78]
        bonus = small[:, 78:110].rearrange("p (t h) -> p t h", t=TILES)
        decayC = small[:, 110:174].rearrange("p (t h c) -> p t h c", t=TILES, h=R_HEADS)
        sincos = small[:, 174:238].rearrange("p (k t j) -> p k t j", k=2, t=TILES)
        rmean, rvar = small[:, 238:254], small[:, 254:270]
        turns_f = small[:, 270:302].rearrange("p (t j) -> p t j", t=TILES)
        ang = small[:, 302:334].rearrange("p (t j) -> p t j", t=TILES)
        turns_i = ints[:, 0:32].rearrange("p (t j) -> p t j", t=TILES)
        zero_row = small[:, 334:335]
        yst = small[:, 335:367].rearrange("p (k h) -> p k h", k=2)

        zone = base
        p = at(zone, TILES, IN_COLS); zone += TILES * IN_COLS
        ckT = at(zone, C_HEADS, SEQ); zone += C_HEADS * SEQ
        cv = at(zone, TILES, C_W); zone += TILES * C_W
        Z = zone
        mem = at(base, TILES, D)
        memT = at(base + TILES * D, SLABS, SEQ)
        xn = at(Z, TILES, D)
        prev = at(Z + TILES * D, TILES, RWKV_COLS)
        mu = at(Z + TILES * D + TILES * RWKV_COLS, RWKV_COLS)
        z = Z
        key_t = at(z, TILES, R_W); z += TILES * R_W
        beta_t = at(z, TILES, R_W); z += TILES * R_W
        gate = at(z, TILES, R_W); z += TILES * R_W
        state = at(z, R_W); z += R_W
        lnx = at(z, 2, R_W); z += 2 * R_W
        zs = z
        logd = at(z, R_W); z += R_W
        tmp = at(z, R_W); z += R_W
        params = at(z, 4, R_W); z += 4 * R_W
        w0 = gate[:, 1]
        n4 = 4 * P
        zz = zs
        scr = []
        for i in range(26):
            if i < 8:
                scr.append(xT.rearrange("p s c -> p (s c)")[:, i * n4:(i + 1) * n4].rearrange("p (j c) -> p j c", j=4))
            else:
                scr.append(at(zz, 4, P)); zz += n4
        zmax = max(z, zz)
        lora_up = at(TOTAL - 3 * R_W - 3 * SEQ, 3, R_W)
        loraT = at(TOTAL - 3 * SEQ, 3, SEQ)
        assert z <= TOTAL - 3 * R_W - 3 * SEQ and zz <= TOTAL

        z = Z + TILES * R_W
        keyI = at(z, TILES, P); z += TILES * P
        kiT = at(z, SEQ); z += SEQ
        kT = at(z, A_KV, SEQ); z += A_KV * SEQ
        qiT = at(z, TILES, I_HEADS // 2, P); z += SEQ * I_HEADS // 2
        qT = at(z, TILES, A_HEADS, P); z += SEQ * A_HEADS
        rel = at(z, 4, 2, SEQ); z += 8 * SEQ
        score = at(z, TILES, SEQ); z += TILES * SEQ
        left = at(z, SEQ); z += SEQ
        unsel = at(z, TILES, SEQ); z += TILES * SEQ
        rot = at(z, 4, (I_HEADS + 1) * 16); z += 4 * (I_HEADS + 1) * 16
        prob = at(z, 3, 2 * CTX); z += 6 * CTX
        probT = at(z, 2, 4 * P); z += 8 * P
        cqT = at(z, C_HEADS, SEQ); z += C_HEADS * SEQ
        co = at(z, TILES, C_W); z += TILES * C_W
        assert z <= TOTAL, z
        hidT = at(base, FF // P, SEQ)
        xn_mlp = xn
        final_gain = at(Z + TILES * D, D)
        head_gains = small[:, 389:391]
        fbias = small[:, 391:392]
        eps_col = small[:, 392:393]
        nmax = small[:, 367:373].rearrange("p (b j) -> p b j", j=2)
        psums = small[:, 373:381].rearrange("p (b j) -> p b j", j=2)
        pinv = small[:, 381:389].rearrange("p (b j) -> p b j", j=2)
        z = base
        sqT = at(z, HEADS2, SEQ); z += HEADS2 * SEQ
        skT = at(z, HEADS2, CTX); z += HEADS2 * CTX
        sv = at(z, TILES, W2); z += TILES * W2
        sv_meta = at(z, W2); z += W2
        fqT = at(z, HEADS2, SEQ); z += HEADS2 * SEQ
        fkT = at(z, HEADS2, CTX); z += HEADS2 * CTX
        fv = at(z, TILES, W2); z += TILES * W2
        fv_meta = at(z, W2); z += W2
        fgate = at(z, TILES, W2); z += TILES * W2
        vT = at(z, HEADS2, CTX); z += HEADS2 * CTX
        merged = at(z, TILES, D); z += TILES * D
        xn2 = merged
        hmeta = at(z, D); z += D
        ones = at(z, P); z += P
        prob2 = at(z, 3, CTX); z += 3 * CTX
        probT2 = at(z, 2, 3 * P); z += 6 * P
        stick = at(z, 3, 3, CTX); z += 9 * CTX
        seen = at(z, TILES, CTX); z += TILES * CTX
        pick = at(z, HEADS2, P); z += HEADS2 * P
        w_logit = at(z, SLABS, HEADS2); z += SLABS * HEADS2
        logf = at(z, 3, CTX); z += 3 * CTX
        cumf = at(z, TILES, HEADS2); z += TILES * HEADS2
        assert z <= TOTAL, z
        sq_tmp = merged.rearrange("p t d -> p (t d)")
        z = base
        hb = at(z, TILES, D); z += TILES * D
        gain_row = at(z, D); z += D
        pqT = at(z, 2 * E_HEADS, SEQ); z += 2 * E_HEADS * SEQ
        subk = at(z, 2 * E_HEADS, P); z += 2 * E_HEADS * P
        subkT = at(z, 2 * E_HEADS, P); z += 2 * E_HEADS * P
        xn3 = at(z, TILES, D); z += TILES * D
        scores = at(z, TILES, 2 * E_HEADS * N_KEYS); z += TILES * 2 * E_HEADS * N_KEYS
        bufs_z = z
        best1 = at(z, 2 * E_HEADS, E_TOP); z += 2 * E_HEADS * E_TOP
        bestf = at(z, 2 * E_HEADS, E_TOP); z += 2 * E_HEADS * E_TOP
        work1 = at(z, 256); z += 256
        best2 = at(z, TILES, E_HEADS, E_TOP); z += TILES * E_HEADS * E_TOP
        hot = at(z, E_HEADS * E_TOP, E_TOP); z += E_HEADS * E_TOP * E_TOP
        picked = at(z, 3, E_HEADS * E_TOP); z += 3 * E_HEADS * E_TOP
        iota16 = at(z, E_TOP); z += E_TOP
        experts = at(z, TILES * P + 4).bitcast(U32); z += TILES * P + 4
        expert_now = at(z, 16).bitcast(U32); z += 16
        dots_now = at(z, 16); z += 16
        coef_now = at(z, 16); z += 16
        dots = at(z, TILES, P); z += TILES * P
        coef = at(z, TILES, P); z += TILES * P
        esum = at(z, TILES, E_HEADS); z += TILES * E_HEADS
        assert z <= TOTAL, z
        rows_buf = [at(n * D, D) for n in range(4)] + [at(base + 3 * D + n * D, D) for n in range(4)]
        junk = scores[:, 0]

        G = {}
        w = lambda n: A[n][0]
        for g in (
            Product("cross_k", w("w_kv_cross"), D, 0, [CHUNK], False, 1, 0, SEQ),
            Product("cross_v", w("w_kv_cross"), D, C_W, [CHUNK], True, 1),
            Product("in", w("w_in"), D, 0, [CHUNK] * 10, True, 2),
            Product("in_end", w("w_in"), D, 10 * CHUNK, [CHUNK, IN_COLS - 11 * CHUNK], True, 2),
            Product("mix", w("w_mix_out"), D, 0, [CHUNK] * 4, True, 2),
            Product("cross_q", w("w_q_cross"), D, 0, [CHUNK], False, 1),
            Product("cross_o", w("w_o_cross"), C_W, 0, [CHUNK] * 4, True, 4),
            Product("up", w("w_up"), D, 0, [CHUNK] * (FF // CHUNK), False, 1),
            Product("down", w("w_down"), FF, 0, [CHUNK] * 4, True, 2),
            Product("sb_q", w("w_in_2"), D, 0, [CHUNK] * 2, False, 1),
            Product("sb_kv", w("w_in_2"), D, W2, [CHUNK] * 4, False, 1, 0),
            Product("fox_q", w("w_in_2"), D, 3 * W2, [CHUNK] * 2, False, 1),
            Product("fox_kv", w("w_in_2"), D, 4 * W2, [CHUNK] * 4, False, 1, 0),
            Product("fox_gate", w("w_in_2"), D, 6 * W2, [CHUNK] * 2, True, 2),
            Product("out2", w("w_out_2"), D, 0, [CHUNK] * 4, True, 2),
            Product("query", w("peer_w_query_2"), D, 0, [CHUNK] * 4, False, 1),
        ):
            G[g.name] = g
        lay_out(list(G.values()))
        tile_full = [sem(f"tile_full{i}") for i in range(SLOTS)]
        tile_used = [sem(f"tile_used{i}") for i in range(SLOTS)]
        acc_free = [sem(f"acc_free{i}") for i in range(4)]

        def chunk_done(eng, g, c, i=0):
            slot, turn = g.tile(c, g.tiles - 1)
            eng.wait_ge(tile_used[slot], i * g.turns + g.turn0 + turn + 2)

        n_groups = {"mem": 8, "x": 8, "mixed": 8, "cross": 8, "o": 2, "mlp": 8, "meta": 4, "mix2": 8, "merged": 8, "ffn": 8}
        g0, n0 = {}, 0
        for name in n_groups:
            g0[name] = n0
            n0 += n_groups[name]
        norm_tiles = {"mem": 2, "x": 2, "cross": 2, "mlp": 2, "final": 2, "meta": 1, "mix2": 2, "heads2": 4, "ffn": 2}
        norm_no = {name: n for n, name in enumerate(norm_tiles)}
        sums0, xn0 = {}, {}
        n0 = n1 = 0
        for name, k in norm_tiles.items():
            sums0[name], xn0[name] = n0, n1
            n0 += k
            n1 += k if name not in ("final", "heads2") else 0
        s_ss, s_var, s_sd, s_rstd, s_xn = (sem(n) for n in (
            "squares_summed", "variance_ready", "deviation_ready", "scale_ready", "normed_ready"))
        s_tr, s_xT = sem("transposed"), sem("xT_ready")
        s_const, s_vec, s_act, s_pool = sem("const_ready"), sem("vector_step"), sem("scalar_step"), sem("pool_step")
        s_gain, s_x, s_mem = sem("gains_loaded"), sem("x_loaded"), sem("mem_loaded")

        STAGES = [("turned", 1, 1), ("pairs", 1, 0), ("square", 1, 1), ("fourth", 1, 1), ("eighth", 1, 1),
                  ("inverse", 1, 0), ("solve0", 1, 1), ("solve1", 1, 0), ("solve2", 1, 0), ("solve3", 1, 0),
                  ("w_turned", 0, 1), ("sa0", 1, 0), ("state0", 1, 0), ("sa1", 1, 0), ("state1", 1, 0), ("y", 0, 1)]
        stage_no = {s[0]: n for n, s in enumerate(STAGES)}
        g_pe, g_ve, g_ac = sem("group_products"), sem("group_vector"), sem("group_scalar")

        def g_count(pair, name, u, who):
            n = stage_no[name]
            inside = n if who == 0 else sum(s[who] for s in STAGES[:n])
            whole = len(STAGES) if who == 0 else sum(s[who] for s in STAGES)
            return (pair * whole + inside) * 2 + u + 1

        def g_wait(eng, pair, name, u, who):
            if who == 0 or STAGES[stage_no[name]][who]:
                eng.wait_ge((g_pe, g_ve, g_ac)[who], g_count(pair, name, u, who))

        PAIRS = [(t, q) for t in range(TILES) for q in (0, 2)]
        (sAT, sBT, sKT, sRT, sD, sL, sDT, sAK, sRB, sRK, sX, sR, sY0) = range(13)

        def S_(u, n):
            return scr[u * 13 + n]

        def loop(eng, n, body):
            if n == 1:
                body(0)
            else:
                with eng.Fori(0, n) as i:
                    body(i)

        s_shift, s_mixed, s_par, s_lora = sem("shifted_loaded"), sem("mixed"), sem("params_loaded"), sem("lora_loaded")
        s_tanh, s_sig, s_lt, s_lT = sem("tanh_done"), sem("gate_sigmoid"), sem("lora_turned"), sem("loraT_ready")
        s_zd, s_ad, s_gd, s_cd = sem("z_done"), sem("a_done"), sem("g_done"), sem("c_done")
        s_zv, s_av, s_ze, s_ae, s_ld, s_kss, s_ksd = (sem(n) for n in (
            "z_biased", "a_biased", "z_exp", "a_exp", "logd_ready", "kk_summed", "kk_root"))
        s_cp, s_ea, s_en, s_kd, s_ep, s_el, s_gate = (sem(n) for n in (
            "c_before", "exp_before", "exp_minus", "key_scaled", "exp_plus", "elementwise", "gate_copied"))
        s_eg = sem("lora_exp")
        s_rw, s_lnx, s_yv, s_ysd, s_yr, s_out = (sem(n) for n in (
            "rwkv_ln_free", "lnx_loaded", "y_var", "y_sd", "y_rwkv", "out_written"))
        a_S, a_sm, a_pr, a_T, a_PT, a_O, a_done = (sem(n) for n in (
            "scores_done", "max_ready", "prob_ready", "prob_turned", "probT_ready", "output_done", "output_read"))
        M_DSA, M_CROSS, M_TWO = 0, 8, 12
        s_ang, s_trig, s_rope, s_kturn, s_kT2 = (sem(n) for n in ("angle_ready", "sines_ready", "rotated", "keys_turned", "keyT_ready"))
        s_qturn, s_qT2, s_ix, s_rel, s_acc2, s_sel = (sem(n) for n in (
            "queries_turned", "queryT_ready", "index_product", "relu_ready", "index_added", "selected"))
        s_meta, s_c2, s_vt, s_vr, s_lg, s_lf0, s_lf1, s_lf2, s_ct, s_cc = (sem(n) for n in (
            "meta_loaded", "const2_ready", "values_turned", "values_read", "logits_done", "logits_biased", "logits_log",
            "cum_ready", "cum_turned", "cum_column"))
        s_fs, s_fp, s_fr, s_fn, s_l, s_fg, s_mg, s_erow = (sem(n) for n in (
            "fox_squares", "fox_sums", "fox_roots", "fox_normed", "stick_log", "gate2_exp", "merged_ready", "expert_rows_loaded"))
        s_sk, s_skT, s_sp, s_sc, s_bs, s_be, s_ix0, s_dot, s_gelu, s_coef, s_hb = (sem(n) for n in (
            "subkeys_turned", "subkeysT_ready", "key_scores_done", "key_scores_read", "best_shifted", "best_exp",
            "experts_ready", "dots_ready", "gelu_done", "coef_ready", "hb_ready"))
        s_now = sem("experts_staged")
        rows_full = [sem(f"rows_full{n}") for n in range(2)]
        rows_used = [sem(f"rows_used{n}") for n in range(2)]
        s_cq, s_hid, s_fin, s_fgain = sem("cross_q_ready"), sem("hidden_ready"), sem("final_norm"), sem("final_gain_loaded")
        block = ctx.enter_context(nc.Block())

        @block.sync
        def _(sp):
            def stream(g):
                rows = g.w.rearrange("(s p) n -> p s n", p=P)

                def body(i):
                    for c in range(g.per_body):
                        width = g.widths[c]
                        for j in range(g.tiles):
                            slot, turn = g.tile(c, j)
                            sp.wait_ge(tile_used[slot], i * g.turns + g.turn0 + turn + 1)
                            cols = bass.ds(i * (g.per_body * CHUNK) + g.col0 + c * CHUNK, width)
                            sp.dma_start(ring[:, slot, :, 0:width],
                                         rows[:, SLOT_SLABS * j:SLOT_SLABS * (j + 1), cols]
                                         ).then_inc(tile_full[slot], 16)
                loop(sp, g.bodies, body)

            for t in range(TILES):
                sp.dma_start(mem[:, t], A["mem"][0, t * P:(t + 1) * P, :]).then_inc(s_mem, 16)
            for t in range(TILES):
                sp.dma_start(h[:, t], A["x"][0, t * P:(t + 1) * P, :]).then_inc(s_x, 16)
            for g in G.values():
                stream(g)
            for t in range(TILES):
                for k in range(2):
                    sp.wait_ge(rows_used[k], 2 * TILES * P // 8 + 1)
                sp.dma_start(out[0, t * P:(t + 1) * P, :], h[:, t]).then_inc(s_out, 16)
            sp.wait_ge(s_out, 16 * TILES)

        @block.gpsimd
        def _(pool):
            step = Chain(pool, s_pool)

            def keep(m, pattern, base, cm, cmp=ALU.is_ge, fill=0.0):
                return step(pool.affine_select(out=m, in_=m, pattern=pattern, base=base,
                                               channel_multiplier=cm, compare_op=cmp, fill=fill))

            def block_diagonal(m, b):
                v = m.rearrange("p (n b) -> p n b", b=b)
                keep(v, [[-b, P // b], [0, b]], 0, 1)
                keep(v, [[b, P // b], [0, b]], b - 1, -1)

            pool.dma_start(lora_up[0:LORA_W, 0], A["w_decay_up"][0]).then_inc(s_lora, 16)
            pool.dma_start(lora_up[LORA_W:P, 0], A["a_up"][0]).then_inc(s_lora, 16)
            pool.dma_start(lora_up[:, 1], A["g_up"][0, 0:P]).then_inc(s_lora, 16)
            pool.dma_start(lora_up[0:LORA_G - P, 2], A["g_up"][0, P:LORA_G]).then_inc(s_lora, 16)
            step(pool.memset(ident, 0.0))
            keep(ident, [[-1, P]], 0, 1, ALU.not_equal, 1.0)
            for m in (tri, upper, upper16):
                step(pool.memset(m, 1.0))
                keep(m, [[1, P]], 0 if m is tri else -1, -1)
                block_diagonal(m, 16 if m is upper16 else 64)
            for m, b in ((lower16, 16), (lower_rest, 64)):
                step(pool.memset(m, 1.0))
                keep(m, [[-1, P]], -1, 1)
                block_diagonal(m, b)
            step(pool.tensor_tensor(lower_rest, lower_rest, lower16, ALU.subtract))
            step(pool.memset(halves, 1.0))
            keep(halves, [[-64, 2]], 0, 1)
            keep(halves, [[64, 2]], 63, -1)
            for m, off in ((causal, 0), (strict, -1)):
                step(pool.memset(m, 0.0))
                for t in range(TILES):
                    keep(m[:, t, META:CTX], [[-1, SEQ]], t * P + off, 1, fill=NEG)
            pool.memset(zero_row, 0.0).then_inc(s_const, 1)

            pool.dma_start(mu, A["rwkv_mu"][0].partition_broadcast(P)).then_inc(s_shift, 16)
            step(pool.memset(prev[0:1, 0], 0.0))
            gi = G["in"]
            for k in range(4):
                pool.wait_ge(acc_free[k], gi.used0[k] + 1 + 4)
            for t in range(TILES):
                pool.dma_start(prev[1:P, t], p[0:P - 1, t, 0:RWKV_COLS]).then_inc(s_shift, 16)
            pool.dma_start(prev[0:1, 1], p[P - 1:P, 0, 0:RWKV_COLS]).then_inc(s_shift, 16)
            pool.wait_ge(s_mixed, TILES)
            pool.dma_start(w0, A["w_decay0"][0].partition_broadcast(P)).then_inc(s_par, 16)
            for n, name in enumerate(("a0", "k_k", "k_a")):
                pool.dma_start(params[:, n], A[name][0].partition_broadcast(P)).then_inc(s_par, 16)
            pool.dma_start(params[:, 3], A["r_k"][0].rearrange("h n -> (h n)").partition_broadcast(P)).then_inc(s_par, 16)
            pool.wait_ge(s_rw, 1)
            pool.dma_start(lnx[:, 0], A["lnx_w"][0].partition_broadcast(P)).then_inc(s_lnx, 16)
            pool.dma_start(lnx[:, 1], A["lnx_b"][0].partition_broadcast(P)).then_inc(s_lnx, 16)

            for k in range(4):
                pool.wait_ge(acc_free[k], G["sb_q"].used0[k] + 1)
            pool.dma_start(hmeta[0:META], A["meta_tokens_2"]).then_inc(s_meta, 16)
            pool.dma_start(w_logit, A["w_in_2"][0].rearrange("(s p) n -> p s n", p=P)[:, :, 7 * W2:C_IN]).then_inc(s_meta, 16)
            step(pool.memset(pick[0:HEADS2], 0.0))
            keep(pick[0:HEADS2], [[-1, HEADS2], [0, P]], 0, 1, ALU.not_equal, 1.0)
            step(pool.memset(eps_col, 1e-6))
            pool.memset(ones, 1.0).then_inc(s_c2, 1)
            zero4 = zero_row.bitcast(U32).to_broadcast([P, 4])
            now = lambda n: expert_now[:, 4 * (n % 4):4 * (n % 4) + 4]
            for k in range(2):
                pool.sem_inc(rows_used[k], 1)
            pool.wait_ge(s_ix0, TILES + 1)
            pool.tensor_tensor(now(0), experts[:, 0:4], zero4, ALU.add).then_inc(s_now, 1)
            per = TILES * P // 16
            for phase, table in enumerate((A["peer_u_2"][0], A["peer_v_2"][0])):
                with pool.Fori(0, per) as i:
                    for n in range(4):
                        pool.wait_ge(rows_used[n % 2], i * 2 + (phase * per * 2 + n // 2 + 1))
                        pool.wait_ge(s_now, i * 4 + (phase * per * 4 + n + 1))
                        pool.tensor_tensor(now(n + 1), experts[:, bass.ds(i * 16 + 4 * (n + 1), 4)], zero4, ALU.add
                                           ).then_inc(s_now, 1)
                        for j in range(4):
                            pool.indirect_dma_start(
                                out=rows_buf[4 * (n % 2) + j], out_offset=None, in_=table,
                                in_offset=bass.IndirectOffsetOnAxis(ap=now(n)[:, j:j + 1], axis=0)
                            ).then_inc(rows_full[n % 2], 16)

        @block.scalar
        def _(act):
            step = Chain(act, s_act)
            for dst, name in [(gains[:, 0], "norm_mem"), (gains[:, 1], "norm_mix"), (gains[:, 2], "norm_cross"),
                              (gains[:, 3], "norm_mlp"), (gains[:, 4], "norm_mix_2"), (gains[:, 5, 0:8], "sb_out_gain_2"),
                              (gains[:, 5, 8:16], "fox_out_gain_2"), (gains[:, 6], "norm_ffn_2"),
                              (head_gains[:, 0:1], "fox_q_gain_2"), (head_gains[:, 1:2], "fox_k_gain_2")]:
                act.dma_start(dst, A[name][0].rearrange("(s p) -> p s", p=P), allow_slow_non_contiguous=True).then_inc(s_gain, 16)
            act.dma_start(fbias[0:HEADS2], A["b_forget_2"].rearrange("l h -> h l"), allow_slow_non_contiguous=True).then_inc(s_gain, 16)
            act.dma_start(posi, A["positions"][0].rearrange("(t p) -> p t", p=P), allow_slow_non_contiguous=True).then_inc(s_gain, 16)

            def norm_rows(name, src, rows=P, xn=xn):
                tiles = norm_tiles[name]
                for t in range(tiles):
                    act.activation(xn[0:rows, t], src(t), ACT.Square, accum_out=ssum[0:rows, t:t + 1]
                                   ).then_inc(s_ss, 1)
                act.wait_ge(s_var, norm_no[name] + 1)
                act.activation(rstd[0:rows, 0:tiles], var[0:rows, 0:tiles], ACT.Sqrt).then_inc(s_sd, 1)
                act.wait_ge(s_rstd, norm_no[name] + 1)
                if name == "final":
                    return
                act.wait_ge(s_ss, sums0[name] + tiles)
                for t in range(tiles):
                    act.activation(xn[0:rows, t], src(t), ACT.Copy, scale=var[0:rows, t:t + 1]
                                   ).then_inc(s_xn, 1)

            def read_chunk(g, i, c, put):
                chunk_done(act, g, c, i)
                for t in range(TILES):
                    k = 2 * (c % 2) + t
                    put(t, bank(k)[:, 0:g.widths[c]]).then_inc(acc_free[k], 1)

            act.wait_ge(s_mem, 16 * TILES)
            norm_rows("mem", lambda t: mem[:, t])
            act.wait_ge(s_x, 16 * TILES)
            act.wait_ge(s_tr, 8)
            norm_rows("x", lambda t: h[:, t])
            g = G["cross_k"]
            chunk_done(act, g, 0)
            for f in range(4):
                act.activation(ckT[:, f], bank(f)[:, 0:SEQ], ACT.Copy).then_inc(acc_free[f], 1)
            g = G["cross_v"]
            read_chunk(g, 0, 0, lambda t, src: act.activation(cv[:, t], src, ACT.Copy))
            g = G["in"]

            def body(i):
                for c in range(2):
                    read_chunk(g, i, c, lambda t, src: act.activation(
                        p[:, t, bass.ds(i * 2 * CHUNK + c * CHUNK, CHUNK)], src, ACT.Copy))
            loop(act, g.bodies, body)
            g = G["in_end"]
            for c in range(2):
                col = g.col0 + c * CHUNK
                read_chunk(g, 0, c, lambda t, src: act.activation(p[:, t, col:col + g.widths[c]], src, ACT.Copy))

            act.wait_ge(s_mixed, TILES)
            for t in range(TILES):
                xw = p[:, t, XW0:XW0 + LORA_W]
                xg = p[:, t, XG0:XG0 + LORA_G]
                act.activation(xw, xw, ACT.Tanh).then_inc(s_tanh, 1)
                act.activation(xg, xg, ACT.Exp, scale=-1.0).then_inc(s_eg, 1)
            for t in range(TILES):
                act.wait_ge(s_zv, t + 1)
                act.activation(tmp, tmp, ACT.Exp, scale=-1.0).then_inc(s_ze, 1)
                act.wait_ge(s_av, t + 1)
                act.activation(beta_t[:, t], beta_t[:, t], ACT.Exp, scale=-1.0).then_inc(s_ae, 1)
                act.wait_ge(s_gd, t + 1)
                act.activation(gate[:, t], acc[:, 0:2].rearrange("p a b -> p (a b)"), ACT.Copy).then_inc(s_gate, 1)
                act.wait_ge(s_kss, t + 1)
                act.activation(kss, kss, ACT.Sqrt).then_inc(s_ksd, 1)
                act.wait_ge(s_cp, t + 1)
                act.activation(tmp, tmp, ACT.Exp).then_inc(s_ea, 1)
                c_all = acc[:, 2:4].rearrange("p a b -> p (a b)")
                act.activation(logd, c_all, ACT.Exp, scale=-1.0).then_inc(s_en, 1)
                act.activation(decayC[0:R_HEAD, t], bank(6)[0:R_HEAD, 0:2 * R_HEADS].rearrange("p (h c) -> p h c", c=2),
                               ACT.Exp)
                act.wait_ge(s_kd, t + 1)
                act.activation(tmp, c_all, ACT.Exp).then_inc(s_ep, 1)

            for n, (t, q) in enumerate(PAIRS):
                def copy(u, dst, b):
                    return act.activation(dst, b, ACT.Copy)
                for u in range(2):
                    g_wait(act, n, "turned", u, 0)
                    B = 4 * u
                    copy(u, S_(u, sKT)[0:64], bank(B + 2)[0:64].rearrange("p (j c) -> p j c", j=4))
                    copy(u, S_(u, sRT)[0:64], bank(B + 3)[0:64].rearrange("p (j c) -> p j c", j=4)).then_inc(g_ac, 1)
                b4 = lambda k: bank(k).rearrange("p (j c) -> p j c", j=4)
                for u in range(2):
                    B = 4 * u
                    g_wait(act, n, "square", u, 0)
                    copy(u, S_(u, sKT), b4(B + 1))
                    copy(u, S_(u, sBT), b4(B + 2))
                    cols = slice((q + u) * 256, (q + u) * 256 + 256)
                    copy(u, S_(u, sR)[:, :, 0:64], key_t[:, t, cols].rearrange("p (j c) -> p j c", j=4))
                    copy(u, S_(u, sR)[:, :, 64:128], b4(B + 3)[:, :, 0:64]).then_inc(g_ac, 1)
                for u in range(2):
                    B = 4 * u
                    g_wait(act, n, "fourth", u, 0)
                    copy(u, S_(u, sD), b4(B + 1))
                    copy(u, S_(u, sDT), b4(B + 2)).then_inc(g_ac, 1)
                for u in range(2):
                    g_wait(act, n, "eighth", u, 0)
                    copy(u, S_(u, sKT), b4(4 * u + 1)).then_inc(g_ac, 1)
                for u in range(2):
                    g_wait(act, n, "solve0", u, 0)
                    copy(u, S_(u, sY0), b4(4 * u + 1)).then_inc(g_ac, 1)
                for u in range(2):
                    g_wait(act, n, "w_turned", u, 0)
                    copy(u, S_(u, sAT)[0:64], b4(4 * u)[0:64]).then_inc(g_ac, 1)
                for u in range(2):
                    g_wait(act, n, "y", u, 0)
                    cols = slice((q + u) * 256, (q + u) * 256 + 256)
                    copy(u, key_t[:, t, cols].rearrange("p (j c) -> p j c", j=4), b4(4 * u + 1)[:, :, 0:64]).then_inc(g_ac, 1)
            for t in range(TILES):
                act.wait_ge(s_yv, t + 1)
                act.activation(yst[:, 1], yst[:, 1], ACT.Sqrt).then_inc(s_ysd, 1)

            act.wait_ge(s_ang, 1)
            act.activation(sincos[:, 0], ang, ACT.Sin)
            act.wait_ge(s_ang, 2)
            act.activation(sincos[:, 1], turns_f, ACT.Sin).then_inc(s_trig, 1)
            act.wait_ge(s_kturn, 1)
            act.activation(kiT, bank(0)[:, 0:SEQ], ACT.Copy)
            act.activation(kT, bank(1).rearrange("p (k s) -> p k s", k=A_KV), ACT.Copy).then_inc(s_kT2, 1)
            for t in range(TILES):
                act.wait_ge(s_qturn, t + 1)
                act.activation(qiT[:, t], acc[:, 2:4].rearrange("p a (j c) -> p (a j) c", c=P), ACT.Copy)
                act.activation(qT[:, t], acc[:, 4:6].rearrange("p a (j c) -> p (a j) c", c=P), ACT.Copy,
                               scale=A_HEAD ** -0.5).then_inc(s_qT2, 1)
                nk = (t + 1) * P
                for i in range(I_HEADS // 2):
                    m = t * (I_HEADS // 2) + i
                    act.wait_ge(s_ix, m + 1)
                    if m >= 4:
                        act.wait_ge(s_acc2, m - 3)
                    act.activation(rel[:, m % 4, :, 0:nk], acc[:, 6 * (m % 2):6 * (m % 2) + 2, 0:nk],
                                   ACT.Relu).then_inc(s_rel, 1)

            def attend(m0, n, exps, blocks, pre=None):
                for m in range(m0, m0 + n + 2):
                    if pre and m < m0 + n:
                        pre(m)
                    if m0 <= m - 1 < m0 + n:
                        act.wait_ge(a_sm, m)
                        if m - 1 >= 4:
                            act.wait_ge(a_done, m - 4)
                        if m - 1 >= 3:
                            act.wait_ge(a_T, m - 3)
                        exps(m - 1)
                    if m0 <= m - 2:
                        act.wait_ge(a_T, m - 1)
                        if m - 2 >= 2:
                            act.wait_ge(a_O, m - 3)
                        blocks(m - 2)

            def exps_of(src, nk):
                def go(m):
                    for j in range(2):
                        last = act.activation(prob[:, m % 3, j * nk(m):(j + 1) * nk(m)], src(m, j), ACT.Exp,
                                              bias=nmax[:, m % 3, j:j + 1], accum_out=psums[:, m % 4, j:j + 1])
                    last.then_inc(a_pr, 1)
                return go

            def blocks_of(nb):
                def go(m):
                    n = 2 * nb(m) * P
                    act.activation(probT[:, m % 2, 0:n], bank(3 + m % 2)[:, 0:n], ACT.Copy).then_inc(a_PT, 1)
                return go

            tile_of = lambda m: (m - M_DSA) // 4
            nk1 = lambda m: (tile_of(m) + 1) * P
            attend(M_DSA, 8, exps_of(lambda m, j: prob[:, m % 3, j * nk1(m):(j + 1) * nk1(m)], nk1),
                   blocks_of(lambda m: tile_of(m) + 1))

            for k in range(4):
                act.wait_ge(acc_free[k], G["cross_q"].used0[k] + 1)
            norm_rows("cross", lambda t: h[:, t])
            g = G["cross_q"]
            chunk_done(act, g, 0)
            for f in range(4):
                act.activation(cqT[:, f], bank(f)[:, 0:SEQ], ACT.Copy, scale=C_HEAD ** -0.5).then_inc(acc_free[f], 1)
            sc = lambda m, j: bank(m % 3)[:, j * SEQ:(j + 1) * SEQ]
            attend(M_CROSS, 4, exps_of(sc, lambda m: SEQ), blocks_of(lambda m: 2))
            for k in range(4):
                act.wait_ge(acc_free[k], G["up"].used0[k] + 1)
            norm_rows("mlp", lambda t: h[:, t])
            act.dma_start(final_gain, A["norm_final"].partition_broadcast(P)).then_inc(s_fgain, 16)
            g = G["up"]
            hid = hidT.rearrange("p s c -> p (s c)")

            def up_body(i):
                chunk_done(act, g, 0, i)
                for f in range(4):
                    act.activation(hid[:, bass.ds(i * (4 * SEQ) + f * SEQ, SEQ)], bank(f)[:, 0:SEQ], ACT.Relu
                                   ).then_inc(acc_free[f], 1)
                act.drain()
                part = hid[:, bass.ds(i * (4 * SEQ), 4 * SEQ)]
                act.activation(part, part, ACT.Square).then_inc(s_hid, 1)
            loop(act, g.bodies, up_body)
            for k in range(4):
                act.wait_ge(acc_free[k], G["sb_q"].used0[k] + 1)
            norm_rows("final", lambda t: h[:, t])

            act.wait_ge(s_fin, TILES)
            act.wait_ge(s_meta, 32)
            norm_rows("meta", lambda t: hmeta[0:META], META, xn2)
            act.wait_ge(s_tr, g0["meta"] + 4)
            norm_rows("mix2", lambda t: h[:, t], P, xn2)

            def read_T(name, dst, n, first, width, scale=1.0):
                g = G[name]
                flat = dst.rearrange("p h c -> p (h c)")

                def body(i):
                    chunk_done(act, g, 0, i + first)
                    for f in range(4):
                        act.activation(flat[:, bass.ds(i * (4 * width) + f * width, width)], bank(f)[:, 0:width],
                                       ACT.Copy, scale=scale).then_inc(acc_free[f], 1)
                loop(act, n, body)

            def read_values(v, v_meta, n0):
                two = lambda k, rows: acc[0:rows, k:k + 2].rearrange("p a c -> p (a c)")
                for t in range(TILES):
                    act.wait_ge(s_vt, n0 + t + 1)
                    act.activation(v[:, t], two(4 + 2 * t, P), ACT.Copy).then_inc(s_vr, 1)
                act.wait_ge(s_vt, n0 + 3)
                act.activation(v_meta[0:META], two(4, META), ACT.Copy).then_inc(s_vr, 1)

            read_T("sb_q", sqT, 2, 0, SEQ, HEAD2 ** -0.5)
            read_T("sb_kv", skT, 2, 0, CTX)
            read_T("sb_kv", vT, 2, 2, CTX)
            read_T("fox_q", fqT, 2, 0, SEQ)
            read_values(sv, sv_meta, 0)
            read_T("fox_kv", fkT, 2, 0, CTX)
            read_T("fox_kv", vT, 2, 2, CTX)
            for c in range(2):
                read_chunk(G["fox_gate"], 0, c, lambda t, src: act.activation(
                    fgate[:, t, c * CHUNK:(c + 1) * CHUNK], src, ACT.Exp, scale=-1.0))
            act.wait_ge(s_c2, 1)
            act.wait_ge(s_lg, 1)
            step(act.activation(logf[0:HEADS2, 0], bank(4)[0:HEADS2, 0:CTX], ACT.Identity, bias=fbias[0:HEADS2]))
            step(act.activation(logf[0:HEADS2, 1], logf[0:HEADS2, 0], ACT.Abs))
            step(act.activation(logf[0:HEADS2, 1], logf[0:HEADS2, 1], ACT.Exp, scale=-1.0))
            act.activation(logf[0:HEADS2, 1], logf[0:HEADS2, 1], ACT.Ln, bias=1.0).then_inc(s_lf1, 1)
            flat_q, flat_k = (x.rearrange("p h c -> p (h c)") for x in (fqT, fkT))
            FOX_ROUNDS = [(flat_q, 0, 2048), (flat_k, 0, 2048), (flat_k, 2048, HEADS2 * CTX - 2048)]
            for r, (x, c0, n) in enumerate(FOX_ROUNDS):
                act.activation(sq_tmp[:, 0:n], x[:, c0:c0 + n], ACT.Square).then_inc(s_fs, 1)
                act.wait_ge(s_fp, r + 1)
                if r:
                    act.wait_ge(s_fn, r)
                act.activation(sq_tmp[:, D:D + n], acc[:, 4:8].rearrange("p a c -> p (a c)")[:, 0:n], ACT.Sqrt,
                               scale=1.0 / HEAD2, bias=eps_col).then_inc(s_fr, 1)
            read_values(fv, fv_meta, 3)

            of = lambda m: ((m - M_TWO) // 16, (m - M_TWO) % 2, (m - M_TWO) % 16 // 2)
            nk2 = lambda m: META + ((m - M_TWO) // 16 + 1) * P

            def stick_log(m):
                t, fox, hd = of(m)
                if fox:
                    return
                act.wait_ge(a_S, m + 1)
                act.wait_ge(a_sm, m - 2)
                x = stick[:, m % 3, 0, 0:nk2(m)]
                step(act.activation(x, bank(m % 3)[:, 0:nk2(m)], ACT.Abs))
                step(act.activation(x, x, ACT.Exp, scale=-1.0))
                act.activation(x, x, ACT.Ln, bias=1.0).then_inc(s_l, 1)

            def two_exps(m):
                t, fox, hd = of(m)
                pr = prob2[:, m % 3, 0:nk2(m)]
                if fox:
                    act.activation(pr, pr, ACT.Exp, bias=nmax[:, m % 3, 0:1], accum_out=psums[:, m % 4, 0:1]).then_inc(a_pr, 1)
                else:
                    act.activation(pr, stick[:, m % 3, 1, 0:nk2(m)], ACT.Exp).then_inc(a_pr, 1)

            def two_blocks(m):
                n = ((m - M_TWO) // 16 + 1) * P
                src = bank(3 + m % 2)
                act.activation(probT2[0:META, m % 2, 0:P], src[0:META, 0:P], ACT.Copy)
                act.activation(probT2[:, m % 2, P:P + n], src[:, P:P + n], ACT.Copy).then_inc(a_PT, 1)

            attend(M_TWO, 32, two_exps, two_blocks, stick_log)
            act.wait_ge(a_done, M_TWO + 32)
            for t in range(TILES):
                for kind in range(2):
                    act.activation(at(base + (2 * t + kind) * W2, W2), merged[:, t, kind * W2:(kind + 1) * W2], ACT.Square,
                                   accum_out=ssum[:, 2 * t + kind:2 * t + kind + 1]).then_inc(s_ss, 1)
            act.wait_ge(s_var, norm_no["heads2"] + 1)
            act.activation(rstd[:, 0:4], var[:, 0:4], ACT.Sqrt).then_inc(s_sd, 1)
            for k in range(4):
                act.wait_ge(acc_free[k], G["query"].used0[k] + 1)
            act.dma_start(gain_row, A["norm_ffn_2"][0].partition_broadcast(P)).then_inc(s_erow, 16)
            act.dma_start(subk, A["peer_sub_keys_2"][0].rearrange("h q n c -> n (h q) c")).then_inc(s_erow, 16)
            norm_rows("ffn", lambda t: h[:, t], P, xn3)
            for k in range(4):
                act.wait_ge(s_sk, k + 1)
                act.activation(subkT[:, 4 * k:4 * k + 4], bank(4 + k).rearrange("p (j c) -> p j c", j=4), ACT.Copy).then_inc(s_skT, 1)
            read_T("query", pqT, 4, 0, SEQ)
            for t in range(TILES):
                act.wait_ge(s_sp, t + 1)
                act.activation(scores[:, t], acc[:, 4 * t:4 * t + 4].rearrange("p a c -> p (a c)"), ACT.Copy).then_inc(s_sc, 1)
            for t in range(TILES):
                act.wait_ge(s_bs, t + 1)
                act.activation(coef[:, t], coef[:, t], ACT.Exp).then_inc(s_be, 1)
            act.wait_ge(s_dot, TILES)
            act.activation(dots, dots, ACT.Gelu).then_inc(s_gelu, 1)

        @block.vector
        def _(dve):
            step = Chain(dve, s_vec)
            TT, TS, STT, RED = dve.tensor_tensor, dve.tensor_scalar, dve.scalar_tensor_tensor, dve.tensor_reduce

            def norm_scale(name, eps, rows=P, width=D):
                tiles = norm_tiles[name]
                dve.wait_ge(s_ss, sums0[name] + tiles)
                TS(var[0:rows, 0:tiles], ssum[0:rows, 0:tiles], 1.0 / width, eps, ALU.mult, ALU.add).then_inc(s_var, 1)
                dve.wait_ge(s_sd, norm_no[name] + 1)
                dve.reciprocal(var[0:rows, 0:tiles], rstd[0:rows, 0:tiles]).then_inc(s_rstd, 1)

            def read_turned(group, dst, gain, rows=P):
                dve.wait_ge(s_tr, group + 1)
                src = bank(4 + group % 4)[:, 0:4 * rows].rearrange("p (s c) -> p s c", s=4)
                if gain is None:
                    dve.tensor_copy(dst, src).then_inc(s_xT, 1)
                else:
                    TT(dst, src, gain.unsqueeze(2).to_broadcast([P, 4, rows]), ALU.mult).then_inc(s_xT, 1)

            norm_scale("mem", 1e-5)
            dve.wait_ge(s_gain, 16 * 12)
            for t in range(TILES):
                for k in range(4):
                    read_turned(g0["mem"] + 4 * t + k, memT[:, 4 * k:4 * k + 4, t * P:(t + 1) * P], gains[:, 0, 4 * k:4 * k + 4])
            norm_scale("x", 1e-5)
            for t in range(TILES):
                for k in range(4):
                    read_turned(g0["x"] + 4 * t + k, xT[:, 4 * k:4 * k + 4, META + t * P:META + (t + 1) * P],
                                gains[:, 1, 4 * k:4 * k + 4])
            dve.wait_ge(s_shift, 16 * 4)
            for t in range(TILES):
                cur = p[:, t, 0:RWKV_COLS]
                step(TT(prev[:, t], prev[:, t], cur, ALU.subtract))
                step(TT(prev[:, t], prev[:, t], mu, ALU.mult))
                TT(cur, cur, prev[:, t], ALU.add).then_inc(s_mixed, 1)
            for t in range(TILES):
                xg = p[:, t, XG0:XG0 + LORA_G]
                dve.wait_ge(s_eg, t + 1)
                step(dve.tensor_scalar_add(xg, xg, 1.0))
                dve.reciprocal(xg, xg).then_inc(s_sig, 1)
            dve.wait_ge(s_lt, 1)
            step(dve.tensor_copy(loraT[:, 0:2], acc[:, 4:6, 0:SEQ]))
            dve.tensor_copy(loraT[0:LORA_G - P, 2], bank(6)[0:LORA_G - P, 0:SEQ]).then_inc(s_lT, 1)
            step(dve.memset(state[0:R_HEAD], 0.0))
            dve.wait_ge(s_par, 16 * 5)
            heads = lambda x: x.rearrange("p (h n) -> p h n", n=R_HEAD)
            for t in range(TILES):
                r_, k_ = p[:, t, 0:R_W], p[:, t, R_W:2 * R_W]
                a_, kk = beta_t[:, t], key_t[:, t]
                if t:
                    dve.wait_ge(s_el, t)
                dve.wait_ge(s_zd, t + 1)
                TT(tmp, acc[:, 4:6].rearrange("p a b -> p (a b)"), w0, ALU.add).then_inc(s_zv, 1)
                dve.wait_ge(s_ad, t + 1)
                TT(a_, acc[:, 6:8].rearrange("p a b -> p (a b)"), params[:, 0], ALU.add).then_inc(s_av, 1)
                dve.wait_ge(s_ze, t + 1)
                step(dve.tensor_scalar_add(tmp, tmp, 1.0))
                step(dve.reciprocal(logd, tmp))
                dve.tensor_scalar_mul(logd, logd, -E_HALF).then_inc(s_ld, 1)
                step(TT(kk, k_, params[:, 1], ALU.mult))
                step(TT(tmp, kk, kk, ALU.mult))
                RED(kss, heads(tmp), AX, ALU.add).then_inc(s_kss, 1)
                dve.wait_ge(s_ae, t + 1)
                step(dve.tensor_scalar_add(a_, a_, 1.0))
                step(dve.reciprocal(a_, a_))
                step(STT(tmp, a_, -1.0, params[:, 2], ALU.add, ALU.mult))
                step(STT(k_, tmp, 1.0, k_, ALU.add, ALU.mult))
                step(TT(tmp, r_, k_, ALU.mult))
                step(TT(tmp, tmp, params[:, 3], ALU.mult))
                step(RED(bonus[:, t], heads(tmp), AX, ALU.add))
                dve.wait_ge(s_ksd, t + 1)
                step(dve.tensor_scalar_max(kss, kss, 1e-12))
                step(dve.reciprocal(kss, kss))
                step(TT(heads(kk), heads(kk), kss.unsqueeze(2).to_broadcast([P, R_HEADS, R_HEAD]), ALU.mult))
                step(TT(a_, a_, kk, ALU.mult))
                dve.wait_ge(s_cd, t + 1)
                TT(tmp, acc[:, 2:4].rearrange("p a b -> p (a b)"), logd, ALU.subtract).then_inc(s_cp, 1)
                dve.wait_ge(s_en, t + 1)
                STT(kk, kk, -1.0, tmp, ALU.mult, ALU.mult).then_inc(s_kd, 1)
                TT(a_, a_, logd, ALU.mult)
                TT(k_, k_, logd, ALU.mult)
                dve.wait_ge(s_ep, t + 1)
                TT(r_, r_, tmp, ALU.mult).then_inc(s_el, 1)

            b4 = lambda k: bank(k).rearrange("p (j c) -> p j c", j=4)
            m4 = lambda m: m.unsqueeze(1).to_broadcast([P, 4, P])
            for n, (t, q) in enumerate(PAIRS):
                for u in range(2):
                    B = 4 * u
                    g_wait(dve, n, "turned", u, 0)
                    dve.tensor_copy(S_(u, sAT)[0:64], b4(B)[0:64])
                    dve.tensor_copy(S_(u, sBT)[0:64], b4(B + 1)[0:64]).then_inc(g_ve, 1)
                for u in range(2):
                    B = 4 * u
                    g_wait(dve, n, "pairs", u, 0)
                    TT(S_(u, sD), b4(B), m4(lower16), ALU.mult)
                    TT(S_(u, sL), b4(B), m4(lower_rest), ALU.mult)
                    step(TT(S_(u, sDT), b4(B + 1), m4(upper16), ALU.mult))
                    TT(S_(u, sX), S_(u, sDT), m4(ident), ALU.add)
                    TT(S_(u, sAK), b4(B + 2), m4(upper), ALU.mult)
                    TT(S_(u, sRB), b4(B + 3), m4(tri), ALU.mult).then_inc(g_ve, 1)
                for u in range(2):
                    g_wait(dve, n, "square", u, 0)
                    TT(S_(u, sRK), b4(4 * u), m4(tri), ALU.mult).then_inc(g_ve, 1)
                for name in ("fourth", "eighth", "inverse"):
                    for u in range(2):
                        g_wait(dve, n, name, u, 0)
                        TT(S_(u, sX), b4(4 * u), S_(u, sX), ALU.add).then_inc(g_ve, 1)
                for u in range(2):
                    g_wait(dve, n, "solve0", u, 0)
                    dve.tensor_copy(S_(u, sDT), b4(4 * u + 2)).then_inc(g_ve, 1)
                for name in ("solve1", "solve2", "solve3"):
                    for u in range(2):
                        g_wait(dve, n, name, u, 0)
                        g_wait(dve, n, "solve0", u, 2)
                        TT(S_(u, sR), b4(4 * u + 3), S_(u, sY0), ALU.add).then_inc(g_ve, 1)
                for c in range(2):
                    rows = slice(64 * c, 64 * c + 64)
                    for u in range(2):
                        g_wait(dve, n, f"sa{c}", u, 0)
                        TT(S_(u, sKT)[rows, :, 0:64], b4(4 * u + 2)[rows, :, 0:64], S_(u, sR)[rows, :, 64:128],
                           ALU.add).then_inc(g_ve, 1)
                    for u in range(2):
                        g_wait(dve, n, f"state{c}", u, 0)
                        st = state[0:64, (q + u) * 256:(q + u + 1) * 256].rearrange("p (j v) -> p j v", j=4)
                        step(TT(st, st, b4(4 * u + 3)[0:64, :, 0:64], ALU.add))
                        dec = decayC[0:64, t, 4 * (q + u):4 * (q + u) + 4, c:c + 1].to_broadcast([64, 4, 64])
                        TT(st, st, dec, ALU.mult).then_inc(g_ve, 1)
            for u in range(2):
                g_wait(dve, len(PAIRS) - 1, "y", u, 2)
            dve.nop().then_inc(s_rw, 1)
            dve.wait_ge(s_lnx, 32)
            bc = lambda x: x.unsqueeze(2).to_broadcast([P, R_HEADS, R_HEAD])
            for t in range(TILES):
                y = key_t[:, t]
                step(RED(yst[:, 0], heads(y), AX, ALU.add))
                step(dve.tensor_scalar_mul(yst[:, 0], yst[:, 0], 1.0 / R_HEAD))
                step(TT(heads(y), heads(y), bc(yst[:, 0]), ALU.subtract))
                step(TT(beta_t[:, t], y, y, ALU.mult))
                step(RED(yst[:, 1], heads(beta_t[:, t]), AX, ALU.add))
                TS(yst[:, 1], yst[:, 1], 1.0 / R_HEAD, 64e-5, ALU.mult, ALU.add).then_inc(s_yv, 1)
                dve.wait_ge(s_ysd, t + 1)
                step(dve.reciprocal(yst[:, 1], yst[:, 1]))
                step(TT(heads(y), heads(y), bc(yst[:, 1]), ALU.mult))
                step(TT(y, y, lnx[:, 0], ALU.mult))
                step(TT(y, y, lnx[:, 1], ALU.add))
                step(TT(heads(beta_t[:, t]), heads(p[:, t, 2 * R_W:3 * R_W]), bc(bonus[:, t]), ALU.mult))
                step(TT(y, y, beta_t[:, t], ALU.add))
                TT(y, y, gate[:, t], ALU.mult).then_inc(s_yr, 1)

            def whole_turns(x, off):
                step(TS(turns_f, x, 1.0 / (2 * 3.141592653589793), off / (2 * 3.141592653589793), ALU.mult, ALU.add))
                step(dve.tensor_copy(turns_i, turns_f))
                step(dve.tensor_copy(turns_f, turns_i))
                step(STT(rot2, turns_f, -TWO_PI_HI, x, ALU.mult, ALU.add))
                step(STT(rot2, turns_f, -TWO_PI_LO, rot2, ALU.mult, ALU.add))
                step(dve.tensor_scalar_add(rot2, rot2, off))

            rot2 = rot[:, 0, 0:2 * 16].rearrange("p (t j) -> p t j", t=TILES)
            for j in range(16):
                dve.memset(invf[:, j:j + 1], float(np.float32(THETA) ** np.float32(-j / 16)))
            step(dve.tensor_copy(posf, posi))
            step(TT(ang, posf.unsqueeze(2).to_broadcast([P, TILES, 16]), invf.unsqueeze(1).to_broadcast([P, TILES, 16]), ALU.mult))
            whole_turns(ang, 3.141592653589793 / 2)
            step(TS(turns_f, rot2, -PI, PI, ALU.max, ALU.min))
            step(dve.tensor_copy(rot[:, 1, 0:32].rearrange("p (t j) -> p t j", t=TILES), turns_f))
            whole_turns(ang, 0.0)
            TS(ang, rot2, -PI, PI, ALU.max, ALU.min).then_inc(s_ang, 1)
            dve.tensor_copy(turns_f, rot[:, 1, 0:32].rearrange("p (t j) -> p t j", t=TILES)).then_inc(s_ang, 1)
            dve.wait_ge(s_trig, 1)
            for t in range(TILES):
                for col, heads_n, width, half, stride in ((Q0, A_HEADS + A_KV, A_HEAD, 16, 1), (QI0, I_HEADS + 1, I_HEAD, 8, 2)):
                    x = p[:, t, col:col + heads_n * width].rearrange("p (h d) -> p h d", h=heads_n)
                    x1, x2 = x[:, :, 0:half], x[:, :, half:2 * half]
                    sn, cs = (sincos[:, k, t, 0:16:stride].unsqueeze(1).to_broadcast([P, heads_n, half]) for k in range(2))
                    r = [rot[:, k, 0:heads_n * half].rearrange("p (h d) -> p h d", h=heads_n) for k in range(4)]
                    TT(r[0], x1, cs, ALU.mult)
                    TT(r[1], x2, sn, ALU.mult)
                    TT(r[2], x2, cs, ALU.mult)
                    step(TT(r[3], x1, sn, ALU.mult))
                    TT(x1, r[0], r[1], ALU.subtract)
                    step(TT(x2, r[2], r[3], ALU.add))
                step(TS(p[:, t, WI0:WI0 + I_HEADS], p[:, t, WI0:WI0 + I_HEADS], (I_HEADS * I_HEAD) ** -0.5, None, ALU.mult))
                dve.tensor_copy(keyI[:, t].rearrange("p (a d) -> p a d", a=2),
                                p[:, t, KI0:KI0 + I_HEAD].unsqueeze(1).to_broadcast([P, 2, I_HEAD])).then_inc(s_rope, 1)
            for t in range(TILES):
                nk = (t + 1) * P
                sc = score[:, t, 0:nk]
                step(dve.tensor_copy(sc, causal[:, t, META:META + nk]))
                for i in range(I_HEADS // 2):
                    m = t * (I_HEADS // 2) + i
                    dve.wait_ge(s_rel, m + 1)
                    for j in range(2):
                        last = STT(sc, rel[:, m % 4, j, 0:nk], p[:, t, WI0 + 2 * i + j:WI0 + 2 * i + j + 1], sc,
                                   ALU.mult, ALU.add)
                        if j == 0:
                            step(last)
                    last.then_inc(s_acc2, 1)
                    dve.wait_ge(s_acc2, m + 1)
                src = sc
                for r in range(TOPK // 8):
                    step(dve.max(m8, src))
                    step(dve.match_replace(left[:, 0:nk], m8, src, TAKEN))
                    src = left[:, 0:nk]
                un = unsel[:, t, 0:nk]
                step(TS(un, left[:, 0:nk], TAKEN / 2, NEG, ALU.is_gt, ALU.mult))
                step(TT(un, un, causal[:, t, META:META + nk], ALU.add))

            def attend(m0, n, prepare, finish):
                for m in range(m0, m0 + n + 3):
                    if m < m0 + n:
                        dve.wait_ge(a_S, m + 1)
                        if m >= 3:
                            dve.wait_ge(a_T, m - 2)
                            dve.wait_ge(a_pr, m - 2)
                        prepare(m)
                    if m0 <= m - 3:
                        dve.wait_ge(a_O, m - 2)
                        finish(m - 3)

            def finish_of(dst):
                def go(m):
                    step(dve.reciprocal(pinv[:, m % 4], psums[:, m % 4]))
                    TT(dst(m), bank(5 + m % 2)[:, 0:2 * P].rearrange("p (j d) -> p j d", j=2),
                       pinv[:, m % 4].unsqueeze(2).to_broadcast([P, 2, P]), ALU.mult).then_inc(a_done, 1)
                return go

            def dsa_prepare(m):
                t = (m - M_DSA) // 4
                nk = (t + 1) * P
                pr = prob[:, m % 3, 0:2 * nk].rearrange("p (j s) -> p j s", j=2)
                step(TT(pr, bank(m % 3)[:, 0:2 * nk].rearrange("p (j s) -> p j s", j=2),
                        unsel[:, t, 0:nk].unsqueeze(1).to_broadcast([P, 2, nk]), ALU.add))
                RED(nmax[:, m % 3], pr, AX, ALU.max, negate=True).then_inc(a_sm, 1)

            def dsa_out(m):
                t, i = (m - M_DSA) // 4, (m - M_DSA) % 4
                return p[:, t, Q0 + 2 * i * P:Q0 + 2 * (i + 1) * P].rearrange("p (j d) -> p j d", j=2)
            attend(M_DSA, 8, dsa_prepare, finish_of(dsa_out))


            def turned_plain(name, tiles, slabs):
                for t in range(tiles):
                    for k in range(slabs // 4):
                        read_turned(g0[name] + (slabs // 4) * t + k,
                                    xT[:, 4 * k:4 * k + 4, META + t * P:META + (t + 1) * P], None)

            def turned_normed(name, n):
                for t in range(TILES):
                    for k in range(4):
                        read_turned(g0[name] + 4 * t + k, xT[:, 4 * k:4 * k + 4, META + t * P:META + (t + 1) * P],
                                    gains[:, n, 4 * k:4 * k + 4])

            def add_to_h(g):
                def body(i):
                    for c in range(g.per_body):
                        chunk_done(dve, g, c, i)
                        for t in range(TILES):
                            k = 2 * (c % 2) + t
                            cols = h[:, t, bass.ds(i * (g.per_body * CHUNK) + c * CHUNK, CHUNK)]
                            TT(cols, bank(k), cols, ALU.add).then_inc(acc_free[k], 1)
                loop(dve, g.bodies, body)

            turned_plain("mixed", TILES, SLABS)
            add_to_h(G["mix"])
            norm_scale("cross", 1e-5)
            turned_normed("cross", 2)

            def cross_prepare(m):
                RED(nmax[:, m % 3], bank(m % 3).rearrange("p (j s) -> p j s", j=2), AX, ALU.max, negate=True
                    ).then_inc(a_sm, 1)

            def cross_out(m):
                t, i = (m - M_CROSS) // 2, (m - M_CROSS) % 2
                return co[:, t, 2 * i * P:2 * (i + 1) * P].rearrange("p (j d) -> p j d", j=2)
            attend(M_CROSS, 4, cross_prepare, finish_of(cross_out))
            turned_plain("o", TILES, C_W // P)
            add_to_h(G["cross_o"])
            norm_scale("mlp", 1e-5)
            turned_normed("mlp", 3)
            add_to_h(G["down"])
            norm_scale("final", 1e-5)
            dve.wait_ge(s_fgain, 16)
            dve.wait_ge(s_rstd, norm_no["final"] + 1)
            for t in range(TILES):
                STT(h[:, t], h[:, t], var[:, t:t + 1], final_gain, ALU.mult, ALU.mult).then_inc(s_fin, 1)

            norm_scale("meta", 1e-6, META)
            for k in range(4):
                read_turned(g0["meta"] + k, xT[:, 4 * k:4 * k + 4, 0:META], gains[:, 4, 4 * k:4 * k + 4], META)
            norm_scale("mix2", 1e-6)
            turned_normed("mix2", 4)
            dve.wait_ge(s_c2, 1)
            step(TS(seen, strict, NEG / 2, None, ALU.is_gt))
            step(dve.tensor_scalar_mul(head_gains[:, 0:1], head_gains[:, 0:1], HEAD2 ** -0.5))
            dve.wait_ge(s_lf1, 1)
            lf = logf[0:HEADS2]
            step(STT(lf[:, 2], lf[:, 0], 0.0, lf[:, 1], ALU.min, ALU.subtract))
            step(dve.tensor_tensor_scan(lf[:, 0], lf[:, 2], lf[:, 2], 0.0, ALU.add, ALU.bypass))
            dve.tensor_scalar_mul(lf[:, 1], lf[:, 0], -1.0).then_inc(s_lf2, 1)
            dve.wait_ge(s_ct, 1)
            dve.tensor_copy(cumf, bank(4)[:, 0:TILES * HEADS2].rearrange("p (t h) -> p t h", t=TILES)).then_inc(s_cc, 1)
            flat_q, flat_k = (x.rearrange("p h c -> p (h c)") for x in (fqT, fkT))
            for r, (x, c0, n) in enumerate([(flat_q, 0, 2048), (flat_k, 0, 2048), (flat_k, 2048, HEADS2 * CTX - 2048)]):
                dve.wait_ge(s_fr, r + 1)
                root = sq_tmp[:, D:D + n]
                step(dve.reciprocal(root, root))
                gcol = head_gains[:, min(r, 1):min(r, 1) + 1]
                STT(x[:, c0:c0 + n], x[:, c0:c0 + n], gcol, root, ALU.mult, ALU.mult).then_inc(s_fn, 1)
            fg = fgate.rearrange("p t c -> p (t c)")
            step(dve.tensor_scalar_add(fg, fg, 1.0))
            step(dve.reciprocal(fg, fg))

            of = lambda m: ((m - M_TWO) // 16, (m - M_TWO) % 2, (m - M_TWO) % 16 // 2)
            nk2 = lambda m: META + ((m - M_TWO) // 16 + 1) * P

            def two_prepare(m):
                t, fox, hd = of(m)
                z = bank(m % 3)[:, 0:nk2(m)]
                if fox:
                    pr = prob2[:, m % 3, 0:nk2(m)]
                    step(STT(pr, z, cumf[:, t, hd:hd + 1], causal[:, t, 0:nk2(m)], ALU.add, ALU.add))
                    RED(nmax[:, m % 3, 0:1], pr, AX, ALU.max, negate=True).then_inc(a_sm, 1)
                    return
                a, b, c = (stick[:, m % 3, k, 0:nk2(m)] for k in range(3))
                dve.wait_ge(s_l, (m - M_TWO) // 2 + 1)
                step(STT(b, z, 0.0, a, ALU.max, ALU.add))
                step(dve.tensor_tensor_scan(c[:, ::-1], b[:, ::-1], seen[:, t, 0:nk2(m)][:, ::-1], 0.0, ALU.add, ALU.mult))
                step(TT(b, z, c, ALU.subtract))
                TT(b, b, strict[:, t, 0:nk2(m)], ALU.add).then_inc(a_sm, 1)

            def two_finish(m):
                t, fox, hd = of(m)
                dst = merged[:, t, fox * W2 + hd * P:fox * W2 + (hd + 1) * P]
                src = bank(5 + m % 2)[:, 0:P]
                if fox:
                    step(dve.reciprocal(pinv[:, m % 4, 0:1], psums[:, m % 4, 0:1]))
                    TS(dst, src, pinv[:, m % 4, 0:1], None, ALU.mult).then_inc(a_done, 1)
                else:
                    dve.tensor_copy(dst, src).then_inc(a_done, 1)

            attend(M_TWO, 32, two_prepare, two_finish)
            norm_scale("heads2", 1e-6, P, W2)
            dve.wait_ge(s_rstd, norm_no["heads2"] + 1)
            for t in range(TILES):
                TS(merged[:, t, 0:W2], merged[:, t, 0:W2], var[:, 2 * t:2 * t + 1], None, ALU.mult).then_inc(s_mg, 1)
                STT(merged[:, t, W2:D], merged[:, t, W2:D], var[:, 2 * t + 1:2 * t + 2], fgate[:, t], ALU.mult, ALU.mult
                    ).then_inc(s_mg, 1)
            turned_normed("merged", 5)
            add_to_h(G["out2"])
            norm_scale("ffn", 1e-6)
            turned_normed("ffn", 6)
            dve.wait_ge(s_erow, 32)
            dve.wait_ge(s_xn, xn0["ffn"] + TILES)
            for t in range(TILES):
                TT(hb[:, t], xn3[:, t], gain_row, ALU.mult).then_inc(s_hb, 1)
            b1 = best1.bitcast(FP32)
            i1 = bestf.bitcast(U32)
            jn = picked[:, 0].bitcast(U32)
            hi, lo = picked[:, 1].bitcast(U32), picked[:, 2].bitcast(U32)
            step(dve.memset(iota16[:, 0:1], 0.0))
            for k in range(1, E_TOP):
                step(dve.memset(iota16[:, k:k + 1], float(k)))

            def best16(val, idx, src):
                step(dve.max(val[:, 0:8], src))
                step(dve.max_index(idx[:, 0:8], val[:, 0:8], src))
                w = work1[:, 0:src.shape[-1]]
                step(dve.match_replace(w, val[:, 0:8], src, TAKEN))
                step(dve.max(val[:, 8:16], w))
                step(dve.max_index(idx[:, 8:16], val[:, 8:16], w))

            cw = lambda t: coef[:, t].rearrange("p (h k) -> p h k", h=E_HEADS)
            for t in range(TILES):
                dve.wait_ge(s_sc, t + 1)
                for k in range(2 * E_HEADS):
                    best16(best1[:, k], i1[:, k], scores[:, t, k * N_KEYS:(k + 1) * N_KEYS])
                cand = hot.rearrange("p (h a) b -> p h a b", h=E_HEADS)
                pair = best1.rearrange("p (h q) a -> p h q a", q=2)
                shape = [P, E_HEADS, E_TOP, E_TOP]
                step(TT(cand, pair[:, :, 0].unsqueeze(3).to_broadcast(shape), pair[:, :, 1].unsqueeze(2).to_broadcast(shape), ALU.add))
                flat = hot.rearrange("p a b -> p (a b)")
                for e in range(E_HEADS):
                    best16(best2[:, t, e], jn[:, e * E_TOP:(e + 1) * E_TOP], flat[:, e * 256:(e + 1) * 256])
                TT(cw(t), best2[:, t], best2[:, t, :, 0:1].to_broadcast([P, E_HEADS, E_TOP]), ALU.subtract).then_inc(s_bs, 1)
                step(TS(hi, jn, 4, None, ALU.logical_shift_right))
                step(TS(lo, jn, 15, None, ALU.bitwise_and))
                step(dve.tensor_copy(picked[:, 1], hi))
                step(dve.tensor_copy(picked[:, 2], lo))
                step(dve.tensor_copy(bestf, i1))
                lists = bestf.rearrange("p (h q) a -> p h q a", q=2)
                for q_ in range(2):
                    at_ = picked[:, 1 + q_].rearrange("p (h k) -> p h k", h=E_HEADS).unsqueeze(3).to_broadcast(shape)
                    step(TT(cand, at_, iota16.unsqueeze(1).unsqueeze(1).to_broadcast(shape), ALU.is_equal))
                    step(TT(cand, cand, lists[:, :, q_].unsqueeze(2).to_broadcast(shape), ALU.mult))
                    step(RED(picked[:, 1 + q_], hot, AX, ALU.add))
                STT(experts[:, t * P:(t + 1) * P], picked[:, 1], float(N_KEYS), picked[:, 2], ALU.mult, ALU.add).then_inc(s_ix0, 1)
                dve.wait_ge(s_ix0, t + 1)
            dve.tensor_copy(experts[:, TILES * P:TILES * P + 4], experts[:, 0:4]).then_inc(s_ix0, 1)
            for t in range(TILES):
                dve.wait_ge(s_be, t + 1)
                step(RED(esum[:, t], cw(t), AX, ALU.add))
                step(dve.reciprocal(esum[:, t], esum[:, t]))
                step(TT(cw(t), cw(t), esum[:, t].unsqueeze(2).to_broadcast([P, E_HEADS, E_TOP]), ALU.mult))
            per = P // 16
            for t in range(TILES):
                with dve.Fori(0, per) as i:
                    for n in range(4):
                        dve.wait_ge(rows_full[n % 2], i * 128 + (t * per * 128 + 64 * (n // 2 + 1)))
                        for j in range(4):
                            last = dve.tensor_tensor_reduce(out=junk, in0=rows_buf[4 * (n % 2) + j], in1=hb[:, t], scale=1.0, scalar=0.0,
                                                            op0=ALU.mult, op1=ALU.add, accum_out=dots_now[:, 4 * n + j:4 * n + j + 1])
                            if j == 3:
                                last.then_inc(rows_used[n % 2], 1)
                            dve.drain()
                    dve.tensor_copy(dots[:, t, bass.ds(i * 16, 16)], dots_now)
                    dve.drain()
                dve.nop().then_inc(s_dot, 1)
            dve.wait_ge(s_gelu, 1)
            step(TT(coef, coef, dots, ALU.mult))
            for t in range(TILES):
                with dve.Fori(0, per) as i:
                    dve.tensor_copy(coef_now, coef[:, t, bass.ds(i * 16, 16)])
                    dve.drain()
                    for n in range(4):
                        dve.wait_ge(rows_full[n % 2], i * 128 + ((TILES + t) * per * 128 + 64 * (n // 2 + 1)))
                        for j in range(4):
                            last = STT(h[:, t], rows_buf[4 * (n % 2) + j], coef_now[:, 4 * n + j:4 * n + j + 1], h[:, t],
                                       ALU.mult, ALU.add)
                            if j == 3:
                                last.then_inc(rows_used[n % 2], 1)
                            dve.drain()

        @block.tensor
        def _(pe):
            for k in range(4):
                pe.sem_inc(acc_free[k], 1)
            for s in range(SLOTS):
                pe.sem_inc(tile_used[s], 1)

            def product(g, x):
                def body(i):
                    for c in range(g.per_body):
                        width = g.widths[c]
                        banks = (2 * (c % 2), 2 * (c % 2) + 1) if g.tok else range(4)
                        for b in banks:
                            n = sum(1 for d in range(c) if not g.tok or b // 2 == d % 2)
                            pe.wait_ge(acc_free[b], i * g.uses(b) + g.used0[b] + n + 1)
                        for j in range(g.tiles):
                            slot, turn = g.tile(c, j)
                            pe.wait_ge(tile_full[slot], i * (16 * g.turns) + 16 * (g.turn0 + turn + 1))
                            for s in range(SLOT_SLABS):
                                slab = SLOT_SLABS * j + s
                                kw = dict(start=slab == 0, stop=slab == g.k // P - 1)
                                if g.tok:
                                    for t in range(TILES):
                                        last = pe.matmul(bank(banks[t])[:, 0:width],
                                                         x(slab)[:, g.lo + t * P:g.lo + (t + 1) * P],
                                                         ring[:, slot, s, 0:width], **kw)
                                else:
                                    for f in range(4):
                                        last = pe.matmul(bank(f)[:, 0:g.hi - g.lo], ring[:, slot, s, f * P:(f + 1) * P],
                                                         x(slab)[:, g.lo:g.hi], **kw)
                            last.then_inc(tile_used[slot], 1)
                loop(pe, g.bodies, body)

            def turn(name, is_norm, block_of, rows=P, tiles=TILES, slabs=SLABS):
                group = g0[name]
                for t in range(tiles):
                    if is_norm:
                        pe.wait_ge(s_xn, xn0[name] + t + 1)
                    for k in range(slabs // 4):
                        if group >= 4:
                            pe.wait_ge(s_xT, group - 3)
                        for j in range(4):
                            last = pe.transpose(bank(4 + group % 4)[:, j * rows:(j + 1) * rows],
                                                block_of(t, 4 * k + j), ident[0:rows, 0:rows])
                        last.then_inc(s_tr, 1)
                        group += 1
                return group

            xn_block = lambda t, s: xn[:, t, s * P:(s + 1) * P]
            pe.wait_ge(s_const, 1)
            turn("mem", True, xn_block)
            turn("x", True, xn_block)
            pe.wait_ge(s_xT, 8)
            product(G["cross_k"], lambda s: memT[:, s])
            g = G["cross_v"]; g.lo = 0
            product(g, lambda s: memT[:, s])
            g.lo = META
            pe.wait_ge(s_xT, 16)
            product(G["in"], lambda s: xT[:, s])
            product(G["in_end"], lambda s: xT[:, s])

            for k in range(4):
                pe.wait_ge(acc_free[k], G["mix"].used0[k] + 1)
            for t in range(TILES):
                pe.wait_ge(s_tanh, t + 1)
                pe.transpose(bank(4)[:, t * P:(t + 1) * P], p[:, t, XW0:XW0 + P], ident)
                pe.wait_ge(s_sig, t + 1)
                pe.transpose(bank(5)[:, t * P:(t + 1) * P], p[:, t, XG0:XG0 + P], ident)
                last = pe.transpose(bank(6)[0:LORA_G - P, t * P:(t + 1) * P], p[:, t, XG0 + P:XG0 + LORA_G], ident)
            last.then_inc(s_lt, 1)
            pe.wait_ge(s_lT, 1)
            pe.wait_ge(s_lora, 64)
            for t in range(TILES):
                tok = slice(t * P, (t + 1) * P)
                if t:
                    pe.wait_ge(s_ep, t)
                for c in range(2):
                    cols = slice(c * CHUNK, (c + 1) * CHUNK)
                    last = pe.matmul(bank(4 + c), loraT[0:LORA_W, 0, tok], lora_up[0:LORA_W, 0, cols], start=True, stop=True)
                last.then_inc(s_zd, 1)
                for c in range(2):
                    cols = slice(c * CHUNK, (c + 1) * CHUNK)
                    last = pe.matmul(bank(6 + c), loraT[LORA_W:P, 0, tok], lora_up[LORA_W:P, 0, cols], start=True, stop=True)
                last.then_inc(s_ad, 1)
                if t:
                    pe.wait_ge(s_gate, t)
                for c in range(2):
                    cols = slice(c * CHUNK, (c + 1) * CHUNK)
                    pe.matmul(bank(c), loraT[:, 1, tok], lora_up[:, 1, cols], start=True, stop=False)
                    last = pe.matmul(bank(c), loraT[0:LORA_G - P, 2, tok], lora_up[0:LORA_G - P, 2, cols], start=False, stop=True)
                last.then_inc(s_gd, 1)
                pe.wait_ge(s_ld, t + 1)
                for c in range(2):
                    pe.matmul(bank(2 + c), tri, logd[:, c * CHUNK:(c + 1) * CHUNK], start=True, stop=True)
                for hd in range(R_HEADS):
                    last = pe.matmul(bank(6)[0:R_HEAD, 2 * hd:2 * hd + 2], logd[:, hd * R_HEAD:(hd + 1) * R_HEAD], halves,
                                     start=hd == 0, stop=True, skip_group_check=True)
                last.then_inc(s_cd, 1)
            pe.wait_ge(s_el, TILES)
            for n, (t, q) in enumerate(PAIRS):
                b4 = lambda k: bank(k).rearrange("p (j c) -> p j c", j=4)
                V = lambda u, j: p[:, t, 2 * R_W + (q + u) * 256 + j * 64:2 * R_W + (q + u) * 256 + (j + 1) * 64]
                K = lambda u, j: p[:, t, R_W + (q + u) * 256 + j * 64:R_W + (q + u) * 256 + (j + 1) * 64]
                R = lambda u, j: p[:, t, (q + u) * 256 + j * 64:(q + u) * 256 + (j + 1) * 64]
                AK_ = lambda u, j: key_t[:, t, (q + u) * 256 + j * 64:(q + u) * 256 + (j + 1) * 64]
                BT_ = lambda u, j: beta_t[:, t, (q + u) * 256 + j * 64:(q + u) * 256 + (j + 1) * 64]
                S0 = lambda u, j: state[0:64, (q + u) * 256 + j * 64:(q + u) * 256 + (j + 1) * 64]

                def mm(b, j, lhsT, rhs, start=True, stop=True, rows=slice(0, P), width=P, check=False):
                    return pe.matmul(b4(b)[rows, j, 0:width], lhsT, rhs, start=start, stop=stop, skip_group_check=check)

                def after(prev_stage, u):
                    g_wait(pe, n, prev_stage, u, 1)
                    g_wait(pe, n, prev_stage, u, 2)

                for u in range(2):
                    if n:
                        g_wait(pe, n - 1, "state1", u, 1)
                        g_wait(pe, n - 1, "y", u, 2)
                    for b, src in enumerate((AK_, BT_, K, R)):
                        for j in range(4):
                            last = pe.transpose(b4(4 * u + b)[0:64, j], src(u, j), ident)
                    last.then_inc(g_pe, 1)
                for u in range(2):
                    after("turned", u)
                    at_, bt, kt, rt = (S_(u, x) for x in (sAT, sBT, sKT, sRT))
                    for j in range(4):
                        mm(4 * u, j, at_[0:64, j], bt[0:64, j])
                        mm(4 * u + 1, j, bt[0:64, j], at_[0:64, j])
                        mm(4 * u + 2, j, kt[0:64, j], at_[0:64, j])
                        last = mm(4 * u + 3, j, bt[0:64, j], rt[0:64, j])
                    last.then_inc(g_pe, 1)
                for u in range(2):
                    after("pairs", u)
                    for j in range(4):
                        mm(4 * u, j, S_(u, sKT)[0:64, j], S_(u, sRT)[0:64, j])
                        mm(4 * u + 1, j, S_(u, sDT)[:, j], S_(u, sD)[:, j])
                        mm(4 * u + 2, j, S_(u, sD)[:, j], S_(u, sDT)[:, j])
                        last = mm(4 * u + 3, j, S_(u, sAK)[:, j], V(u, j), width=64)
                    last.then_inc(g_pe, 1)
                for u in range(2):
                    after("square", u)
                    for j in range(4):
                        mm(4 * u, j, S_(u, sKT)[:, j], S_(u, sX)[:, j])
                        mm(4 * u + 1, j, S_(u, sBT)[:, j], S_(u, sKT)[:, j])
                        last = mm(4 * u + 2, j, S_(u, sKT)[:, j], S_(u, sBT)[:, j])
                    last.then_inc(g_pe, 1)
                for u in range(2):
                    after("fourth", u)
                    for j in range(4):
                        mm(4 * u, j, S_(u, sD)[:, j], S_(u, sX)[:, j])
                        last = mm(4 * u + 1, j, S_(u, sDT)[:, j], S_(u, sD)[:, j])
                    last.then_inc(g_pe, 1)
                for u in range(2):
                    after("eighth", u)
                    for j in range(4):
                        last = mm(4 * u, j, S_(u, sKT)[:, j], S_(u, sX)[:, j])
                    last.then_inc(g_pe, 1)
                for u in range(2):
                    after("inverse", u)
                    for j in range(4):
                        mm(4 * u + 1, j, S_(u, sX)[:, j], S_(u, sR)[:, j])
                        last = mm(4 * u + 2, j, S_(u, sL)[:, j], S_(u, sX)[:, j])
                    last.then_inc(g_pe, 1)
                for a, b in (("solve0", "solve1"), ("solve1", "solve2"), ("solve2", "solve3")):
                    for u in range(2):
                        after(a, u)
                        y = S_(u, sY0) if a == "solve0" else S_(u, sR)
                        for j in range(4):
                            last = mm(4 * u + 3, j, S_(u, sDT)[:, j], y[:, j])
                        last.then_inc(g_pe, 1)
                for u in range(2):
                    after("solve3", u)
                    for j in range(4):
                        last = pe.transpose(b4(4 * u)[0:64, j], S_(u, sR)[:, j, 0:64], ident)
                    last.then_inc(g_pe, 1)
                for c in range(2):
                    rows = slice(64 * c, 64 * c + 64)
                    for u in range(2):
                        if c == 0:
                            after("w_turned", u)
                            for j in range(4):
                                mm(4 * u + 1, j, S_(u, sRK)[:, j], V(u, j), start=j == 0, stop=False, width=64, check=True)
                        else:
                            after("state0", u)
                        for j in range(4):
                            last = mm(4 * u + 2, j, S_(u, sAT)[0:64, j, rows], S0(u, j), rows=rows, width=64)
                        last.then_inc(g_pe, 1)
                    for u in range(2):
                        for j in range(4):
                            mm(4 * u + 1, j, S_(u, sRT)[0:64, j, rows], S0(u, j), start=False, stop=False, rows=rows,
                               width=64, check=True)
                        after(f"sa{c}", u)
                        for j in range(4):
                            mm(4 * u + 3, j, BT_(u, j)[rows], S_(u, sKT)[rows, j, 0:64], start=True, stop=False,
                               rows=slice(0, 64), width=64)
                            last = mm(4 * u + 3, j, K(u, j)[rows], V(u, j)[rows], start=False, stop=True,
                                      rows=slice(0, 64), width=64)
                        last.then_inc(g_pe, 1)
                for u in range(2):
                    for j in range(4):
                        last = mm(4 * u + 1, j, S_(u, sRB)[:, j], S_(u, sKT)[:, j, 0:64], start=False, stop=j == 3,
                                  width=64, check=True)
                    last.then_inc(g_pe, 1)

            pe.wait_ge(s_yr, TILES)
            pe.wait_ge(s_rope, TILES)
            for t in range(TILES):
                pe.transpose(bank(0)[:, t * P:(t + 1) * P], keyI[:, t], ident)
                for k in range(A_KV):
                    last = pe.transpose(bank(1)[:, k * SEQ + t * P:k * SEQ + (t + 1) * P],
                                        p[:, t, K0 + k * P:K0 + (k + 1) * P], ident)
            last.then_inc(s_kturn, 1)
            for t in range(TILES):
                if t:
                    pe.wait_ge(s_qT2, t)
                for k, col in ((2, QI0), (4, Q0)):
                    for i in range(8):
                        last = pe.transpose(bank(k + i // 4)[:, (i % 4) * P:(i % 4 + 1) * P],
                                            p[:, t, col + i * P:col + (i + 1) * P], ident)
                last.then_inc(s_qturn, 1)
                pe.wait_ge(s_kT2, 1)
                pe.wait_ge(s_qT2, t + 1)
                nk = (t + 1) * P
                for i in range(I_HEADS // 2):
                    m = t * (I_HEADS // 2) + i
                    if m >= 2:
                        pe.wait_ge(s_rel, m - 1)
                    for j in range(2):
                        half = slice(j * I_HEAD, (j + 1) * I_HEAD)
                        last = pe.matmul(bank(6 * (m % 2) + j)[:, 0:nk], qiT[half, t, i], kiT[half, 0:nk],
                                         start=True, stop=True)
                    last.then_inc(s_ix, 1)

            def attend(m0, n, heads_n, scores_of, blocks, values, pr_of, pT_of):
                for m in range(m0, m0 + n + 3):
                    if m < m0 + n:
                        if m >= 3:
                            pe.wait_ge(a_pr, m - 2)
                        scores_of(m).then_inc(a_S, 1)
                    if m0 <= m - 2 < m0 + n:
                        k = m - 2
                        pe.wait_ge(a_pr, k + 1)
                        if k >= 2:
                            pe.wait_ge(a_PT, k - 1)
                        slot = 0
                        for j in range(heads_n):
                            for off, size in blocks(k):
                                last = pe.transpose(bank(3 + k % 2)[0:size, slot * P:(slot + 1) * P],
                                                    pr_of(k, j)[:, off:off + size], ident)
                                slot += 1
                        last.then_inc(a_T, 1)
                    if m0 <= m - 3:
                        k = m - 3
                        pe.wait_ge(a_PT, k + 1)
                        if k >= 2:
                            pe.wait_ge(a_done, k - 1)
                        nb = len(blocks(k))
                        for j in range(heads_n):
                            for n_, (off, size) in enumerate(blocks(k)):
                                slot = j * nb + n_
                                last = pe.matmul(bank(5 + k % 2)[:, j * P:(j + 1) * P],
                                                 pT_of(k)[0:size, slot * P:(slot + 1) * P], values(k, j, n_),
                                                 start=n_ == 0, stop=n_ == nb - 1)
                        last.then_inc(a_O, 1)

            def dsa_scores(m):
                t, i = (m - M_DSA) // 4, (m - M_DSA) % 4
                nk = (t + 1) * P
                for j in range(2):
                    hd = 2 * i + j
                    last = pe.matmul(bank(m % 3)[:, j * nk:(j + 1) * nk], qT[:, t, hd], kT[:, hd // (A_HEADS // A_KV), 0:nk],
                                     start=True, stop=True)
                return last

            def dsa_values(m, j, n_):
                kv = (2 * ((m - M_DSA) % 4) + j) // (A_HEADS // A_KV)
                return p[:, n_, V0 + kv * P:V0 + (kv + 1) * P]

            nk1 = lambda m: ((m - M_DSA) // 4 + 1) * P
            pe.wait_ge(s_rel, I_HEADS)
            attend(M_DSA, 8, 2, dsa_scores, lambda m: [(b * P, P) for b in range((m - M_DSA) // 4 + 1)], dsa_values,
                   lambda m, j: prob[:, m % 3, j * nk1(m):(j + 1) * nk1(m)], lambda m: probT[:, m % 2])
            pe.wait_ge(a_done, M_DSA + 8)
            turn("mixed", False, lambda t, s: key_t[:, t, s * P:(s + 1) * P] if s < R_W // P else
                 p[:, t, Q0 + (s - R_W // P) * P:Q0 + (s - R_W // P + 1) * P])
            pe.wait_ge(s_xT, g0["mixed"] + 8)
            product(G["mix"], lambda s: xT[:, s])
            turn("cross", True, xn_block)
            pe.wait_ge(s_xT, g0["cross"] + 8)
            product(G["cross_q"], lambda s: xT[:, s])
            for k in range(4):
                pe.wait_ge(acc_free[k], G["cross_o"].used0[k] + 1)

            def cross_scores(m):
                t, i = (m - M_CROSS) // 2, (m - M_CROSS) % 2
                for j in range(2):
                    last = pe.matmul(bank(m % 3)[:, j * SEQ:(j + 1) * SEQ], cqT[:, 2 * i + j, t * P:(t + 1) * P],
                                     ckT[:, 2 * i + j], start=True, stop=True)
                return last
            attend(M_CROSS, 4, 2, cross_scores, lambda m: [(0, P), (P, P)],
                   lambda m, j, n_: cv[:, n_, (2 * ((m - M_CROSS) % 2) + j) * P:(2 * ((m - M_CROSS) % 2) + j + 1) * P],
                   lambda m, j: prob[:, m % 3, j * SEQ:(j + 1) * SEQ], lambda m: probT[:, m % 2])
            pe.wait_ge(a_done, M_CROSS + 4)
            turn("o", False, lambda t, s: co[:, t, s * P:(s + 1) * P], slabs=C_W // P)
            pe.wait_ge(s_xT, g0["o"] + 2)
            product(G["cross_o"], lambda s: xT[:, s])
            turn("mlp", True, xn_block)
            pe.wait_ge(s_xT, g0["mlp"] + 8)
            product(G["up"], lambda s: xT[:, s])
            pe.wait_ge(s_hid, FF // CHUNK)
            down = G["down"]
            down.lo = 0
            product(down, lambda s: hidT[:, s])
            down.lo = META
            turn("meta", True, lambda t, s: xn2[0:META, 0, s * P:(s + 1) * P], META, 1)
            turn("mix2", True, lambda t, s: xn2[:, t, s * P:(s + 1) * P])
            pe.wait_ge(s_xT, g0["mix2"] + 8)
            x_ = lambda s: xT[:, s]

            def turn_values(v0, v_free):
                for k in range(4):
                    pe.wait_ge(acc_free[k], v_free.used0[k] + 1)
                for n in range(3):
                    if n == 2:
                        pe.wait_ge(s_vr, v0 + 1)
                    for hd in range(HEADS2):
                        b = (4, 6, 4)[n] + hd // 4
                        src = vT[:, hd, META + n * P:META + (n + 1) * P] if n < 2 else vT[:, hd, 0:META]
                        last = pe.transpose(bank(b)[0:src.shape[-1], (hd % 4) * P:(hd % 4 + 1) * P], src, ident)
                    last.then_inc(s_vt, 1)

            product(G["sb_q"], x_)
            product(G["sb_kv"], x_)
            product(G["fox_q"], x_)
            turn_values(0, G["fox_q"])
            product(G["fox_kv"], x_)
            product(G["fox_gate"], x_)
            pe.wait_ge(s_vr, 3)
            pe.wait_ge(s_meta, 32)
            pe.wait_ge(s_c2, 1)
            for s_ in range(SLABS):
                last = pe.matmul(bank(4)[0:HEADS2, 0:CTX], w_logit[:, s_], xT[:, s_], start=s_ == 0, stop=s_ == SLABS - 1)
            last.then_inc(s_lg, 1)
            pe.wait_ge(s_lf2, 1)
            for t in range(TILES):
                last = pe.transpose(bank(4)[:, t * HEADS2:(t + 1) * HEADS2], logf[0:HEADS2, 0, META + t * P:META + (t + 1) * P],
                                    ident[0:HEADS2, 0:HEADS2])
            last.then_inc(s_ct, 1)
            pe.wait_ge(s_cc, 1)
            for r, n in enumerate((2048, 2048, HEADS2 * CTX - 2048)):
                pe.wait_ge(s_fs, r + 1)
                if r:
                    pe.wait_ge(s_fr, r)
                for c in range(0, n, CHUNK):
                    w_ = min(CHUNK, n - c)
                    last = pe.matmul(bank(4 + c // CHUNK)[:, 0:w_], ones, sq_tmp[:, c:c + w_], start=True, stop=True)
                last.then_inc(s_fp, 1)
            pe.wait_ge(s_fr, 3)
            turn_values(3, G["fox_gate"])
            pe.wait_ge(s_vr, 6)
            for k in range(4):
                pe.wait_ge(acc_free[k], G["out2"].used0[k] + 1)
            pe.wait_ge(s_fn, 3)

            of = lambda m: ((m - M_TWO) // 16, (m - M_TWO) % 2, (m - M_TWO) % 16 // 2)

            def two_scores(m):
                t, fox, hd = of(m)
                nk = META + (t + 1) * P
                z, tok = bank(m % 3)[:, 0:nk], slice(t * P, (t + 1) * P)
                if not fox:
                    return pe.matmul(z, sqT[:, hd, tok], skT[:, hd, 0:nk], start=True, stop=True)
                pe.matmul(z, fqT[:, hd, tok], fkT[:, hd, 0:nk], start=True, stop=False)
                return pe.matmul(z, pick[0:HEADS2, hd], logf[0:HEADS2, 1, 0:nk], start=False, stop=True)

            def two_values(m, j, n_):
                t, fox, hd = of(m)
                cols = slice(hd * P, (hd + 1) * P)
                if n_ == 0:
                    return (fv_meta if fox else sv_meta)[0:META, cols]
                return (fv if fox else sv)[:, n_ - 1, cols]

            attend(M_TWO, 32, 1, two_scores,
                   lambda m: [(0, META)] + [(META + b * P, P) for b in range((m - M_TWO) // 16 + 1)], two_values,
                   lambda m, j: prob2[:, m % 3], lambda m: probT2[:, m % 2])
            pe.wait_ge(s_mg, 2 * TILES)
            turn("merged", False, lambda t, s: merged[:, t, s * P:(s + 1) * P])
            pe.wait_ge(s_xT, g0["merged"] + 8)
            product(G["out2"], x_)
            turn("ffn", True, lambda t, s: xn3[:, t, s * P:(s + 1) * P])
            pe.wait_ge(s_xT, g0["ffn"] + 8)
            pe.wait_ge(s_erow, 32)
            for k in range(4):
                for j in range(4):
                    last = pe.transpose(bank(4 + k)[:, j * P:(j + 1) * P], subk[:, 4 * k + j], ident)
                last.then_inc(s_sk, 1)
            product(G["query"], x_)
            g = G["query"]
            for k in range(4):
                pe.wait_ge(acc_free[k], g.used0[k] + g.bodies + 1)
            pe.wait_ge(s_skT, 4)
            for t in range(TILES):
                for k in range(2 * E_HEADS):
                    last = pe.matmul(bank(4 * t + k // 4)[:, (k % 4) * P:(k % 4 + 1) * P], pqT[:, k, t * P:(t + 1) * P], subkT[:, k],
                                     start=True, stop=True)
                last.then_inc(s_sp, 1)


def kernel(**inputs):
    import concourse.bacc as bacc
    from concourse.bass_utils import run_bass_kernel_spmd

    nc = bacc.Bacc("TRN2", target_bir_lowering=False, num_devices=1)
    arrays, dram = {}, {}
    for name, value in inputs.items():
        value = np.ascontiguousarray(value)
        arrays["in_" + name] = value
        dram[name] = nc.dram_tensor("in_" + name, value.shape, mybir.dt.from_np(value.dtype), kind="ExternalInput").ap()
    out = nc.dram_tensor("out_x", (1, SEQ, D), FP32, kind="ExternalOutput").ap()
    build(nc, dram, out)
    result = run_bass_kernel_spmd(nc, [arrays], core_ids=[0])
    return result.results[0]["out_x"]
```

```python
import numpy as np
import concourse.bass as bass
from concourse import mybir
from concourse.alu_op_type import AluOpType as ALU
from contextlib import ExitStack

FP32 = mybir.dt.float32
I32 = mybir.dt.int32
U32 = mybir.dt.uint32
FP32R = mybir.dt.float32r
ACT = mybir.ActivationFunctionType
AX = mybir.AxisListType.X

P = 128
D = 2048
SEQ = 256
TILES = SEQ // P
META = 16
CTX = META + SEQ
SLABS = D // P
FF = 4 * D
R_W, R_HEAD = 1024, 64
R_HEADS = R_W // R_HEAD
LORA_W, LORA_A, LORA_G = 64, 64, 160
RWKV_COLS = 3 * R_W + LORA_W + LORA_A + LORA_G
A_W, A_HEAD, A_HEADS, A_KV = 1024, 128, 8, 2
I_HEADS, I_HEAD = 16, 64
IN_COLS = RWKV_COLS + A_W + 2 * A_KV * A_HEAD + I_HEADS * I_HEAD + I_HEAD + I_HEADS
TOPK = min(256, SEQ // 4)
C_HEADS, C_HEAD = 4, 128
C_W = C_HEADS * C_HEAD
HEADS2, HEAD2 = 8, 128
W2 = HEADS2 * HEAD2
C_IN = 7 * W2 + HEADS2
E_HEADS, E_TOP, N_KEYS = 8, 16, 128
N_EXPERTS = N_KEYS * N_KEYS
THETA = 500000.0
XW0 = 3 * R_W
XG0 = XW0 + LORA_W + LORA_A
Q0 = RWKV_COLS
K0 = Q0 + A_W
V0 = K0 + A_KV * A_HEAD
QI0 = V0 + A_KV * A_HEAD
KI0 = QI0 + I_HEADS * I_HEAD
WI0 = KI0 + I_HEAD

CHUNK = 512
SLOTS = 4
SLOT_SLABS = 2
PARTS = 4
AHEAD = 3
NEG = -1.0e30
TAKEN = -3.0e38
E_HALF = 0.6065306597126334
TWO_PI_HI = 6.28125
TWO_PI_LO = 0.0019353071795864769
PI = 3.1415925


class Product:

    def __init__(self, name, w, k, col0, widths, tok, per_body, lo=META, hi=CTX, row0=0):
        self.name, self.w, self.k, self.col0, self.widths, self.tok = name, w, k, col0, widths, tok
        self.row0, self.slabs = row0, k // P
        self.per_body, self.bodies = per_body, len(widths) // per_body
        self.lo, self.hi = lo, hi
        self.tiles = k // (P * SLOT_SLABS)
        self.turns = self.tiles * per_body // SLOTS

    def uses(self, bank):
        if not self.tok:
            return sum(bank // 4 == c % 2 for c in range(self.per_body))
        return sum(bank // 2 == c % 2 for c in range(self.per_body))

    def slab(self, i, c, n):
        return i * (self.per_body * self.slabs) + (self.slab0 + c * self.slabs + n)

    def tile(self, i, c, j):
        t = c * self.tiles + j
        return t % SLOTS, i * self.turns + (self.turn0 + t // SLOTS + 1)


def lay_out(products):
    turn, slab, used = 0, 0, [0] * 8
    for g in products:
        g.turn0, g.slab0, g.used0 = turn, slab, list(used)
        turn += g.turns * g.bodies
        slab += g.slabs * len(g.widths)
        used = [u + g.uses(b) * g.bodies for b, u in enumerate(used)]


class Chain:

    def __init__(self, eng, sem):
        self.eng, self.sem, self.n = eng, sem, 0

    def __call__(self, ins):
        self.n += 1
        ins.then_inc(self.sem, 1)
        self.eng.wait_ge(self.sem, self.n)
        return self.n


def build(nc, A, out):
    with ExitStack() as ctx:
        sems = {}

        def sem(name):
            if name not in sems:
                sems[name] = ctx.enter_context(nc.semaphore(name))
            return sems[name]

        TOTAL = 53120
        X0 = 14816
        XN = SLABS * CTX
        BASE = X0 + 2 * XN
        with nc.sbuf_tensor("lasting", [P, BASE], FP32) as lasting, nc.sbuf_tensor("zone", [P, TOTAL - BASE], FP32) as zone_all:
            pass
        parts, place = {}, 0
        for name, off, n in (("w_hi", 4096, PARTS * CHUNK), ("w_lo", 4096 + PARTS * CHUNK, PARTS * CHUNK),
                             ("x_hi", X0, XN), ("x_lo", X0 + XN, XN),
                             ("hid_hi", BASE, 8192), ("hid_lo", BASE + 8192, 8192),
                             ("mem_hi", BASE + 18144, 4096), ("mem_lo", BASE + 18144 + 4096, 4096), ("", TOTAL, 0)):
            if off > place:
                ctx.enter_context(nc.sbuf_tensor(f"space_{place}", [P, off - place], FP32))
            if n:
                parts[off] = ctx.enter_context(nc.sbuf_tensor(name, [P, n], FP32R))
            place = off + n
        ints = ctx.enter_context(nc.sbuf_tensor("ints", [P, 32], I32))
        acc = ctx.enter_context(nc.psum_tensor("acc", [P, 8, CHUNK], FP32))
        top = [0]

        def at(off, *shape):
            n = 1
            for s in shape:
                n *= s
            assert off + n <= TOTAL, (off, n)
            v = zone_all[:, off - BASE:off - BASE + n] if off >= BASE else lasting[:, off:off + n]
            assert off >= BASE or off + n <= BASE
            if len(shape) == 2:
                v = v.rearrange("p (a b) -> p a b", a=shape[0])
            if len(shape) == 3:
                v = v.rearrange("p (a b c) -> p a b c", a=shape[0], b=shape[1])
            return v

        def part_at(off, *shape):
            n = shape[0] * shape[1]
            return parts[off][:, 0:n].rearrange("p (a b) -> p a b", a=shape[0])

        def take(*shape):
            n = 1
            for s in shape:
                n *= s
            v = at(top[0], *shape)
            top[0] += n
            return v

        ring = take(SLOTS, SLOT_SLABS, CHUNK)
        w_hi, w_lo = part_at(top[0], PARTS, CHUNK), part_at(top[0] + PARTS * CHUNK, PARTS, CHUNK)
        top[0] += 2 * PARTS * CHUNK
        h = take(TILES, D)
        ident = take(P)
        tri = take(P)
        upper = take(P)
        upper16 = take(P)
        lower16 = take(P)
        lower_rest = take(P)
        halves = take(8)[:, 0:2]
        causal = take(TILES, CTX)
        strict = take(TILES, CTX)
        gains = take(7, SLABS)
        small = take(552)
        assert top[0] == X0
        xT = (part_at(X0, SLABS, CTX), part_at(X0 + XN, SLABS, CTX))
        top[0] += 2 * XN
        base = top[0]
        assert base == BASE

        bank = lambda k: acc[:, k, :]
        ssum, var, rstd = small[:, 0:4], small[:, 4:8], small[:, 8:12]
        rmax, rsum, rinv = small[:, 12:20], small[:, 20:28], small[:, 28:36]
        invf = small[:, 36:52]
        posf = small[:, 52:54]
        posi = ints[:, 0:2]
        m8 = small[:, 54:62]
        kss = small[:, 62:78]
        bonus = small[:, 78:110].rearrange("p (t h) -> p t h", t=TILES)
        decayC = small[:, 110:174].rearrange("p (t h c) -> p t h c", t=TILES, h=R_HEADS)
        sincos = small[:, 174:238].rearrange("p (k t j) -> p k t j", k=2, t=TILES)
        rmean, rvar = small[:, 238:254], small[:, 254:270]
        turns_f = small[:, 270:302].rearrange("p (t j) -> p t j", t=TILES)
        ang = small[:, 302:334].rearrange("p (t j) -> p t j", t=TILES)
        turns_i = ints[:, 0:32].rearrange("p (t j) -> p t j", t=TILES)
        zero_row = small[:, 334:335]
        yst = small[:, 424:488].rearrange("p (k t h) -> p k t h", k=2, t=TILES)
        turn_tmp = small[:, 488:552].rearrange("p (k t j) -> p k t j", k=2, t=TILES)

        zone = base
        p = at(zone, TILES, IN_COLS); zone += TILES * IN_COLS
        ckT = at(zone, C_HEADS, SEQ); zone += C_HEADS * SEQ
        cv = at(zone, TILES, C_W); zone += TILES * C_W
        Z = zone
        mem = at(base, TILES, D)
        memT = (part_at(Z + TILES * D, SLABS, SEQ), part_at(Z + 2 * TILES * D, SLABS, SEQ))
        xn = at(Z, TILES, D)
        prev = at(Z + TILES * D, TILES, RWKV_COLS)
        mu = at(Z + TILES * D + TILES * RWKV_COLS, RWKV_COLS)
        z = Z
        key_t = at(z, TILES, R_W); z += TILES * R_W
        beta_t = at(z, TILES, R_W); z += TILES * R_W
        gate = at(z, TILES, R_W); z += TILES * R_W
        zs = z
        logd = at(z, R_W); z += R_W
        params = at(z, 4, R_W); z += 4 * R_W
        w0 = gate[:, 1]
        lora_up = at(X0, 3, R_W)
        loraT = at(X0 + 3 * R_W, 3, SEQ)
        x_rest = X0 + 3 * R_W + 3 * SEQ
        state = at(x_rest, R_W)
        lnx = at(x_rest + R_W, 2, R_W)
        tmp = at(x_rest + 3 * R_W, R_W)
        n4 = 4 * P
        spots = [X0 + i * n4 for i in range(7)] + [x_rest + 3 * R_W + i * n4 for i in range(3)]
        spots += [zs + i * n4 for i in range(26 - len(spots))]
        scr = [at(spot, 4, P) for spot in spots]
        assert X0 + 7 * n4 <= x_rest and spots[9] + n4 <= X0 + 2 * XN

        z = Z + 3 * TILES * R_W
        qiT = at(z, TILES, I_HEADS // 2, P); z += SEQ * I_HEADS // 2
        qT = at(z, TILES, A_HEADS, P); z += SEQ * A_HEADS
        score = at(z, TILES, SEQ); z += TILES * SEQ
        left = at(z, SEQ); z += SEQ
        unsel = at(z, TILES, SEQ); z += TILES * SEQ
        prob = at(z, 3, 2 * CTX); z += 6 * CTX
        probT = at(z, 2, 4 * P); z += 8 * P
        assert z <= TOTAL, z
        cqT = at(Z + 2 * TILES * R_W, C_HEADS, SEQ)
        co = at(Z + 2 * TILES * R_W + C_HEADS * SEQ, TILES, C_W)
        rel = at(X0, 4, 2, SEQ)
        kiT = at(x_rest + R_W - 3 * SEQ, SEQ)
        assert X0 + 8 * SEQ * 2 <= x_rest + R_W - 3 * SEQ
        kT = at(x_rest + R_W - 2 * SEQ, A_KV, SEQ)
        y_sq = tmp
        z = TOTAL - 4 * (A_HEADS + A_KV) * 16 - TILES * P
        rot = at(z, 4, (A_HEADS + A_KV) * 16); z += 4 * (A_HEADS + A_KV) * 16
        keyI = at(z, TILES, P)
        assert max(spots) + n4 <= TOTAL - 4 * (A_HEADS + A_KV) * 16 - TILES * P
        HALF = FF // P // 2
        hidT = (part_at(base, HALF, SEQ), part_at(base + HALF * SEQ, HALF, SEQ))
        relu_now, square_now = at(base + 2 * HALF * SEQ + 4096, 4 * SEQ), at(base + 2 * HALF * SEQ + 4096 + 4 * SEQ, 4 * SEQ)
        xn_mlp = xn
        final_gain = at(Z + TILES * D, D)
        assert Z + TILES * D + D <= base + 2 * HALF * SEQ + 4096
        head_gains = small[:, 389:391]
        fbias = small[:, 391:392]
        eps_col = small[:, 392:393]
        nmax = small[:, 367:373].rearrange("p (b j) -> p b j", j=2)
        psums = small[:, 373:381].rearrange("p (b j) -> p b j", j=2)
        pinv = small[:, 381:389].rearrange("p (b j) -> p b j", j=2)
        z = base
        sqT = at(z, HEADS2, SEQ); z += HEADS2 * SEQ
        skT = at(z, HEADS2, CTX); z += HEADS2 * CTX
        sv = at(z, TILES, W2); z += TILES * W2
        sv_meta = at(z, W2); z += W2
        fqT = at(z, HEADS2, SEQ); z += HEADS2 * SEQ
        fkT = at(z, HEADS2, CTX); z += HEADS2 * CTX
        fv = at(z, TILES, W2); z += TILES * W2
        fv_meta = at(z, W2); z += W2
        fgate = at(z, TILES, W2); z += TILES * W2
        vT = at(z, HEADS2, CTX); z += HEADS2 * CTX
        merged = at(z, TILES, D); z += TILES * D
        xn2 = merged
        hmeta = fgate.rearrange("p t c -> p (t c)")
        ones = at(z, P); z += P
        prob2 = at(z, 3, CTX); z += 3 * CTX
        probT2 = at(z, 2, 3 * P); z += 6 * P
        stick = at(z, 3, 3, CTX); z += 9 * CTX
        seen = at(z, TILES, CTX); z += TILES * CTX
        pick = at(z, HEADS2, P); z += HEADS2 * P
        w_logit = at(z, SLABS, HEADS2); z += SLABS * HEADS2
        logf = at(z, 3, CTX); z += 3 * CTX
        cumf = at(z, TILES, HEADS2); z += TILES * HEADS2
        assert z <= TOTAL, z
        sq_tmp = merged.rearrange("p t d -> p (t d)")
        z = base
        hb = at(z, TILES, D); z += TILES * D
        gain_row = at(z, D); z += D
        pqT = at(z, 2 * E_HEADS, SEQ); z += 2 * E_HEADS * SEQ
        subk = at(z, 2 * E_HEADS, P); z += 2 * E_HEADS * P
        subkT = at(z, 2 * E_HEADS, P); z += 2 * E_HEADS * P
        xn3 = at(z, TILES, D); z += TILES * D
        scores = at(z, TILES, 2 * E_HEADS * N_KEYS); z += TILES * 2 * E_HEADS * N_KEYS
        bufs_z = z
        best1 = at(z, 2 * E_HEADS, E_TOP); z += 2 * E_HEADS * E_TOP
        bestf = at(z, 2 * E_HEADS, E_TOP); z += 2 * E_HEADS * E_TOP
        work1 = at(z, 256); z += 256
        best2 = at(z, TILES, E_HEADS, E_TOP); z += TILES * E_HEADS * E_TOP
        hot = at(z, E_HEADS * E_TOP, E_TOP); z += E_HEADS * E_TOP * E_TOP
        picked = at(z, 3, E_HEADS * E_TOP); z += 3 * E_HEADS * E_TOP
        iota16 = at(z, E_TOP); z += E_TOP
        experts = at(z, TILES, P + 4).bitcast(U32); z += TILES * (P + 4)
        expert_now = at(z, 32).bitcast(U32); z += 32
        dots_now = at(z, 16); z += 16
        coef_now = at(z, 16); z += 16
        dots = at(z, TILES, P); z += TILES * P
        coef = at(z, TILES, P); z += TILES * P
        esum = at(z, TILES, E_HEADS); z += TILES * E_HEADS
        assert z <= TOTAL, z
        spots = [n * D for n in range(4)] + [base + (3 + n) * D for n in range(4)] + [X0 + n * D for n in range(4)]
        spots += [base + 2 * D, base + 7 * D, base + 8 * D, z]
        assert z + D <= TOTAL
        rows_buf = [at(spot, D) for spot in spots]
        junk = scores[:, 0]

        G = {}
        w = lambda n: A[n][0]
        for g in (
            Product("cross_k", w("w_kv_cross"), D, 0, [CHUNK], False, 1, 0, SEQ),
            Product("cross_v", w("w_kv_cross"), D, C_W, [CHUNK], True, 1, 0, SEQ),
            Product("in", w("w_in"), D, 0, [CHUNK] * 10, True, 2),
            Product("in_end", w("w_in"), D, 10 * CHUNK, [CHUNK, IN_COLS - 11 * CHUNK], True, 2),
            Product("mix", w("w_mix_out"), D, 0, [CHUNK] * 4, True, 2),
            Product("cross_q", w("w_q_cross"), D, 0, [CHUNK], False, 1),
            Product("cross_o", w("w_o_cross"), C_W, 0, [CHUNK] * 4, True, 4),
            Product("up0", w("w_up"), D, 0, [CHUNK] * (FF // CHUNK // 2), False, 2),
            Product("down0", w("w_down"), FF // 2, 0, [CHUNK] * 4, True, 2, 0, SEQ),
            Product("up1", w("w_up"), D, FF // 2, [CHUNK] * (FF // CHUNK // 2), False, 2),
            Product("down1", w("w_down"), FF // 2, 0, [CHUNK] * 4, True, 2, 0, SEQ, FF // 2),
            Product("sb_q", w("w_in_2"), D, 0, [CHUNK] * 2, False, 2),
            Product("sb_kv", w("w_in_2"), D, W2, [CHUNK] * 4, False, 4, 0),
            Product("fox_q", w("w_in_2"), D, 3 * W2, [CHUNK] * 2, False, 2),
            Product("fox_kv", w("w_in_2"), D, 4 * W2, [CHUNK] * 4, False, 4, 0),
            Product("fox_gate", w("w_in_2"), D, 6 * W2, [CHUNK] * 2, True, 2),
            Product("out2", w("w_out_2"), D, 0, [CHUNK] * 4, True, 2),
            Product("query", w("peer_w_query_2"), D, 0, [CHUNK] * 4, False, 2),
        ):
            G[g.name] = g
        lay_out(list(G.values()))
        following = dict(zip(list(G)[:-1], list(G)[1:]))
        tile_full = [sem(f"tile_full{i}") for i in range(SLOTS)]
        hi_ready, lo_ready = sem("hi_ready"), sem("lo_ready")
        slab_used = sem("slab_used")
        acc_free = [sem(f"acc_free{i}") for i in range(8)]

        def chunk_done(eng, g, c, i=0):
            eng.wait_ge(slab_used, g.slab(i, c, g.slabs - 1) + PARTS + 1)

        n_groups = {"mem": 8, "x": 8, "mixed": 8, "cross": 8, "o": 2, "mlp": 8, "meta": 4, "mix2": 8, "merged": 8, "ffn": 8}
        g0, n0 = {}, 0
        for name in n_groups:
            g0[name] = n0
            n0 += n_groups[name]
        norm_tiles = {"mem": 2, "x": 2, "cross": 2, "mlp": 2, "final": 2, "meta": 1, "mix2": 2, "heads2": 4, "ffn": 2}
        norm_no = {name: n for n, name in enumerate(norm_tiles)}
        sums0, xn0 = {}, {}
        n0 = n1 = 0
        for name, k in norm_tiles.items():
            sums0[name], xn0[name] = n0, n1
            n0 += k
            n1 += k if name not in ("final", "heads2") else 0
        s_ss, s_var, s_sd, s_rstd, s_xn = (sem(n) for n in (
            "squares_summed", "variance_ready", "deviation_ready", "scale_ready", "normed_ready"))
        s_tr, s_xh, s_xT = sem("transposed"), sem("x_hi_ready"), sem("xT_ready")
        s_const, s_vec, s_act, s_pool = sem("const_ready"), sem("vector_step"), sem("scalar_step"), sem("pool_step")
        s_gain, s_x, s_mem = sem("gains_loaded"), sem("x_loaded"), sem("mem_loaded")

        STAGES = [("turned", 1, 1), ("pairs", 1, 0), ("square", 1, 1), ("fourth", 1, 1), ("eighth", 1, 1),
                  ("inverse", 1, 0), ("solve0", 1, 1), ("solve1", 1, 0), ("solve2", 1, 0), ("solve3", 1, 0),
                  ("w_turned", 0, 1), ("sa0", 1, 0), ("state0", 1, 0), ("sa1", 1, 0), ("state1", 1, 0), ("y", 0, 1)]
        stage_no = {s[0]: n for n, s in enumerate(STAGES)}
        g_pe, g_ve, g_ac = sem("group_products"), sem("group_vector"), sem("group_scalar")

        def g_count(pair, name, u, who):
            n = stage_no[name]
            inside = n if who == 0 else sum(s[who] for s in STAGES[:n])
            whole = len(STAGES) if who == 0 else sum(s[who] for s in STAGES)
            return (pair * whole + inside) * 2 + u + 1

        def g_wait(eng, pair, name, u, who):
            if who == 0 or STAGES[stage_no[name]][who]:
                eng.wait_ge((g_pe, g_ve, g_ac)[who], g_count(pair, name, u, who))

        PAIRS = [(t, q) for t in range(TILES) for q in (0, 2)]
        (sAT, sBT, sKT, sRT, sD, sL, sDT, sAK, sRB, sRK, sX, sR, sY0) = range(13)

        def S_(u, n):
            return scr[u * 13 + n]

        def loop(eng, n, body):
            if n == 1:
                body(0)
            else:
                with eng.Fori(0, n) as i:
                    body(i)

        s_shift, s_mixed, s_par, s_lora = sem("shifted_loaded"), sem("mixed"), sem("params_loaded"), sem("lora_loaded")
        s_tanh, s_sig, s_lt, s_lT = sem("tanh_done"), sem("gate_sigmoid"), sem("lora_turned"), sem("loraT_ready")
        s_zd, s_ad, s_gd, s_cd = sem("z_done"), sem("a_done"), sem("g_done"), sem("c_done")
        s_zv, s_av, s_ze, s_ae, s_ld, s_kss, s_ksd = (sem(n) for n in (
            "z_biased", "a_biased", "z_exp", "a_exp", "logd_ready", "kk_summed", "kk_root"))
        s_cp, s_ea, s_en, s_kd, s_ep, s_el, s_gate = (sem(n) for n in (
            "c_before", "exp_before", "exp_minus", "key_scaled", "exp_plus", "elementwise", "gate_copied"))
        s_eg = sem("lora_exp")
        s_yr0, s_lnx, s_yv, s_ysd, s_yr, s_out = (sem(n) for n in (
            "y_rooted", "lnx_loaded", "y_var", "y_sd", "y_rwkv", "out_written"))
        a_S, a_sm, a_pr, a_T, a_PT, a_O, a_done = (sem(n) for n in (
            "scores_done", "max_ready", "prob_ready", "prob_turned", "probT_ready", "output_done", "output_read"))
        M_DSA, M_CROSS, M_TWO = 0, 8, 12
        s_ang, s_trig, s_rope, s_kturn, s_kT2 = (sem(n) for n in ("angle_ready", "sines_ready", "rotated", "keys_turned", "keyT_ready"))
        s_qturn, s_qT2, s_ix, s_rel, s_acc2, s_sel = (sem(n) for n in (
            "queries_turned", "queryT_ready", "index_product", "relu_ready", "index_added", "selected"))
        s_meta, s_c2, s_vt, s_vr, s_lg, s_lf0, s_lf1, s_lf2, s_ct, s_cc = (sem(n) for n in (
            "meta_loaded", "const2_ready", "values_turned", "values_read", "logits_done", "logits_biased", "logits_log",
            "cum_ready", "cum_turned", "cum_column"))
        s_fs, s_fp, s_fr, s_fn, s_l, s_fg, s_mg, s_erow = (sem(n) for n in (
            "fox_squares", "fox_sums", "fox_roots", "fox_normed", "stick_log", "gate2_exp", "merged_ready", "expert_rows_loaded"))
        s_sk, s_skT, s_sp, s_sc, s_bs, s_be, s_ix0, s_dot, s_gelu, s_coef, s_hb = (sem(n) for n in (
            "subkeys_turned", "subkeysT_ready", "key_scores_done", "key_scores_read", "best_shifted", "best_exp",
            "experts_ready", "dots_ready", "gelu_done", "coef_ready", "hb_ready"))
        s_now = sem("experts_staged")
        rows_full = [sem(f"rows_full{n}") for n in range(4)]
        rows_used = [sem(f"rows_used{n}") for n in range(4)]
        s_hid, s_fin, s_fgain = sem("hidden_ready"), sem("final_norm"), sem("final_gain_loaded")
        block = ctx.enter_context(nc.Block())

        @block.sync
        def _(sp):
            def stream(g):
                rows = g.w.rearrange("(s p) n -> p s n", p=P)

                def body(i):
                    for c in range(g.per_body):
                        width = g.widths[c]
                        for j in range(g.tiles):
                            slot = g.tile(i, c, j)[0]
                            if g.slab0 or c or j >= SLOTS:
                                sp.wait_ge(lo_ready, g.slab(i, c, SLOT_SLABS * (j + 1 - SLOTS)))
                            cols = bass.ds(i * (g.per_body * CHUNK) + g.col0 + c * CHUNK, width)
                            r0 = g.row0 // P + SLOT_SLABS * j
                            sp.dma_start(ring[:, slot, :, 0:width], rows[:, r0:r0 + SLOT_SLABS, cols]
                                         ).then_inc(tile_full[slot], 16)
                loop(sp, g.bodies, body)

            for t in range(TILES):
                sp.dma_start(mem[:, t], A["mem"][0, t * P:(t + 1) * P, :]).then_inc(s_mem, 16)
            for t in range(TILES):
                sp.dma_start(h[:, t], A["x"][0, t * P:(t + 1) * P, :]).then_inc(s_x, 16)
            for g in G.values():
                stream(g)
            for t in range(TILES):
                for k in range(4):
                    sp.wait_ge(rows_used[k], 2 * TILES * P // 16 + 1)
                sp.dma_start(out[0, t * P:(t + 1) * P, :], h[:, t]).then_inc(s_out, 16)
            sp.wait_ge(s_out, 16 * TILES)

        @block.gpsimd
        def _(pool):
            step = Chain(pool, s_pool)

            def keep(m, pattern, base, cm, cmp=ALU.is_ge, fill=0.0):
                return step(pool.affine_select(out=m, in_=m, pattern=pattern, base=base,
                                               channel_multiplier=cm, compare_op=cmp, fill=fill))

            def block_diagonal(m, b):
                v = m.rearrange("p (n b) -> p n b", b=b)
                keep(v, [[-b, P // b], [0, b]], 0, 1)
                keep(v, [[b, P // b], [0, b]], b - 1, -1)

            def rests(*names):
                for name in names:
                    g = G[name]

                    def body(i):
                        for c in range(g.per_body):
                            width = g.widths[c]
                            for s in range(g.slabs):
                                slot, k = g.tile(i, c, s // SLOT_SLABS)[0], s % PARTS
                                pool.wait_ge(hi_ready, g.slab(i, c, s) + 1)
                                pool.tensor_tensor(w_lo[:, k, 0:width], ring[:, slot, s % SLOT_SLABS, 0:width],
                                                   w_hi[:, k, 0:width].bitcast(FP32), ALU.subtract).then_inc(lo_ready, 1)
                    loop(pool, g.bodies, body)

            step(pool.memset(ident, 0.0))
            keep(ident, [[-1, P]], 0, 1, ALU.not_equal, 1.0)
            for m in (tri, upper, upper16):
                step(pool.memset(m, 1.0))
                keep(m, [[1, P]], 0 if m is tri else -1, -1)
                block_diagonal(m, 16 if m is upper16 else 64)
            for m, b in ((lower16, 16), (lower_rest, 64)):
                step(pool.memset(m, 1.0))
                keep(m, [[-1, P]], -1, 1)
                block_diagonal(m, b)
            step(pool.tensor_tensor(lower_rest, lower_rest, lower16, ALU.subtract))
            step(pool.memset(halves, 1.0))
            keep(halves, [[-64, 2]], 0, 1)
            keep(halves, [[64, 2]], 63, -1)
            for m, off in ((causal, 0), (strict, -1)):
                step(pool.memset(m, 0.0))
                for t in range(TILES):
                    keep(m[:, t, META:CTX], [[-1, SEQ]], t * P + off, 1, fill=NEG)
            pool.memset(zero_row, 0.0).then_inc(s_const, 1)

            step(pool.memset(eps_col, 1e-6))
            rests("cross_k", "cross_v", "in", "in_end")
            pool.wait_ge(s_mixed, TILES)
            pool.dma_start(w0, A["w_decay0"][0].partition_broadcast(P)).then_inc(s_par, 16)
            for n, name in enumerate(("a0", "k_k", "k_a")):
                pool.dma_start(params[:, n], A[name][0].partition_broadcast(P)).then_inc(s_par, 16)
            pool.dma_start(params[:, 3], A["r_k"][0].rearrange("h n -> (h n)").partition_broadcast(P)).then_inc(s_par, 16)
            TT = pool.tensor_tensor
            pool.wait_ge(s_trig, 1)
            for k in range(4):
                pool.wait_ge(acc_free[k], G["mix"].used0[k] + 1)
            for t in range(TILES):
                for col, heads_n, width, half, stride in ((Q0, A_HEADS + A_KV, A_HEAD, 16, 1), (QI0, I_HEADS + 1, I_HEAD, 8, 2)):
                    x = p[:, t, col:col + heads_n * width].rearrange("p (h d) -> p h d", h=heads_n)
                    x1, x2 = x[:, :, 0:half], x[:, :, half:2 * half]
                    sn, cs = (sincos[:, k, t, 0:16:stride].unsqueeze(1).to_broadcast([P, heads_n, half]) for k in range(2))
                    r = [rot[:, k, 0:heads_n * half].rearrange("p (h d) -> p h d", h=heads_n) for k in range(4)]
                    TT(r[0], x1, cs, ALU.mult)
                    TT(r[1], x2, sn, ALU.mult)
                    TT(r[2], x2, cs, ALU.mult)
                    step(TT(r[3], x1, sn, ALU.mult))
                    TT(x1, r[0], r[1], ALU.subtract)
                    step(TT(x2, r[2], r[3], ALU.add))
                step(pool.tensor_scalar(p[:, t, WI0:WI0 + I_HEADS], p[:, t, WI0:WI0 + I_HEADS], (I_HEADS * I_HEAD) ** -0.5, None, ALU.mult))
                pool.tensor_copy(keyI[:, t].rearrange("p (a d) -> p a d", a=2),
                                 p[:, t, KI0:KI0 + I_HEAD].unsqueeze(1).to_broadcast([P, 2, I_HEAD])).then_inc(s_rope, 1)
            for u in range(2):
                g_wait(pool, len(PAIRS) - 1, "y", u, 2)
            pool.wait_ge(s_lnx, 32)
            heads = lambda x: x.rearrange("p (h n) -> p h n", n=R_HEAD)
            bc = lambda x: x.unsqueeze(2).to_broadcast([P, R_HEADS, R_HEAD])

            def head_sums(dst, x):
                part, n = heads(y_sq), R_HEAD // 2
                while n > 1:
                    step(TT(part[:, :, 0:n], x[:, :, 0:n], x[:, :, n:2 * n], ALU.add))
                    x, n = part, n // 2
                step(TT(dst, part[:, :, 0], part[:, :, 1], ALU.add))

            for t in range(TILES):
                y = key_t[:, t]
                head_sums(yst[:, 0, t], heads(y))
                step(pool.tensor_scalar(yst[:, 0, t], yst[:, 0, t], 1.0 / R_HEAD, None, ALU.mult))
                step(TT(heads(y), heads(y), bc(yst[:, 0, t]), ALU.subtract))
                step(TT(y_sq, y, y, ALU.mult))
                head_sums(yst[:, 1, t], heads(y_sq))
                pool.tensor_scalar(yst[:, 1, t], yst[:, 1, t], 1.0 / R_HEAD, 64e-5, ALU.mult, ALU.add).then_inc(s_yv, 1)
            pool.wait_ge(s_ysd, 1)
            for t in range(TILES):
                y = key_t[:, t]
                step(TT(heads(y), heads(y), bc(yst[:, 1, t]), ALU.mult))
                step(TT(y, y, lnx[:, 0], ALU.mult))
                step(TT(y, y, lnx[:, 1], ALU.add))
                step(TT(heads(y_sq), heads(p[:, t, 2 * R_W:3 * R_W]), bc(bonus[:, t]), ALU.mult))
                step(TT(y, y, y_sq, ALU.add))
                TT(y, y, gate[:, t], ALU.mult).then_inc(s_yr, 1)

            rests("mix", "cross_q", "cross_o", "up0", "down0", "up1", "down1")
            for k in range(8):
                pool.wait_ge(acc_free[k], G["sb_q"].used0[k] + 1)
            pool.dma_start(hmeta[0:META], A["meta_tokens_2"]).then_inc(s_meta, 16)
            pool.dma_start(w_logit, A["w_in_2"][0].rearrange("(s p) n -> p s n", p=P)[:, :, 7 * W2:C_IN]).then_inc(s_meta, 16)
            step(pool.memset(pick[0:HEADS2], 0.0))
            keep(pick[0:HEADS2], [[-1, HEADS2], [0, P]], 0, 1, ALU.not_equal, 1.0)
            pool.memset(ones, 1.0).then_inc(s_c2, 1)
            rests("sb_q", "sb_kv", "fox_q", "fox_kv", "fox_gate", "out2", "query")
            zero4 = zero_row.bitcast(U32).to_broadcast([P, 4])
            now = lambda n: expert_now[:, 4 * (n % 8):4 * (n % 8) + 4]
            for k in range(4):
                pool.sem_inc(rows_used[k], 1)
            pool.wait_ge(s_sc, TILES)
            per, rounds, staged = P // 32, 0, 0
            for phase, table in enumerate((A["peer_u_2"][0], A["peer_v_2"][0])):
                for t in range(TILES):
                    pool.wait_ge(s_ix0, t + 1)
                    if staged:
                        pool.wait_ge(s_now, staged)
                    pool.tensor_tensor(now(0), experts[:, t, 0:4], zero4, ALU.add).then_inc(s_now, 1)
                    with pool.Fori(0, per) as i:
                        for n in range(8):
                            pool.wait_ge(rows_used[n % 4], i * 2 + (rounds + n // 4 + 1))
                            pool.wait_ge(s_now, i * 8 + (staged + n + 1))
                            pool.tensor_tensor(now(n + 1), experts[:, t, bass.ds(i * 32 + 4 * (n + 1), 4)], zero4, ALU.add
                                               ).then_inc(s_now, 1)
                            for j in range(4):
                                pool.indirect_dma_start(
                                    out=rows_buf[4 * (n % 4) + j], out_offset=None, in_=table,
                                    in_offset=bass.IndirectOffsetOnAxis(ap=now(n)[:, j:j + 1], axis=0)
                                ).then_inc(rows_full[n % 4], 16)
                    rounds, staged = rounds + 2 * per, staged + 8 * per + 1

        @block.scalar
        def _(act):
            step = Chain(act, s_act)
            for dst, name in [(gains[:, 0], "norm_mem"), (gains[:, 1], "norm_mix"), (gains[:, 2], "norm_cross"),
                              (gains[:, 3], "norm_mlp"), (gains[:, 4], "norm_mix_2"), (gains[:, 5, 0:8], "sb_out_gain_2"),
                              (gains[:, 5, 8:16], "fox_out_gain_2"), (gains[:, 6], "norm_ffn_2"),
                              (head_gains[:, 0:1], "fox_q_gain_2"), (head_gains[:, 1:2], "fox_k_gain_2")]:
                act.dma_start(dst, A[name][0].rearrange("(s p) -> p s", p=P), allow_slow_non_contiguous=True).then_inc(s_gain, 16)
            act.dma_start(fbias[0:HEADS2], A["b_forget_2"].rearrange("l h -> h l"), allow_slow_non_contiguous=True).then_inc(s_gain, 16)
            act.dma_start(posi, A["positions"][0].rearrange("(t p) -> p t", p=P), allow_slow_non_contiguous=True).then_inc(s_gain, 16)

            def norm_rows(name, src, rows=P, xn=xn):
                tiles = norm_tiles[name]
                for t in range(tiles):
                    act.activation(xn[0:rows, t], src(t), ACT.Square, accum_out=ssum[0:rows, t:t + 1]
                                   ).then_inc(s_ss, 1)
                act.wait_ge(s_var, norm_no[name] + 1)
                act.activation(rstd[0:rows, 0:tiles], var[0:rows, 0:tiles], ACT.Sqrt).then_inc(s_sd, 1)
                act.wait_ge(s_rstd, norm_no[name] + 1)
                if name == "final":
                    return
                act.wait_ge(s_ss, sums0[name] + tiles)
                for t in range(tiles):
                    act.activation(xn[0:rows, t], src(t), ACT.Copy, scale=var[0:rows, t:t + 1]
                                   ).then_inc(s_xn, 1)

            def hi(g, i, c, s, width=None):
                width = width or g.widths[min(c, len(g.widths) - 1)]
                slot, turn = g.tile(i, c, s // SLOT_SLABS)
                if s % SLOT_SLABS == 0:
                    act.wait_ge(tile_full[slot], 16 * turn)
                act.wait_ge(slab_used, g.slab(i, c, s) + 1)
                act.activation(w_hi[:, s % PARTS, 0:width], ring[:, slot, s % SLOT_SLABS, 0:width], ACT.Copy).then_inc(hi_ready, 1)

            def round_and_read(g, read=lambda i, c: None, before_last=None):
                def chunk(i, c, last):
                    for s in range(AHEAD, g.slabs):
                        hi(g, i, c, s)
                    if last and g.name in following:
                        for s in range(AHEAD):
                            hi(G[following[g.name]], 0, 0, s)
                    elif not last:
                        for s in range(AHEAD):
                            hi(g, i, c + 1, s)
                    read(i, c)

                def body(i):
                    for c in range(g.per_body):
                        chunk(i, c, False)
                if g.bodies > 1:
                    loop(act, g.bodies - 1, body)
                if before_last:
                    before_last()
                for c in range(g.per_body):
                    chunk(g.bodies - 1, c, c == g.per_body - 1)

            def round_turned(name, dst, gain, rows=P, tiles=TILES, slabs=SLABS, off=META):
                for t in range(tiles):
                    for k in range(slabs // 4):
                        group = g0[name] + t * (slabs // 4) + k
                        act.wait_ge(s_tr, group + 1)
                        src = bank(4 + group % 4)[:, 0:4 * rows].rearrange("p (s c) -> p s c", s=4)
                        cols = slice(off + t * P, off + t * P + rows)
                        if gain is None:
                            act.activation(dst[:, 4 * k:4 * k + 4, cols], src, ACT.Copy).then_inc(s_xh, 1)
                            continue
                        for j in range(4):
                            last = act.activation(dst[:, 4 * k + j, cols], src[:, j], ACT.Copy,
                                                  scale=gains[:, gain, 4 * k + j:4 * k + j + 1])
                        last.then_inc(s_xh, 1)

            def reader(g, put):
                def read(i, c):
                    chunk_done(act, g, c, i)
                    for t in range(TILES):
                        k = 2 * (c % 2) + t
                        put(t, i, c, bank(k)[:, 0:g.widths[c]]).then_inc(acc_free[k], 1)
                return read

            act.wait_ge(s_mem, 16 * TILES)
            norm_rows("mem", lambda t: mem[:, t])
            act.wait_ge(s_gain, 16 * 12)
            round_turned("mem", memT[0], 0, off=0)
            act.wait_ge(s_x, 16 * TILES)
            norm_rows("x", lambda t: h[:, t])
            round_turned("x", xT[0], 1)
            for s in range(AHEAD):
                hi(G["cross_k"], 0, 0, s)

            def read_ck(i, c):
                chunk_done(act, G["cross_k"], 0)
                for f in range(4):
                    act.activation(ckT[:, f], bank(f)[:, 0:SEQ], ACT.Copy).then_inc(acc_free[f], 1)
            round_and_read(G["cross_k"], read_ck)
            round_and_read(G["cross_v"], reader(G["cross_v"], lambda t, i, c, src: act.activation(cv[:, t], src, ACT.Copy)))
            g = G["in"]

            def shift():
                act.wait_ge(s_ang, 1)
                act.activation(sincos[:, 0], ang, ACT.Sin)
                act.wait_ge(s_ang, 2)
                act.activation(sincos[:, 1], turns_f, ACT.Sin).then_inc(s_trig, 1)
                act.dma_start(mu, A["rwkv_mu"][0].partition_broadcast(P)).then_inc(s_shift, 16)
                for k in range(4):
                    act.wait_ge(acc_free[k], g.used0[k] + g.bodies)
                for t in range(TILES):
                    act.dma_start(prev[1:P, t], p[0:P - 1, t, 0:RWKV_COLS]).then_inc(s_shift, 16)
                act.dma_start(prev[0:1, 1], p[P - 1:P, 0, 0:RWKV_COLS]).then_inc(s_shift, 16)
            round_and_read(g, reader(g, lambda t, i, c, src: act.activation(
                p[:, t, bass.ds(i * (2 * CHUNK) + c * CHUNK, CHUNK)], src, ACT.Copy)), shift)
            g = G["in_end"]
            round_and_read(g, reader(g, lambda t, i, c, src: act.activation(
                p[:, t, G["in_end"].col0 + c * CHUNK:G["in_end"].col0 + c * CHUNK + G["in_end"].widths[c]], src, ACT.Copy)))
            act.dma_start(lora_up[0:LORA_W, 0], A["w_decay_up"][0]).then_inc(s_lora, 16)
            act.dma_start(lora_up[LORA_W:P, 0], A["a_up"][0]).then_inc(s_lora, 16)
            act.dma_start(lora_up[:, 1], A["g_up"][0, 0:P]).then_inc(s_lora, 16)
            act.dma_start(lora_up[0:LORA_G - P, 2], A["g_up"][0, P:LORA_G]).then_inc(s_lora, 16)
            act.dma_start(lnx[:, 0], A["lnx_w"][0].partition_broadcast(P)).then_inc(s_lnx, 16)
            act.dma_start(lnx[:, 1], A["lnx_b"][0].partition_broadcast(P)).then_inc(s_lnx, 16)

            act.wait_ge(s_mixed, TILES)
            for t in range(TILES):
                xw = p[:, t, XW0:XW0 + LORA_W]
                xg = p[:, t, XG0:XG0 + LORA_G]
                act.activation(xw, xw, ACT.Tanh).then_inc(s_tanh, 1)
                act.activation(xg, xg, ACT.Exp, scale=-1.0).then_inc(s_eg, 1)
            for t in range(TILES):
                act.wait_ge(s_zv, t + 1)
                act.activation(tmp, tmp, ACT.Exp, scale=-1.0).then_inc(s_ze, 1)
                act.wait_ge(s_av, t + 1)
                act.activation(beta_t[:, t], beta_t[:, t], ACT.Exp, scale=-1.0).then_inc(s_ae, 1)
                act.wait_ge(s_gd, t + 1)
                act.activation(gate[:, t], acc[:, 0:2].rearrange("p a b -> p (a b)"), ACT.Copy).then_inc(s_gate, 1)
                act.wait_ge(s_kss, t + 1)
                act.activation(kss, kss, ACT.Sqrt).then_inc(s_ksd, 1)
                act.wait_ge(s_cp, t + 1)
                act.activation(tmp, tmp, ACT.Exp).then_inc(s_ea, 1)
                c_all = acc[:, 2:4].rearrange("p a b -> p (a b)")
                act.activation(logd, c_all, ACT.Exp, scale=-1.0).then_inc(s_en, 1)
                act.activation(decayC[0:R_HEAD, t], bank(6)[0:R_HEAD, 0:2 * R_HEADS].rearrange("p (h c) -> p h c", c=2),
                               ACT.Exp)
                act.wait_ge(s_kd, t + 1)
                act.activation(tmp, c_all, ACT.Exp).then_inc(s_ep, 1)

            for n, (t, q) in enumerate(PAIRS):
                def copy(u, dst, b):
                    return act.activation(dst, b, ACT.Copy)
                for u in range(2):
                    g_wait(act, n, "turned", u, 0)
                    B = 4 * u
                    copy(u, S_(u, sKT)[0:64], bank(B + 2)[0:64].rearrange("p (j c) -> p j c", j=4))
                    copy(u, S_(u, sRT)[0:64], bank(B + 3)[0:64].rearrange("p (j c) -> p j c", j=4)).then_inc(g_ac, 1)
                b4 = lambda k: bank(k).rearrange("p (j c) -> p j c", j=4)
                for u in range(2):
                    B = 4 * u
                    g_wait(act, n, "square", u, 0)
                    copy(u, S_(u, sKT), b4(B + 1))
                    copy(u, S_(u, sBT), b4(B + 2))
                    cols = slice((q + u) * 256, (q + u) * 256 + 256)
                    copy(u, S_(u, sR)[:, :, 0:64], key_t[:, t, cols].rearrange("p (j c) -> p j c", j=4))
                    copy(u, S_(u, sR)[:, :, 64:128], b4(B + 3)[:, :, 0:64]).then_inc(g_ac, 1)
                for u in range(2):
                    B = 4 * u
                    g_wait(act, n, "fourth", u, 0)
                    copy(u, S_(u, sD), b4(B + 1))
                    copy(u, S_(u, sDT), b4(B + 2)).then_inc(g_ac, 1)
                for u in range(2):
                    g_wait(act, n, "eighth", u, 0)
                    copy(u, S_(u, sKT), b4(4 * u + 1)).then_inc(g_ac, 1)
                for u in range(2):
                    g_wait(act, n, "solve0", u, 0)
                    copy(u, S_(u, sY0), b4(4 * u + 1)).then_inc(g_ac, 1)
                for u in range(2):
                    g_wait(act, n, "w_turned", u, 0)
                    copy(u, S_(u, sAT)[0:64], b4(4 * u)[0:64]).then_inc(g_ac, 1)
                for u in range(2):
                    g_wait(act, n, "y", u, 0)
                    cols = slice((q + u) * 256, (q + u) * 256 + 256)
                    copy(u, key_t[:, t, cols].rearrange("p (j c) -> p j c", j=4), b4(4 * u + 1)[:, :, 0:64]).then_inc(g_ac, 1)
            act.wait_ge(s_kturn, 1)
            act.activation(kiT, bank(0)[:, 0:SEQ], ACT.Copy)
            act.activation(kT, bank(1).rearrange("p (k s) -> p k s", k=A_KV), ACT.Copy).then_inc(s_kT2, 1)
            for t in range(TILES):
                act.wait_ge(s_qturn, t + 1)
                act.activation(qiT[:, t], acc[:, 2:4].rearrange("p a (j c) -> p (a j) c", c=P), ACT.Copy)
                act.activation(qT[:, t], acc[:, 4:6].rearrange("p a (j c) -> p (a j) c", c=P), ACT.Copy,
                               scale=A_HEAD ** -0.5).then_inc(s_qT2, 1)
                nk = (t + 1) * P
                for i in range(I_HEADS // 2):
                    m = t * (I_HEADS // 2) + i
                    act.wait_ge(s_ix, m + 1)
                    if m >= 4:
                        act.wait_ge(s_acc2, m - 3)
                    act.activation(rel[:, m % 4, :, 0:nk], acc[:, 6 * (m % 2):6 * (m % 2) + 2, 0:nk],
                                   ACT.Relu).then_inc(s_rel, 1)

            act.wait_ge(s_yv, TILES)
            act.activation(yst[:, 1], yst[:, 1], ACT.Sqrt).then_inc(s_yr0, 1)

            def attend(m0, n, exps, blocks, pre=None):
                for m in range(m0, m0 + n + 2):
                    if pre and m < m0 + n:
                        pre(m)
                    if m0 <= m - 1 < m0 + n:
                        act.wait_ge(a_sm, m)
                        if m - 1 >= 4:
                            act.wait_ge(a_done, m - 4)
                        if m - 1 >= 3:
                            act.wait_ge(a_T, m - 3)
                        exps(m - 1)
                    if m0 <= m - 2:
                        act.wait_ge(a_T, m - 1)
                        if m - 2 >= 2:
                            act.wait_ge(a_O, m - 3)
                        blocks(m - 2)

            def exps_of(src, nk):
                def go(m):
                    for j in range(2):
                        last = act.activation(prob[:, m % 3, j * nk(m):(j + 1) * nk(m)], src(m, j), ACT.Exp,
                                              bias=nmax[:, m % 3, j:j + 1], accum_out=psums[:, m % 4, j:j + 1])
                    last.then_inc(a_pr, 1)
                return go

            def blocks_of(nb):
                def go(m):
                    n = 2 * nb(m) * P
                    act.activation(probT[:, m % 2, 0:n], bank(3 + m % 2)[:, 0:n], ACT.Copy).then_inc(a_PT, 1)
                return go

            tile_of = lambda m: (m - M_DSA) // 4
            nk1 = lambda m: (tile_of(m) + 1) * P
            attend(M_DSA, 8, exps_of(lambda m, j: prob[:, m % 3, j * nk1(m):(j + 1) * nk1(m)], nk1),
                   blocks_of(lambda m: tile_of(m) + 1))

            round_turned("mixed", xT[0], None)
            round_and_read(G["mix"])
            for k in range(8):
                act.wait_ge(acc_free[k], G["cross_q"].used0[k] + 1)
            norm_rows("cross", lambda t: h[:, t])
            round_turned("cross", xT[0], 2)

            def read_cq(i, c):
                chunk_done(act, G["cross_q"], 0)
                for f in range(4):
                    act.activation(cqT[:, f], bank(f)[:, 0:SEQ], ACT.Copy, scale=C_HEAD ** -0.5).then_inc(acc_free[f], 1)
            round_and_read(G["cross_q"], read_cq)
            sc = lambda m, j: bank(m % 3)[:, j * SEQ:(j + 1) * SEQ]
            attend(M_CROSS, 4, exps_of(sc, lambda m: SEQ), blocks_of(lambda m: 2))
            round_turned("o", xT[0], None, slabs=C_W // P)
            round_and_read(G["cross_o"])
            for k in range(8):
                act.wait_ge(acc_free[k], G["up0"].used0[k] + 1)
            norm_rows("mlp", lambda t: h[:, t])
            act.dma_start(final_gain, A["norm_final"].partition_broadcast(P)).then_inc(s_fgain, 16)
            round_turned("mlp", xT[0], 3)
            for half in range(2):
                round_and_read(G[f"up{half}"])
                round_and_read(G[f"down{half}"])
            for k in range(8):
                act.wait_ge(acc_free[k], G["sb_q"].used0[k] + 1)
            norm_rows("final", lambda t: h[:, t], P, at(base, TILES, D))

            act.wait_ge(s_fin, TILES)
            act.wait_ge(s_meta, 32)
            norm_rows("meta", lambda t: hmeta[0:META], META, xn2)
            round_turned("meta", xT[0], 4, META, 1, off=0)
            norm_rows("mix2", lambda t: h[:, t], P, xn2)
            round_turned("mix2", xT[0], 4)

            def reader_T(name, dsts, width, scale=1.0):
                g = G[name]

                def read(i, c):
                    chunk_done(act, g, c, i)
                    flat = dsts[c // 2].rearrange("p h c -> p (h c)")
                    for f in range(4):
                        at_, b = i * (8 * width) + (c % 2 * 4 + f) * width, 4 * (c % 2) + f
                        act.activation(flat[:, bass.ds(at_, width)], bank(b)[:, 0:width],
                                       ACT.Copy, scale=scale).then_inc(acc_free[b], 1)
                return read

            def read_values(v, v_meta, n0):
                two = lambda k, rows: acc[0:rows, k:k + 2].rearrange("p a c -> p (a c)")
                for t in range(TILES):
                    act.wait_ge(s_vt, n0 + t + 1)
                    act.activation(v[:, t], two(4 + 2 * t, P), ACT.Copy).then_inc(s_vr, 1)
                act.wait_ge(s_vt, n0 + 3)
                act.activation(v_meta[0:META], two(4, META), ACT.Copy).then_inc(s_vr, 1)

            round_and_read(G["sb_q"], reader_T("sb_q", (sqT,), SEQ, HEAD2 ** -0.5))
            round_and_read(G["sb_kv"], reader_T("sb_kv", (skT, vT), CTX))
            round_and_read(G["fox_q"], reader_T("fox_q", (fqT,), SEQ))
            read_values(sv, sv_meta, 0)
            round_and_read(G["fox_kv"], reader_T("fox_kv", (fkT, vT), CTX))
            round_and_read(G["fox_gate"], reader(G["fox_gate"], lambda t, i, c, src: act.activation(
                fgate[:, t, c * CHUNK:(c + 1) * CHUNK], src, ACT.Exp, scale=-1.0)))
            act.wait_ge(s_c2, 1)
            act.wait_ge(s_lg, 1)
            step(act.activation(logf[0:HEADS2, 0], bank(4)[0:HEADS2, 0:CTX], ACT.Identity, bias=fbias[0:HEADS2]))
            step(act.activation(logf[0:HEADS2, 1], logf[0:HEADS2, 0], ACT.Abs))
            step(act.activation(logf[0:HEADS2, 1], logf[0:HEADS2, 1], ACT.Exp, scale=-1.0))
            act.activation(logf[0:HEADS2, 1], logf[0:HEADS2, 1], ACT.Ln, bias=1.0).then_inc(s_lf1, 1)
            flat_q, flat_k = (x.rearrange("p h c -> p (h c)") for x in (fqT, fkT))
            FOX_ROUNDS = [(flat_q, 0, 2048), (flat_k, 0, 2048), (flat_k, 2048, HEADS2 * CTX - 2048)]
            for r, (x, c0, n) in enumerate(FOX_ROUNDS):
                act.activation(sq_tmp[:, 0:n], x[:, c0:c0 + n], ACT.Square).then_inc(s_fs, 1)
                act.wait_ge(s_fp, r + 1)
                if r:
                    act.wait_ge(s_fn, r)
                act.activation(sq_tmp[:, D:D + n], acc[:, 4:8].rearrange("p a c -> p (a c)")[:, 0:n], ACT.Sqrt,
                               scale=1.0 / HEAD2, bias=eps_col).then_inc(s_fr, 1)
            read_values(fv, fv_meta, 3)

            of = lambda m: ((m - M_TWO) // 16, (m - M_TWO) % 2, (m - M_TWO) % 16 // 2)
            nk2 = lambda m: META + ((m - M_TWO) // 16 + 1) * P

            def stick_log(m):
                t, fox, hd = of(m)
                if fox:
                    return
                act.wait_ge(a_S, m + 1)
                act.wait_ge(a_sm, m - 2)
                x = stick[:, m % 3, 0, 0:nk2(m)]
                step(act.activation(x, bank(m % 3)[:, 0:nk2(m)], ACT.Abs))
                step(act.activation(x, x, ACT.Exp, scale=-1.0))
                act.activation(x, x, ACT.Ln, bias=1.0).then_inc(s_l, 1)

            def two_exps(m):
                t, fox, hd = of(m)
                pr = prob2[:, m % 3, 0:nk2(m)]
                if fox:
                    act.activation(pr, pr, ACT.Exp, bias=nmax[:, m % 3, 0:1], accum_out=psums[:, m % 4, 0:1]).then_inc(a_pr, 1)
                else:
                    act.activation(pr, stick[:, m % 3, 1, 0:nk2(m)], ACT.Exp).then_inc(a_pr, 1)

            def two_blocks(m):
                n = ((m - M_TWO) // 16 + 1) * P
                src = bank(3 + m % 2)
                act.activation(probT2[0:META, m % 2, 0:P], src[0:META, 0:P], ACT.Copy)
                act.activation(probT2[:, m % 2, P:P + n], src[:, P:P + n], ACT.Copy).then_inc(a_PT, 1)

            attend(M_TWO, 32, two_exps, two_blocks, stick_log)
            act.wait_ge(a_done, M_TWO + 32)
            for t in range(TILES):
                for kind in range(2):
                    act.activation(at(base + (2 * t + kind) * W2, W2), merged[:, t, kind * W2:(kind + 1) * W2], ACT.Square,
                                   accum_out=ssum[:, 2 * t + kind:2 * t + kind + 1]).then_inc(s_ss, 1)
            act.wait_ge(s_var, norm_no["heads2"] + 1)
            act.activation(rstd[:, 0:4], var[:, 0:4], ACT.Sqrt).then_inc(s_sd, 1)
            round_turned("merged", xT[0], 5)
            round_and_read(G["out2"])
            for k in range(8):
                act.wait_ge(acc_free[k], G["query"].used0[k] + 1)
            act.dma_start(gain_row, A["norm_ffn_2"][0].partition_broadcast(P)).then_inc(s_erow, 16)
            act.dma_start(subk, A["peer_sub_keys_2"][0].rearrange("h q n c -> n (h q) c")).then_inc(s_erow, 16)
            norm_rows("ffn", lambda t: h[:, t], P, xn3)
            round_turned("ffn", xT[0], 6)
            round_and_read(G["query"], reader_T("query", (pqT,), SEQ))
            for k in range(4):
                act.wait_ge(s_sk, k + 1)
                act.activation(subkT[:, 4 * k:4 * k + 4], bank(4 + k).rearrange("p (j c) -> p j c", j=4), ACT.Copy).then_inc(s_skT, 1)
            for t in range(TILES):
                act.wait_ge(s_sp, t + 1)
                act.activation(scores[:, t], acc[:, 4 * t:4 * t + 4].rearrange("p a c -> p (a c)"), ACT.Copy).then_inc(s_sc, 1)
            for t in range(TILES):
                act.wait_ge(s_bs, t + 1)
                act.activation(coef[:, t], coef[:, t], ACT.Exp).then_inc(s_be, 1)
            act.wait_ge(s_dot, TILES)
            act.activation(dots, dots, ACT.Gelu).then_inc(s_gelu, 1)

        @block.vector
        def _(dve):
            step = Chain(dve, s_vec)
            TT, TS, STT, RED = dve.tensor_tensor, dve.tensor_scalar, dve.scalar_tensor_tensor, dve.tensor_reduce

            def norm_scale(name, eps, rows=P, width=D):
                tiles = norm_tiles[name]
                dve.wait_ge(s_ss, sums0[name] + tiles)
                TS(var[0:rows, 0:tiles], ssum[0:rows, 0:tiles], 1.0 / width, eps, ALU.mult, ALU.add).then_inc(s_var, 1)
                dve.wait_ge(s_sd, norm_no[name] + 1)
                dve.reciprocal(var[0:rows, 0:tiles], rstd[0:rows, 0:tiles]).then_inc(s_rstd, 1)

            def rest_turned(name, dst, gain, rows=P, tiles=TILES, slabs=SLABS, off=META):
                for t in range(tiles):
                    for k in range(slabs // 4):
                        group = g0[name] + t * (slabs // 4) + k
                        dve.wait_ge(s_xh, group + 1)
                        src = bank(4 + group % 4)[:, 0:4 * rows].rearrange("p (s c) -> p s c", s=4)
                        cols = slice(off + t * P, off + t * P + rows)
                        hi, lo = (x[:, 4 * k:4 * k + 4, cols] for x in dst)
                        if gain is None:
                            last = TT(lo, src, hi.bitcast(FP32), ALU.subtract)
                        else:
                            for j in range(4):
                                last = STT(lo[:, j], src[:, j], gains[:, gain, 4 * k + j:4 * k + j + 1],
                                           hi[:, j].bitcast(FP32), ALU.mult, ALU.subtract)
                        last.then_inc(s_xT, 1)

            norm_scale("mem", 1e-5)
            dve.wait_ge(s_gain, 16 * 12)
            rest_turned("mem", memT, 0, off=0)
            norm_scale("x", 1e-5)
            rest_turned("x", xT, 1)
            def whole_turns(x, off):
                step(TS(turns_f, x, 1.0 / (2 * 3.141592653589793), off / (2 * 3.141592653589793), ALU.mult, ALU.add))
                step(dve.tensor_copy(turns_i, turns_f))
                step(dve.tensor_copy(turns_f, turns_i))
                step(STT(rot2, turns_f, -TWO_PI_HI, x, ALU.mult, ALU.add))
                step(STT(rot2, turns_f, -TWO_PI_LO, rot2, ALU.mult, ALU.add))
                step(dve.tensor_scalar_add(rot2, rot2, off))

            rot2, cos_ang = turn_tmp[:, 0], turn_tmp[:, 1]
            for j in range(16):
                dve.memset(invf[:, j:j + 1], float(np.float32(THETA) ** np.float32(-j / 16)))
            step(dve.tensor_copy(posf, posi))
            step(TT(ang, posf.unsqueeze(2).to_broadcast([P, TILES, 16]), invf.unsqueeze(1).to_broadcast([P, TILES, 16]), ALU.mult))
            whole_turns(ang, 3.141592653589793 / 2)
            step(TS(turns_f, rot2, -PI, PI, ALU.max, ALU.min))
            step(dve.tensor_copy(cos_ang, turns_f))
            whole_turns(ang, 0.0)
            TS(ang, rot2, -PI, PI, ALU.max, ALU.min).then_inc(s_ang, 1)
            dve.tensor_copy(turns_f, cos_ang).then_inc(s_ang, 1)
            chunk_done(dve, G["cross_v"], 0)
            step(dve.memset(prev[0:1, 0], 0.0))
            dve.wait_ge(s_shift, 16 * 4)
            for t in range(TILES):
                cur = p[:, t, 0:RWKV_COLS]
                step(TT(prev[:, t], prev[:, t], cur, ALU.subtract))
                step(TT(prev[:, t], prev[:, t], mu, ALU.mult))
                TT(cur, cur, prev[:, t], ALU.add).then_inc(s_mixed, 1)
            for t in range(TILES):
                xg = p[:, t, XG0:XG0 + LORA_G]
                dve.wait_ge(s_eg, t + 1)
                step(dve.tensor_scalar_add(xg, xg, 1.0))
                dve.reciprocal(xg, xg).then_inc(s_sig, 1)
            dve.wait_ge(s_lt, 1)
            step(dve.tensor_copy(loraT[:, 0:2], acc[:, 4:6, 0:SEQ]))
            dve.tensor_copy(loraT[0:LORA_G - P, 2], bank(6)[0:LORA_G - P, 0:SEQ]).then_inc(s_lT, 1)
            step(dve.memset(state[0:R_HEAD], 0.0))
            dve.wait_ge(s_par, 16 * 5)
            heads = lambda x: x.rearrange("p (h n) -> p h n", n=R_HEAD)
            for t in range(TILES):
                r_, k_ = p[:, t, 0:R_W], p[:, t, R_W:2 * R_W]
                a_, kk = beta_t[:, t], key_t[:, t]
                if t:
                    dve.wait_ge(s_el, t)
                dve.wait_ge(s_zd, t + 1)
                TT(tmp, acc[:, 4:6].rearrange("p a b -> p (a b)"), w0, ALU.add).then_inc(s_zv, 1)
                dve.wait_ge(s_ad, t + 1)
                TT(a_, acc[:, 6:8].rearrange("p a b -> p (a b)"), params[:, 0], ALU.add).then_inc(s_av, 1)
                dve.wait_ge(s_ze, t + 1)
                step(dve.tensor_scalar_add(tmp, tmp, 1.0))
                step(dve.reciprocal(logd, tmp))
                dve.tensor_scalar_mul(logd, logd, -E_HALF).then_inc(s_ld, 1)
                step(TT(kk, k_, params[:, 1], ALU.mult))
                step(TT(tmp, kk, kk, ALU.mult))
                RED(kss, heads(tmp), AX, ALU.add).then_inc(s_kss, 1)
                dve.wait_ge(s_ae, t + 1)
                step(dve.tensor_scalar_add(a_, a_, 1.0))
                step(dve.reciprocal(a_, a_))
                step(STT(tmp, a_, -1.0, params[:, 2], ALU.add, ALU.mult))
                step(STT(k_, tmp, 1.0, k_, ALU.add, ALU.mult))
                step(TT(tmp, r_, k_, ALU.mult))
                step(TT(tmp, tmp, params[:, 3], ALU.mult))
                step(RED(bonus[:, t], heads(tmp), AX, ALU.add))
                dve.wait_ge(s_ksd, t + 1)
                step(dve.tensor_scalar_max(kss, kss, 1e-12))
                step(dve.reciprocal(kss, kss))
                step(TT(heads(kk), heads(kk), kss.unsqueeze(2).to_broadcast([P, R_HEADS, R_HEAD]), ALU.mult))
                step(TT(a_, a_, kk, ALU.mult))
                dve.wait_ge(s_cd, t + 1)
                TT(tmp, acc[:, 2:4].rearrange("p a b -> p (a b)"), logd, ALU.subtract).then_inc(s_cp, 1)
                dve.wait_ge(s_en, t + 1)
                STT(kk, kk, -1.0, tmp, ALU.mult, ALU.mult).then_inc(s_kd, 1)
                TT(a_, a_, logd, ALU.mult)
                TT(k_, k_, logd, ALU.mult)
                dve.wait_ge(s_ep, t + 1)
                TT(r_, r_, tmp, ALU.mult).then_inc(s_el, 1)

            b4 = lambda k: bank(k).rearrange("p (j c) -> p j c", j=4)
            m4 = lambda m: m.unsqueeze(1).to_broadcast([P, 4, P])
            for n, (t, q) in enumerate(PAIRS):
                for u in range(2):
                    B = 4 * u
                    g_wait(dve, n, "turned", u, 0)
                    dve.tensor_copy(S_(u, sAT)[0:64], b4(B)[0:64])
                    dve.tensor_copy(S_(u, sBT)[0:64], b4(B + 1)[0:64]).then_inc(g_ve, 1)
                for u in range(2):
                    B = 4 * u
                    g_wait(dve, n, "pairs", u, 0)
                    TT(S_(u, sD), b4(B), m4(lower16), ALU.mult)
                    TT(S_(u, sL), b4(B), m4(lower_rest), ALU.mult)
                    step(TT(S_(u, sDT), b4(B + 1), m4(upper16), ALU.mult))
                    TT(S_(u, sX), S_(u, sDT), m4(ident), ALU.add)
                    TT(S_(u, sAK), b4(B + 2), m4(upper), ALU.mult)
                    TT(S_(u, sRB), b4(B + 3), m4(tri), ALU.mult).then_inc(g_ve, 1)
                for u in range(2):
                    g_wait(dve, n, "square", u, 0)
                    TT(S_(u, sRK), b4(4 * u), m4(tri), ALU.mult).then_inc(g_ve, 1)
                for name in ("fourth", "eighth", "inverse"):
                    for u in range(2):
                        g_wait(dve, n, name, u, 0)
                        TT(S_(u, sX), b4(4 * u), S_(u, sX), ALU.add).then_inc(g_ve, 1)
                for u in range(2):
                    g_wait(dve, n, "solve0", u, 0)
                    dve.tensor_copy(S_(u, sDT), b4(4 * u + 2)).then_inc(g_ve, 1)
                for name in ("solve1", "solve2", "solve3"):
                    for u in range(2):
                        g_wait(dve, n, name, u, 0)
                        g_wait(dve, n, "solve0", u, 2)
                        TT(S_(u, sR), b4(4 * u + 3), S_(u, sY0), ALU.add).then_inc(g_ve, 1)
                for c in range(2):
                    rows = slice(64 * c, 64 * c + 64)
                    for u in range(2):
                        g_wait(dve, n, f"sa{c}", u, 0)
                        TT(S_(u, sKT)[rows, :, 0:64], b4(4 * u + 2)[rows, :, 0:64], S_(u, sR)[rows, :, 64:128],
                           ALU.add).then_inc(g_ve, 1)
                    for u in range(2):
                        g_wait(dve, n, f"state{c}", u, 0)
                        st = state[0:64, (q + u) * 256:(q + u + 1) * 256].rearrange("p (j v) -> p j v", j=4)
                        step(TT(st, st, b4(4 * u + 3)[0:64, :, 0:64], ALU.add))
                        dec = decayC[0:64, t, 4 * (q + u):4 * (q + u) + 4, c:c + 1].to_broadcast([64, 4, 64])
                        TT(st, st, dec, ALU.mult).then_inc(g_ve, 1)
            for t in range(TILES):
                nk = (t + 1) * P
                sc = score[:, t, 0:nk]
                step(dve.tensor_copy(sc, causal[:, t, META:META + nk]))
                for i in range(I_HEADS // 2):
                    m = t * (I_HEADS // 2) + i
                    dve.wait_ge(s_rel, m + 1)
                    for j in range(2):
                        last = STT(sc, rel[:, m % 4, j, 0:nk], p[:, t, WI0 + 2 * i + j:WI0 + 2 * i + j + 1], sc,
                                   ALU.mult, ALU.add)
                        if j == 0:
                            step(last)
                    last.then_inc(s_acc2, 1)
                    dve.wait_ge(s_acc2, m + 1)
                src = sc
                for r in range(TOPK // 8):
                    step(dve.max(m8, src))
                    step(dve.match_replace(left[:, 0:nk], m8, src, TAKEN))
                    src = left[:, 0:nk]
                un = unsel[:, t, 0:nk]
                step(TS(un, left[:, 0:nk], TAKEN / 2, NEG, ALU.is_gt, ALU.mult))
                step(TT(un, un, causal[:, t, META:META + nk], ALU.add))

            dve.wait_ge(s_yr0, 1)
            dve.reciprocal(yst[:, 1], yst[:, 1]).then_inc(s_ysd, 1)

            def attend(m0, n, prepare, finish):
                for m in range(m0, m0 + n + 3):
                    if m < m0 + n:
                        dve.wait_ge(a_S, m + 1)
                        if m >= 3:
                            dve.wait_ge(a_T, m - 2)
                            dve.wait_ge(a_pr, m - 2)
                        prepare(m)
                    if m0 <= m - 3:
                        dve.wait_ge(a_O, m - 2)
                        finish(m - 3)

            def finish_of(dst):
                def go(m):
                    step(dve.reciprocal(pinv[:, m % 4], psums[:, m % 4]))
                    TT(dst(m), bank(5 + m % 2)[:, 0:2 * P].rearrange("p (j d) -> p j d", j=2),
                       pinv[:, m % 4].unsqueeze(2).to_broadcast([P, 2, P]), ALU.mult).then_inc(a_done, 1)
                return go

            def dsa_prepare(m):
                t = (m - M_DSA) // 4
                nk = (t + 1) * P
                pr = prob[:, m % 3, 0:2 * nk].rearrange("p (j s) -> p j s", j=2)
                step(TT(pr, bank(m % 3)[:, 0:2 * nk].rearrange("p (j s) -> p j s", j=2),
                        unsel[:, t, 0:nk].unsqueeze(1).to_broadcast([P, 2, nk]), ALU.add))
                RED(nmax[:, m % 3], pr, AX, ALU.max, negate=True).then_inc(a_sm, 1)

            def dsa_out(m):
                t, i = (m - M_DSA) // 4, (m - M_DSA) % 4
                return p[:, t, Q0 + 2 * i * P:Q0 + 2 * (i + 1) * P].rearrange("p (j d) -> p j d", j=2)
            attend(M_DSA, 8, dsa_prepare, finish_of(dsa_out))


            def add_to_h(g):
                def body(i):
                    for c in range(g.per_body):
                        chunk_done(dve, g, c, i)
                        for t in range(TILES):
                            k = 2 * (c % 2) + t
                            cols = h[:, t, bass.ds(i * (g.per_body * CHUNK) + c * CHUNK, CHUNK)]
                            TT(cols, bank(k), cols, ALU.add).then_inc(acc_free[k], 1)
                loop(dve, g.bodies, body)

            rest_turned("mixed", xT, None)
            add_to_h(G["mix"])
            norm_scale("cross", 1e-5)
            rest_turned("cross", xT, 2)

            def cross_prepare(m):
                RED(nmax[:, m % 3], bank(m % 3).rearrange("p (j s) -> p j s", j=2), AX, ALU.max, negate=True
                    ).then_inc(a_sm, 1)

            def cross_out(m):
                t, i = (m - M_CROSS) // 2, (m - M_CROSS) % 2
                return co[:, t, 2 * i * P:2 * (i + 1) * P].rearrange("p (j d) -> p j d", j=2)
            attend(M_CROSS, 4, cross_prepare, finish_of(cross_out))
            rest_turned("o", xT, None, slabs=C_W // P)
            add_to_h(G["cross_o"])
            norm_scale("mlp", 1e-5)
            rest_turned("mlp", xT, 3)
            hid_hi, hid_lo = (x.rearrange("p s c -> p (s c)") for x in hidT)
            for half in range(2):
                g = G[f"up{half}"]

                def body(i):
                    for c in range(g.per_body):
                        chunk_done(dve, g, c, i)
                        for f in range(4):
                            b = 4 * (c % 2) + f
                            dve.tensor_scalar_max(relu_now[:, f * SEQ:(f + 1) * SEQ], bank(b)[:, 0:SEQ], 0.0
                                                  ).then_inc(acc_free[b], 1)
                        dve.drain()
                        TT(square_now, relu_now, relu_now, ALU.mult)
                        dve.drain()
                        cols = bass.ds(i * (8 * SEQ) + c * (4 * SEQ), 4 * SEQ)
                        dve.tensor_copy(hid_hi[:, cols], square_now)
                        dve.drain()
                        TT(hid_lo[:, cols], square_now, hid_hi[:, cols].bitcast(FP32), ALU.subtract).then_inc(s_hid, 1)
                        dve.drain()
                loop(dve, g.bodies, body)
                add_to_h(G[f"down{half}"])
            norm_scale("final", 1e-5)
            dve.wait_ge(s_fgain, 16)
            dve.wait_ge(s_rstd, norm_no["final"] + 1)
            for t in range(TILES):
                STT(h[:, t], h[:, t], var[:, t:t + 1], final_gain, ALU.mult, ALU.mult).then_inc(s_fin, 1)

            norm_scale("meta", 1e-6, META)
            rest_turned("meta", xT, 4, META, 1, off=0)
            norm_scale("mix2", 1e-6)
            rest_turned("mix2", xT, 4)
            dve.wait_ge(s_c2, 1)
            step(TS(seen, strict, NEG / 2, None, ALU.is_gt))
            step(dve.tensor_scalar_mul(head_gains[:, 0:1], head_gains[:, 0:1], HEAD2 ** -0.5))
            dve.wait_ge(s_lf1, 1)
            lf = logf[0:HEADS2]
            step(STT(lf[:, 2], lf[:, 0], 0.0, lf[:, 1], ALU.min, ALU.subtract))
            step(dve.tensor_tensor_scan(lf[:, 0], lf[:, 2], lf[:, 2], 0.0, ALU.add, ALU.bypass))
            dve.tensor_scalar_mul(lf[:, 1], lf[:, 0], -1.0).then_inc(s_lf2, 1)
            dve.wait_ge(s_ct, 1)
            dve.tensor_copy(cumf, bank(4)[:, 0:TILES * HEADS2].rearrange("p (t h) -> p t h", t=TILES)).then_inc(s_cc, 1)
            flat_q, flat_k = (x.rearrange("p h c -> p (h c)") for x in (fqT, fkT))
            for r, (x, c0, n) in enumerate([(flat_q, 0, 2048), (flat_k, 0, 2048), (flat_k, 2048, HEADS2 * CTX - 2048)]):
                dve.wait_ge(s_fr, r + 1)
                root = sq_tmp[:, D:D + n]
                step(dve.reciprocal(root, root))
                gcol = head_gains[:, min(r, 1):min(r, 1) + 1]
                STT(x[:, c0:c0 + n], x[:, c0:c0 + n], gcol, root, ALU.mult, ALU.mult).then_inc(s_fn, 1)
            fg = fgate.rearrange("p t c -> p (t c)")
            step(dve.tensor_scalar_add(fg, fg, 1.0))
            step(dve.reciprocal(fg, fg))

            of = lambda m: ((m - M_TWO) // 16, (m - M_TWO) % 2, (m - M_TWO) % 16 // 2)
            nk2 = lambda m: META + ((m - M_TWO) // 16 + 1) * P

            def two_prepare(m):
                t, fox, hd = of(m)
                z = bank(m % 3)[:, 0:nk2(m)]
                if fox:
                    pr = prob2[:, m % 3, 0:nk2(m)]
                    step(STT(pr, z, cumf[:, t, hd:hd + 1], causal[:, t, 0:nk2(m)], ALU.add, ALU.add))
                    RED(nmax[:, m % 3, 0:1], pr, AX, ALU.max, negate=True).then_inc(a_sm, 1)
                    return
                a, b, c = (stick[:, m % 3, k, 0:nk2(m)] for k in range(3))
                dve.wait_ge(s_l, (m - M_TWO) // 2 + 1)
                step(STT(b, z, 0.0, a, ALU.max, ALU.add))
                step(dve.tensor_tensor_scan(c[:, ::-1], b[:, ::-1], seen[:, t, 0:nk2(m)][:, ::-1], 0.0, ALU.add, ALU.mult))
                step(TT(b, z, c, ALU.subtract))
                TT(b, b, strict[:, t, 0:nk2(m)], ALU.add).then_inc(a_sm, 1)

            def two_finish(m):
                t, fox, hd = of(m)
                dst = merged[:, t, fox * W2 + hd * P:fox * W2 + (hd + 1) * P]
                src = bank(5 + m % 2)[:, 0:P]
                if fox:
                    step(dve.reciprocal(pinv[:, m % 4, 0:1], psums[:, m % 4, 0:1]))
                    TS(dst, src, pinv[:, m % 4, 0:1], None, ALU.mult).then_inc(a_done, 1)
                else:
                    dve.tensor_copy(dst, src).then_inc(a_done, 1)

            attend(M_TWO, 32, two_prepare, two_finish)
            norm_scale("heads2", 1e-6, P, W2)
            dve.wait_ge(s_rstd, norm_no["heads2"] + 1)
            for t in range(TILES):
                TS(merged[:, t, 0:W2], merged[:, t, 0:W2], var[:, 2 * t:2 * t + 1], None, ALU.mult).then_inc(s_mg, 1)
                STT(merged[:, t, W2:D], merged[:, t, W2:D], var[:, 2 * t + 1:2 * t + 2], fgate[:, t], ALU.mult, ALU.mult
                    ).then_inc(s_mg, 1)
            rest_turned("merged", xT, 5)
            add_to_h(G["out2"])
            norm_scale("ffn", 1e-6)
            rest_turned("ffn", xT, 6)
            dve.wait_ge(s_erow, 32)
            dve.wait_ge(s_xn, xn0["ffn"] + TILES)
            for t in range(TILES):
                TT(hb[:, t], xn3[:, t], gain_row, ALU.mult).then_inc(s_hb, 1)
            b1 = best1.bitcast(FP32)
            i1 = bestf.bitcast(U32)
            jn = picked[:, 0].bitcast(U32)
            hi, lo = picked[:, 1].bitcast(U32), picked[:, 2].bitcast(U32)
            step(dve.memset(iota16[:, 0:1], 0.0))
            for k in range(1, E_TOP):
                step(dve.memset(iota16[:, k:k + 1], float(k)))

            def best16(val, idx, src):
                step(dve.max(val[:, 0:8], src))
                step(dve.max_index(idx[:, 0:8], val[:, 0:8], src))
                w = work1[:, 0:src.shape[-1]]
                step(dve.match_replace(w, val[:, 0:8], src, TAKEN))
                step(dve.max(val[:, 8:16], w))
                step(dve.max_index(idx[:, 8:16], val[:, 8:16], w))

            cw = lambda t: coef[:, t].rearrange("p (h k) -> p h k", h=E_HEADS)
            cand = hot.rearrange("p (h a) b -> p h a b", h=E_HEADS)
            pair = best1.rearrange("p (h q) a -> p h q a", q=2)
            shape = [P, E_HEADS, E_TOP, E_TOP]
            flat = hot.rearrange("p a b -> p (a b)")

            def key_lists(t, k0):
                for k in range(k0, k0 + 4):
                    best16(best1[:, k], i1[:, k], scores[:, t, k * N_KEYS:(k + 1) * N_KEYS])

            def pairs(t, e0, e1):
                if e0 == 0:
                    step(TT(cand, pair[:, :, 0].unsqueeze(3).to_broadcast(shape), pair[:, :, 1].unsqueeze(2).to_broadcast(shape), ALU.add))
                for e in range(e0, e1):
                    best16(best2[:, t, e], jn[:, e * E_TOP:(e + 1) * E_TOP], flat[:, e * 256:(e + 1) * 256])

            def numbers(t):
                TT(cw(t), best2[:, t], best2[:, t, :, 0:1].to_broadcast([P, E_HEADS, E_TOP]), ALU.subtract).then_inc(s_bs, 1)
                step(TS(hi, jn, 4, None, ALU.logical_shift_right))
                step(TS(lo, jn, 15, None, ALU.bitwise_and))
                step(dve.tensor_copy(picked[:, 1], hi))
                step(dve.tensor_copy(picked[:, 2], lo))
                step(dve.tensor_copy(bestf, i1))
                lists = bestf.rearrange("p (h q) a -> p h q a", q=2)
                for q_ in range(2):
                    at_ = picked[:, 1 + q_].rearrange("p (h k) -> p h k", h=E_HEADS).unsqueeze(3).to_broadcast(shape)
                    step(TT(cand, at_, iota16.unsqueeze(1).unsqueeze(1).to_broadcast(shape), ALU.is_equal))
                    step(TT(cand, cand, lists[:, :, q_].unsqueeze(2).to_broadcast(shape), ALU.mult))
                    step(RED(picked[:, 1 + q_], hot, AX, ALU.add))
                step(STT(experts[:, t, 0:P], picked[:, 1], float(N_KEYS), picked[:, 2], ALU.mult, ALU.add))
                dve.tensor_copy(experts[:, t, P:P + 4], experts[:, t, 0:4]).then_inc(s_ix0, 1)

            def choose(t, part):
                if part < 4:
                    key_lists(t, 4 * part)
                elif part < 7:
                    pairs(t, 3 * (part - 4), min(3 * (part - 3), E_HEADS))
                else:
                    numbers(t)

            per = P // 16

            def dot_products(t, i):
                for n in range(4):
                    dve.wait_ge(rows_full[n], i * 64 + (t * per + 1) * 64)
                    for j in range(4):
                        last = dve.tensor_tensor_reduce(out=junk, in0=rows_buf[4 * n + j], in1=hb[:, t], scale=1.0, scalar=0.0,
                                                        op0=ALU.mult, op1=ALU.add, accum_out=dots_now[:, 4 * n + j:4 * n + j + 1])
                        if j == 3:
                            last.then_inc(rows_used[n], 1)
                        dve.drain()
                dve.tensor_copy(dots[:, t, bass.ds(i * 16, 16)], dots_now)
                dve.drain()

            dve.wait_ge(s_sc, TILES)
            for part in range(8):
                choose(0, part)
            assert per == 8
            for i in range(per):
                choose(1, i)
                dot_products(0, i)
            dve.nop().then_inc(s_dot, 1)
            for t in range(TILES):
                dve.wait_ge(s_be, t + 1)
                step(RED(esum[:, t], cw(t), AX, ALU.add))
                step(dve.reciprocal(esum[:, t], esum[:, t]))
                step(TT(cw(t), cw(t), esum[:, t].unsqueeze(2).to_broadcast([P, E_HEADS, E_TOP]), ALU.mult))
            with dve.Fori(0, per) as i:
                dot_products(1, i)
            dve.nop().then_inc(s_dot, 1)
            dve.wait_ge(s_gelu, 1)
            step(TT(coef, coef, dots, ALU.mult))
            for t in range(TILES):
                with dve.Fori(0, per) as i:
                    dve.tensor_copy(coef_now, coef[:, t, bass.ds(i * 16, 16)])
                    dve.drain()
                    for n in range(4):
                        dve.wait_ge(rows_full[n], i * 64 + ((TILES + t) * per + 1) * 64)
                        for j in range(4):
                            last = STT(h[:, t], rows_buf[4 * n + j], coef_now[:, 4 * n + j:4 * n + j + 1], h[:, t],
                                       ALU.mult, ALU.add)
                            if j == 3:
                                last.then_inc(rows_used[n], 1)
                            dve.drain()

        @block.tensor
        def _(pe):
            for k in range(8):
                pe.sem_inc(acc_free[k], 1)
            pe.sem_inc(slab_used, PARTS)

            def product(g, x, upper=None):
                def body(i):
                    for c in range(g.per_body):
                        width = g.widths[c]
                        banks = range(2 * (c % 2), 2 * (c % 2) + 2) if g.tok else range(4 * (c % 2), 4 * (c % 2) + 4)
                        if c == 1 and upper:
                            pe.wait_ge(*upper)
                        for b in banks:
                            n = sum(1 for d in range(c) if d % 2 == c % 2)
                            pe.wait_ge(acc_free[b], i * g.uses(b) + g.used0[b] + n + 1)
                        for s in range(g.slabs):
                            pe.wait_ge(lo_ready, g.slab(i, c, s) + 1)
                            k = s % PARTS
                            for n, (wp, xp) in enumerate(((w_hi, x[0]), (w_hi, x[1]), (w_lo, x[0]))):
                                kw = dict(start=s == 0 and n == 0, stop=s == g.slabs - 1 and n == 2)
                                if g.tok:
                                    for t in range(TILES):
                                        last = pe.matmul(bank(banks[t])[:, 0:width],
                                                         xp[:, s, g.lo + t * P:g.lo + (t + 1) * P],
                                                         wp[:, k, 0:width], **kw)
                                else:
                                    for f in range(4):
                                        last = pe.matmul(bank(banks[f])[:, 0:g.hi - g.lo], wp[:, k, f * P:(f + 1) * P],
                                                         xp[:, s, g.lo:g.hi], **kw)
                            last.then_inc(slab_used, 1)
                loop(pe, g.bodies, body)

            def turn(name, is_norm, block_of, rows=P, tiles=TILES, slabs=SLABS):
                group = g0[name]
                for t in range(tiles):
                    if is_norm:
                        pe.wait_ge(s_xn, xn0[name] + t + 1)
                    for k in range(slabs // 4):
                        if group >= 4:
                            pe.wait_ge(s_xT, group - 3)
                        for j in range(4):
                            last = pe.transpose(bank(4 + group % 4)[:, j * rows:(j + 1) * rows],
                                                block_of(t, 4 * k + j), ident[0:rows, 0:rows])
                        last.then_inc(s_tr, 1)
                        group += 1
                return group

            xn_block = lambda t, s: xn[:, t, s * P:(s + 1) * P]
            pe.wait_ge(s_const, 1)
            turn("mem", True, xn_block)
            turn("x", True, xn_block)
            pe.wait_ge(s_xT, 8)
            product(G["cross_k"], memT)
            product(G["cross_v"], memT)
            pe.wait_ge(s_xT, 16)
            product(G["in"], xT)
            product(G["in_end"], xT)

            for k in range(4):
                pe.wait_ge(acc_free[k], G["mix"].used0[k] + 1)
            for t in range(TILES):
                pe.wait_ge(s_tanh, t + 1)
                pe.transpose(bank(4)[:, t * P:(t + 1) * P], p[:, t, XW0:XW0 + P], ident)
                pe.wait_ge(s_sig, t + 1)
                pe.transpose(bank(5)[:, t * P:(t + 1) * P], p[:, t, XG0:XG0 + P], ident)
                last = pe.transpose(bank(6)[0:LORA_G - P, t * P:(t + 1) * P], p[:, t, XG0 + P:XG0 + LORA_G], ident)
            last.then_inc(s_lt, 1)
            pe.wait_ge(s_lT, 1)
            pe.wait_ge(s_lora, 64)
            for t in range(TILES):
                tok = slice(t * P, (t + 1) * P)
                if t:
                    pe.wait_ge(s_ep, t)
                for c in range(2):
                    cols = slice(c * CHUNK, (c + 1) * CHUNK)
                    last = pe.matmul(bank(4 + c), loraT[0:LORA_W, 0, tok], lora_up[0:LORA_W, 0, cols], start=True, stop=True)
                last.then_inc(s_zd, 1)
                for c in range(2):
                    cols = slice(c * CHUNK, (c + 1) * CHUNK)
                    last = pe.matmul(bank(6 + c), loraT[LORA_W:P, 0, tok], lora_up[LORA_W:P, 0, cols], start=True, stop=True)
                last.then_inc(s_ad, 1)
                if t:
                    pe.wait_ge(s_gate, t)
                for c in range(2):
                    cols = slice(c * CHUNK, (c + 1) * CHUNK)
                    pe.matmul(bank(c), loraT[:, 1, tok], lora_up[:, 1, cols], start=True, stop=False)
                    last = pe.matmul(bank(c), loraT[0:LORA_G - P, 2, tok], lora_up[0:LORA_G - P, 2, cols], start=False, stop=True)
                last.then_inc(s_gd, 1)
                pe.wait_ge(s_ld, t + 1)
                for c in range(2):
                    pe.matmul(bank(2 + c), tri, logd[:, c * CHUNK:(c + 1) * CHUNK], start=True, stop=True)
                for hd in range(R_HEADS):
                    last = pe.matmul(bank(6)[0:R_HEAD, 2 * hd:2 * hd + 2], logd[:, hd * R_HEAD:(hd + 1) * R_HEAD], halves,
                                     start=hd == 0, stop=True, skip_group_check=True)
                last.then_inc(s_cd, 1)
            pe.wait_ge(s_el, TILES)
            for n, (t, q) in enumerate(PAIRS):
                b4 = lambda k: bank(k).rearrange("p (j c) -> p j c", j=4)
                V = lambda u, j: p[:, t, 2 * R_W + (q + u) * 256 + j * 64:2 * R_W + (q + u) * 256 + (j + 1) * 64]
                K = lambda u, j: p[:, t, R_W + (q + u) * 256 + j * 64:R_W + (q + u) * 256 + (j + 1) * 64]
                R = lambda u, j: p[:, t, (q + u) * 256 + j * 64:(q + u) * 256 + (j + 1) * 64]
                AK_ = lambda u, j: key_t[:, t, (q + u) * 256 + j * 64:(q + u) * 256 + (j + 1) * 64]
                BT_ = lambda u, j: beta_t[:, t, (q + u) * 256 + j * 64:(q + u) * 256 + (j + 1) * 64]
                S0 = lambda u, j: state[0:64, (q + u) * 256 + j * 64:(q + u) * 256 + (j + 1) * 64]

                def mm(b, j, lhsT, rhs, start=True, stop=True, rows=slice(0, P), width=P, check=False):
                    return pe.matmul(b4(b)[rows, j, 0:width], lhsT, rhs, start=start, stop=stop, skip_group_check=check)

                def after(prev_stage, u):
                    g_wait(pe, n, prev_stage, u, 1)
                    g_wait(pe, n, prev_stage, u, 2)

                for u in range(2):
                    if n:
                        g_wait(pe, n - 1, "state1", u, 1)
                        g_wait(pe, n - 1, "y", u, 2)
                    for b, src in enumerate((AK_, BT_, K, R)):
                        for j in range(4):
                            last = pe.transpose(b4(4 * u + b)[0:64, j], src(u, j), ident)
                    last.then_inc(g_pe, 1)
                for u in range(2):
                    after("turned", u)
                    at_, bt, kt, rt = (S_(u, x) for x in (sAT, sBT, sKT, sRT))
                    for j in range(4):
                        mm(4 * u, j, at_[0:64, j], bt[0:64, j])
                        mm(4 * u + 1, j, bt[0:64, j], at_[0:64, j])
                        mm(4 * u + 2, j, kt[0:64, j], at_[0:64, j])
                        last = mm(4 * u + 3, j, bt[0:64, j], rt[0:64, j])
                    last.then_inc(g_pe, 1)
                for u in range(2):
                    after("pairs", u)
                    for j in range(4):
                        mm(4 * u, j, S_(u, sKT)[0:64, j], S_(u, sRT)[0:64, j])
                        mm(4 * u + 1, j, S_(u, sDT)[:, j], S_(u, sD)[:, j])
                        mm(4 * u + 2, j, S_(u, sD)[:, j], S_(u, sDT)[:, j])
                        last = mm(4 * u + 3, j, S_(u, sAK)[:, j], V(u, j), width=64)
                    last.then_inc(g_pe, 1)
                for u in range(2):
                    after("square", u)
                    for j in range(4):
                        mm(4 * u, j, S_(u, sKT)[:, j], S_(u, sX)[:, j])
                        mm(4 * u + 1, j, S_(u, sBT)[:, j], S_(u, sKT)[:, j])
                        last = mm(4 * u + 2, j, S_(u, sKT)[:, j], S_(u, sBT)[:, j])
                    last.then_inc(g_pe, 1)
                for u in range(2):
                    after("fourth", u)
                    for j in range(4):
                        mm(4 * u, j, S_(u, sD)[:, j], S_(u, sX)[:, j])
                        last = mm(4 * u + 1, j, S_(u, sDT)[:, j], S_(u, sD)[:, j])
                    last.then_inc(g_pe, 1)
                for u in range(2):
                    after("eighth", u)
                    for j in range(4):
                        last = mm(4 * u, j, S_(u, sKT)[:, j], S_(u, sX)[:, j])
                    last.then_inc(g_pe, 1)
                for u in range(2):
                    after("inverse", u)
                    for j in range(4):
                        mm(4 * u + 1, j, S_(u, sX)[:, j], S_(u, sR)[:, j])
                        last = mm(4 * u + 2, j, S_(u, sL)[:, j], S_(u, sX)[:, j])
                    last.then_inc(g_pe, 1)
                for a, b in (("solve0", "solve1"), ("solve1", "solve2"), ("solve2", "solve3")):
                    for u in range(2):
                        after(a, u)
                        y = S_(u, sY0) if a == "solve0" else S_(u, sR)
                        for j in range(4):
                            last = mm(4 * u + 3, j, S_(u, sDT)[:, j], y[:, j])
                        last.then_inc(g_pe, 1)
                for u in range(2):
                    after("solve3", u)
                    for j in range(4):
                        last = pe.transpose(b4(4 * u)[0:64, j], S_(u, sR)[:, j, 0:64], ident)
                    last.then_inc(g_pe, 1)
                for c in range(2):
                    rows = slice(64 * c, 64 * c + 64)
                    for u in range(2):
                        if c == 0:
                            after("w_turned", u)
                            for j in range(4):
                                mm(4 * u + 1, j, S_(u, sRK)[:, j], V(u, j), start=j == 0, stop=False, width=64, check=True)
                        else:
                            after("state0", u)
                        for j in range(4):
                            last = mm(4 * u + 2, j, S_(u, sAT)[0:64, j, rows], S0(u, j), rows=rows, width=64)
                        last.then_inc(g_pe, 1)
                    for u in range(2):
                        for j in range(4):
                            mm(4 * u + 1, j, S_(u, sRT)[0:64, j, rows], S0(u, j), start=False, stop=False, rows=rows,
                               width=64, check=True)
                        after(f"sa{c}", u)
                        for j in range(4):
                            mm(4 * u + 3, j, BT_(u, j)[rows], S_(u, sKT)[rows, j, 0:64], start=True, stop=False,
                               rows=slice(0, 64), width=64)
                            last = mm(4 * u + 3, j, K(u, j)[rows], V(u, j)[rows], start=False, stop=True,
                                      rows=slice(0, 64), width=64)
                        last.then_inc(g_pe, 1)
                for u in range(2):
                    for j in range(4):
                        last = mm(4 * u + 1, j, S_(u, sRB)[:, j], S_(u, sKT)[:, j, 0:64], start=False, stop=j == 3,
                                  width=64, check=True)
                    last.then_inc(g_pe, 1)

            for u in range(2):
                g_wait(pe, len(PAIRS) - 1, "state1", u, 1)
                g_wait(pe, len(PAIRS) - 1, "y", u, 2)
            pe.wait_ge(s_rope, TILES)
            for t in range(TILES):
                pe.transpose(bank(0)[:, t * P:(t + 1) * P], keyI[:, t], ident)
                for k in range(A_KV):
                    last = pe.transpose(bank(1)[:, k * SEQ + t * P:k * SEQ + (t + 1) * P],
                                        p[:, t, K0 + k * P:K0 + (k + 1) * P], ident)
            last.then_inc(s_kturn, 1)
            for t in range(TILES):
                if t:
                    pe.wait_ge(s_qT2, t)
                for k, col in ((2, QI0), (4, Q0)):
                    for i in range(8):
                        last = pe.transpose(bank(k + i // 4)[:, (i % 4) * P:(i % 4 + 1) * P],
                                            p[:, t, col + i * P:col + (i + 1) * P], ident)
                last.then_inc(s_qturn, 1)
                pe.wait_ge(s_kT2, 1)
                pe.wait_ge(s_qT2, t + 1)
                nk = (t + 1) * P
                for i in range(I_HEADS // 2):
                    m = t * (I_HEADS // 2) + i
                    if m >= 2:
                        pe.wait_ge(s_rel, m - 1)
                    for j in range(2):
                        half = slice(j * I_HEAD, (j + 1) * I_HEAD)
                        last = pe.matmul(bank(6 * (m % 2) + j)[:, 0:nk], qiT[half, t, i], kiT[half, 0:nk],
                                         start=True, stop=True)
                    last.then_inc(s_ix, 1)

            def attend(m0, n, heads_n, scores_of, blocks, values, pr_of, pT_of):
                for m in range(m0, m0 + n + 3):
                    if m < m0 + n:
                        if m >= 3:
                            pe.wait_ge(a_pr, m - 2)
                        scores_of(m).then_inc(a_S, 1)
                    if m0 <= m - 2 < m0 + n:
                        k = m - 2
                        pe.wait_ge(a_pr, k + 1)
                        if k >= 2:
                            pe.wait_ge(a_PT, k - 1)
                        slot = 0
                        for j in range(heads_n):
                            for off, size in blocks(k):
                                last = pe.transpose(bank(3 + k % 2)[0:size, slot * P:(slot + 1) * P],
                                                    pr_of(k, j)[:, off:off + size], ident)
                                slot += 1
                        last.then_inc(a_T, 1)
                    if m0 <= m - 3:
                        k = m - 3
                        pe.wait_ge(a_PT, k + 1)
                        if k >= 2:
                            pe.wait_ge(a_done, k - 1)
                        nb = len(blocks(k))
                        for j in range(heads_n):
                            for n_, (off, size) in enumerate(blocks(k)):
                                slot = j * nb + n_
                                last = pe.matmul(bank(5 + k % 2)[:, j * P:(j + 1) * P],
                                                 pT_of(k)[0:size, slot * P:(slot + 1) * P], values(k, j, n_),
                                                 start=n_ == 0, stop=n_ == nb - 1)
                        last.then_inc(a_O, 1)

            def dsa_scores(m):
                t, i = (m - M_DSA) // 4, (m - M_DSA) % 4
                nk = (t + 1) * P
                for j in range(2):
                    hd = 2 * i + j
                    last = pe.matmul(bank(m % 3)[:, j * nk:(j + 1) * nk], qT[:, t, hd], kT[:, hd // (A_HEADS // A_KV), 0:nk],
                                     start=True, stop=True)
                return last

            def dsa_values(m, j, n_):
                kv = (2 * ((m - M_DSA) % 4) + j) // (A_HEADS // A_KV)
                return p[:, n_, V0 + kv * P:V0 + (kv + 1) * P]

            nk1 = lambda m: ((m - M_DSA) // 4 + 1) * P
            pe.wait_ge(s_rel, I_HEADS)
            attend(M_DSA, 8, 2, dsa_scores, lambda m: [(b * P, P) for b in range((m - M_DSA) // 4 + 1)], dsa_values,
                   lambda m, j: prob[:, m % 3, j * nk1(m):(j + 1) * nk1(m)], lambda m: probT[:, m % 2])
            pe.wait_ge(a_done, M_DSA + 8)
            pe.wait_ge(s_yr, TILES)
            turn("mixed", False, lambda t, s: key_t[:, t, s * P:(s + 1) * P] if s < R_W // P else
                 p[:, t, Q0 + (s - R_W // P) * P:Q0 + (s - R_W // P + 1) * P])
            pe.wait_ge(s_xT, g0["mixed"] + 8)
            product(G["mix"], xT)
            turn("cross", True, xn_block)
            pe.wait_ge(s_xT, g0["cross"] + 8)
            product(G["cross_q"], xT)
            for k in range(4):
                pe.wait_ge(acc_free[k], G["cross_o"].used0[k] + 1)

            def cross_scores(m):
                t, i = (m - M_CROSS) // 2, (m - M_CROSS) % 2
                for j in range(2):
                    last = pe.matmul(bank(m % 3)[:, j * SEQ:(j + 1) * SEQ], cqT[:, 2 * i + j, t * P:(t + 1) * P],
                                     ckT[:, 2 * i + j], start=True, stop=True)
                return last
            attend(M_CROSS, 4, 2, cross_scores, lambda m: [(0, P), (P, P)],
                   lambda m, j, n_: cv[:, n_, (2 * ((m - M_CROSS) % 2) + j) * P:(2 * ((m - M_CROSS) % 2) + j + 1) * P],
                   lambda m, j: prob[:, m % 3, j * SEQ:(j + 1) * SEQ], lambda m: probT[:, m % 2])
            pe.wait_ge(a_done, M_CROSS + 4)
            turn("o", False, lambda t, s: co[:, t, s * P:(s + 1) * P], slabs=C_W // P)
            pe.wait_ge(s_xT, g0["o"] + 2)
            product(G["cross_o"], xT)
            turn("mlp", True, xn_block)
            pe.wait_ge(s_xT, g0["mlp"] + 8)
            for half in range(2):
                product(G[f"up{half}"], xT)
                pe.wait_ge(s_hid, (half + 1) * (FF // CHUNK // 2))
                product(G[f"down{half}"], hidT)
            turn("meta", True, lambda t, s: xn2[0:META, 0, s * P:(s + 1) * P], META, 1)
            turn("mix2", True, lambda t, s: xn2[:, t, s * P:(s + 1) * P])
            pe.wait_ge(s_xT, g0["mix2"] + 8)

            def turn_values(v0, v_free):
                for k in range(8):
                    pe.wait_ge(acc_free[k], v_free.used0[k] + 1)
                for n in range(3):
                    if n == 2:
                        pe.wait_ge(s_vr, v0 + 1)
                    for hd in range(HEADS2):
                        b = (4, 6, 4)[n] + hd // 4
                        src = vT[:, hd, META + n * P:META + (n + 1) * P] if n < 2 else vT[:, hd, 0:META]
                        last = pe.transpose(bank(b)[0:src.shape[-1], (hd % 4) * P:(hd % 4 + 1) * P], src, ident)
                    last.then_inc(s_vt, 1)

            product(G["sb_q"], xT)
            product(G["sb_kv"], xT)
            product(G["fox_q"], xT)
            turn_values(0, G["fox_kv"])
            product(G["fox_kv"], xT, (s_vr, 3))
            product(G["fox_gate"], xT)
            pe.wait_ge(s_vr, 3)
            pe.wait_ge(s_meta, 32)
            pe.wait_ge(s_c2, 1)
            for n in range(2):
                for s_ in range(SLABS):
                    last = pe.matmul(bank(4)[0:HEADS2, 0:CTX], w_logit[:, s_], xT[n][:, s_].bitcast(FP32),
                                     start=n == 0 and s_ == 0, stop=n == 1 and s_ == SLABS - 1)
            last.then_inc(s_lg, 1)
            pe.wait_ge(s_lf2, 1)
            for t in range(TILES):
                last = pe.transpose(bank(4)[:, t * HEADS2:(t + 1) * HEADS2], logf[0:HEADS2, 0, META + t * P:META + (t + 1) * P],
                                    ident[0:HEADS2, 0:HEADS2])
            last.then_inc(s_ct, 1)
            pe.wait_ge(s_cc, 1)
            for r, n in enumerate((2048, 2048, HEADS2 * CTX - 2048)):
                pe.wait_ge(s_fs, r + 1)
                if r:
                    pe.wait_ge(s_fr, r)
                for c in range(0, n, CHUNK):
                    w_ = min(CHUNK, n - c)
                    last = pe.matmul(bank(4 + c // CHUNK)[:, 0:w_], ones, sq_tmp[:, c:c + w_], start=True, stop=True)
                last.then_inc(s_fp, 1)
            pe.wait_ge(s_fr, 3)
            turn_values(3, G["out2"])
            pe.wait_ge(s_vr, 6)
            for k in range(8):
                pe.wait_ge(acc_free[k], G["out2"].used0[k] + 1)
            pe.wait_ge(s_fn, 3)

            of = lambda m: ((m - M_TWO) // 16, (m - M_TWO) % 2, (m - M_TWO) % 16 // 2)

            def two_scores(m):
                t, fox, hd = of(m)
                nk = META + (t + 1) * P
                z, tok = bank(m % 3)[:, 0:nk], slice(t * P, (t + 1) * P)
                if not fox:
                    return pe.matmul(z, sqT[:, hd, tok], skT[:, hd, 0:nk], start=True, stop=True)
                pe.matmul(z, fqT[:, hd, tok], fkT[:, hd, 0:nk], start=True, stop=False)
                return pe.matmul(z, pick[0:HEADS2, hd], logf[0:HEADS2, 1, 0:nk], start=False, stop=True)

            def two_values(m, j, n_):
                t, fox, hd = of(m)
                cols = slice(hd * P, (hd + 1) * P)
                if n_ == 0:
                    return (fv_meta if fox else sv_meta)[0:META, cols]
                return (fv if fox else sv)[:, n_ - 1, cols]

            attend(M_TWO, 32, 1, two_scores,
                   lambda m: [(0, META)] + [(META + b * P, P) for b in range((m - M_TWO) // 16 + 1)], two_values,
                   lambda m, j: prob2[:, m % 3], lambda m: probT2[:, m % 2])
            pe.wait_ge(s_mg, 2 * TILES)
            turn("merged", False, lambda t, s: merged[:, t, s * P:(s + 1) * P])
            pe.wait_ge(s_xT, g0["merged"] + 8)
            product(G["out2"], xT)
            turn("ffn", True, lambda t, s: xn3[:, t, s * P:(s + 1) * P])
            pe.wait_ge(s_xT, g0["ffn"] + 8)
            product(G["query"], xT)
            g = G["query"]
            for k in range(8):
                pe.wait_ge(acc_free[k], g.used0[k] + g.uses(k) * g.bodies + 1)
            pe.wait_ge(s_erow, 32)
            for k in range(4):
                for j in range(4):
                    last = pe.transpose(bank(4 + k)[:, j * P:(j + 1) * P], subk[:, 4 * k + j], ident)
                last.then_inc(s_sk, 1)
            pe.wait_ge(s_skT, 4)
            for t in range(TILES):
                for k in range(2 * E_HEADS):
                    last = pe.matmul(bank(4 * t + k // 4)[:, (k % 4) * P:(k % 4 + 1) * P], pqT[:, k, t * P:(t + 1) * P], subkT[:, k],
                                     start=True, stop=True)
                last.then_inc(s_sp, 1)


def kernel(**inputs):
    import concourse.bacc as bacc
    from concourse.bass_utils import run_bass_kernel_spmd

    nc = bacc.Bacc("TRN2", target_bir_lowering=False, num_devices=1)
    arrays, dram = {}, {}
    for name, value in inputs.items():
        value = np.ascontiguousarray(value)
        arrays["in_" + name] = value
        dram[name] = nc.dram_tensor("in_" + name, value.shape, mybir.dt.from_np(value.dtype), kind="ExternalInput").ap()
    out = nc.dram_tensor("out_x", (1, SEQ, D), FP32, kind="ExternalOutput").ap()
    build(nc, dram, out)
    result = run_bass_kernel_spmd(nc, [arrays], core_ids=[0])
    return result.results[0]["out_x"]
```

```python
import numpy as np
import concourse.bass as bass
from concourse import mybir
from concourse.alu_op_type import AluOpType as ALU
from contextlib import ExitStack

FP32 = mybir.dt.float32
I32 = mybir.dt.int32
U32 = mybir.dt.uint32
FP32R = mybir.dt.float32r
ACT = mybir.ActivationFunctionType
AX = mybir.AxisListType.X

P = 128
D = 2048
SEQ = 256
TILES = SEQ // P
META = 16
CTX = META + SEQ
SLABS = D // P
FF = 4 * D
R_W, R_HEAD = 1024, 64
R_HEADS = R_W // R_HEAD
LORA_W, LORA_A, LORA_G = 64, 64, 160
RWKV_COLS = 3 * R_W + LORA_W + LORA_A + LORA_G
A_W, A_HEAD, A_HEADS, A_KV = 1024, 128, 8, 2
I_HEADS, I_HEAD = 16, 64
IN_COLS = RWKV_COLS + A_W + 2 * A_KV * A_HEAD + I_HEADS * I_HEAD + I_HEAD + I_HEADS
TOPK = min(256, SEQ // 4)
C_HEADS, C_HEAD = 4, 128
C_W = C_HEADS * C_HEAD
HEADS2, HEAD2 = 8, 128
W2 = HEADS2 * HEAD2
C_IN = 7 * W2 + HEADS2
E_HEADS, E_TOP, N_KEYS = 8, 16, 128
N_EXPERTS = N_KEYS * N_KEYS
THETA = 500000.0
XW0 = 3 * R_W
XG0 = XW0 + LORA_W + LORA_A
Q0 = RWKV_COLS
K0 = Q0 + A_W
V0 = K0 + A_KV * A_HEAD
QI0 = V0 + A_KV * A_HEAD
KI0 = QI0 + I_HEADS * I_HEAD
WI0 = KI0 + I_HEAD

CHUNK = 512
SLOTS = 4
SLOT_SLABS = 2
PARTS = 4
AHEAD = 3
NEG = -1.0e30
TAKEN = -3.0e38
E_HALF = 0.6065306597126334
TWO_PI_HI = 6.28125
TWO_PI_LO = 0.0019353071795864769
PI = 3.1415925


class Product:

    def __init__(self, name, w, k, col0, widths, tok, per_body, lo=META, hi=CTX, row0=0):
        self.name, self.w, self.k, self.col0, self.widths, self.tok = name, w, k, col0, widths, tok
        self.row0, self.slabs = row0, k // P
        self.per_body, self.bodies = per_body, len(widths) // per_body
        self.lo, self.hi = lo, hi
        self.tiles = k // (P * SLOT_SLABS)
        self.turns = self.tiles * per_body // SLOTS

    def uses(self, bank):
        if not self.tok:
            return sum(bank // 4 == c % 2 for c in range(self.per_body))
        return sum(bank // 2 == c % 2 for c in range(self.per_body))

    def slab(self, i, c, n):
        return i * (self.per_body * self.slabs) + (self.slab0 + c * self.slabs + n)

    def tile(self, i, c, j):
        t = c * self.tiles + j
        return t % SLOTS, i * self.turns + (self.turn0 + t // SLOTS + 1)


def lay_out(products):
    turn, slab, used = 0, 0, [0] * 8
    for g in products:
        g.turn0, g.slab0, g.used0 = turn, slab, list(used)
        turn += g.turns * g.bodies
        slab += g.slabs * len(g.widths)
        used = [u + g.uses(b) * g.bodies for b, u in enumerate(used)]


class Chain:

    def __init__(self, eng, sem):
        self.eng, self.sem, self.n = eng, sem, 0

    def __call__(self, ins):
        self.n += 1
        ins.then_inc(self.sem, 1)
        self.eng.wait_ge(self.sem, self.n)
        return self.n


def build(nc, A, out):
    with ExitStack() as ctx:
        sems = {}

        def sem(name):
            if name not in sems:
                sems[name] = ctx.enter_context(nc.semaphore(name))
            return sems[name]

        TOTAL = 53120
        X0 = 14816
        XN, RING = SLABS * CTX, SLOTS * SLOT_SLABS * CHUNK
        BASE = X0 + 2 * XN
        MEM_AT = BASE + TILES * IN_COLS + 2 * C_HEADS * SEQ + TILES * D
        with nc.sbuf_tensor("lasting", [P, BASE], FP32) as lasting, nc.sbuf_tensor("zone", [P, TOTAL - BASE], FP32) as zone_all:
            pass
        parts, place = {}, 0
        for name, off, n in (("w_hi", RING, PARTS * CHUNK), ("w_lo", RING + PARTS * CHUNK, PARTS * CHUNK),
                             ("x_hi", X0, XN), ("x_lo", X0 + XN, XN),
                             ("hid_hi", BASE, FF * SEQ // 2 // P), ("hid_lo", BASE + FF * SEQ // 2 // P, FF * SEQ // 2 // P),
                             ("mem_hi", MEM_AT, TILES * D), ("mem_lo", MEM_AT + TILES * D, TILES * D), ("", TOTAL, 0)):
            if off > place:
                ctx.enter_context(nc.sbuf_tensor(f"space_{place}", [P, off - place], FP32))
            if n:
                parts[off] = ctx.enter_context(nc.sbuf_tensor(name, [P, n], FP32R))
            place = off + n
        ints = ctx.enter_context(nc.sbuf_tensor("ints", [P, 32], I32))
        acc = ctx.enter_context(nc.psum_tensor("acc", [P, 8, CHUNK], FP32))
        top = [0]

        def at(off, *shape):
            n = 1
            for s in shape:
                n *= s
            assert off + n <= TOTAL, (off, n)
            v = zone_all[:, off - BASE:off - BASE + n] if off >= BASE else lasting[:, off:off + n]
            assert off >= BASE or off + n <= BASE
            if len(shape) == 2:
                v = v.rearrange("p (a b) -> p a b", a=shape[0])
            if len(shape) == 3:
                v = v.rearrange("p (a b c) -> p a b c", a=shape[0], b=shape[1])
            return v

        def part_at(off, *shape):
            n = shape[0] * shape[1]
            return parts[off][:, 0:n].rearrange("p (a b) -> p a b", a=shape[0])

        def take(*shape):
            n = 1
            for s in shape:
                n *= s
            v = at(top[0], *shape)
            top[0] += n
            return v

        ring = take(SLOTS, SLOT_SLABS, CHUNK)
        w_hi, w_lo = part_at(top[0], PARTS, CHUNK), part_at(top[0] + PARTS * CHUNK, PARTS, CHUNK)
        top[0] += 2 * PARTS * CHUNK
        h = take(TILES, D)
        ident = take(P)
        tri = take(P)
        upper = take(P)
        upper16 = take(P)
        lower16 = take(P)
        lower_rest = take(P)
        halves = take(8)[:, 0:2]
        causal = take(TILES, CTX)
        strict = take(TILES, CTX)
        gains = take(7, SLABS)
        small = take(552)
        assert top[0] == X0
        xT = (part_at(X0, SLABS, CTX), part_at(X0 + XN, SLABS, CTX))
        top[0] += 2 * XN
        base = top[0]
        assert base == BASE

        bank = lambda k: acc[:, k, :]
        ssum, var, rstd = small[:, 0:4], small[:, 4:8], small[:, 8:12]
        rmax, rsum, rinv = small[:, 12:20], small[:, 20:28], small[:, 28:36]
        invf = small[:, 36:52]
        posf = small[:, 52:54]
        posi = ints[:, 0:2]
        m8 = small[:, 54:62]
        bonus = small[:, 78:110].rearrange("p (t h) -> p t h", t=TILES)
        decayC = small[:, 110:174].rearrange("p (t h c) -> p t h c", t=TILES, h=R_HEADS)
        sincos = small[:, 174:238].rearrange("p (k t j) -> p k t j", k=2, t=TILES)
        rmean, rvar = small[:, 238:254], small[:, 254:270]
        turns_f = small[:, 270:302].rearrange("p (t j) -> p t j", t=TILES)
        ang = small[:, 302:334].rearrange("p (t j) -> p t j", t=TILES)
        turns_i = ints[:, 0:32].rearrange("p (t j) -> p t j", t=TILES)
        zero_row = small[:, 334:335]
        yst = small[:, 424:488].rearrange("p (k t h) -> p k t h", k=2, t=TILES)
        kss = yst[:, 0]
        turn_tmp = small[:, 488:552].rearrange("p (k t j) -> p k t j", k=2, t=TILES)

        zone = base
        p = at(zone, TILES, IN_COLS); zone += TILES * IN_COLS
        ckT = at(zone, C_HEADS, SEQ); zone += C_HEADS * SEQ
        cv = at(zone, TILES, C_W); zone += TILES * C_W
        Z = zone
        mem = at(Z, TILES, D)
        mem_sq = at(Z + TILES * D, TILES, D)
        memT = (part_at(Z + TILES * D, SLABS, SEQ), part_at(Z + 2 * TILES * D, SLABS, SEQ))
        xn = at(Z, TILES, D)
        prev = at(Z + TILES * D, TILES, RWKV_COLS)
        mu = at(Z + TILES * D + TILES * RWKV_COLS, RWKV_COLS)
        z = Z
        key_t = at(z, TILES, R_W); z += TILES * R_W
        beta_t = at(z, TILES, R_W); z += TILES * R_W
        gate = at(z, TILES, R_W); z += TILES * R_W
        zs = z
        logd = at(z, R_W); z += R_W
        params = at(z, 4, R_W); z += 4 * R_W
        kk_sq = at(z, R_W)
        w0 = gate[:, 1]
        lora_up = at(X0, 3, R_W)
        loraT = at(X0 + 3 * R_W, 3, SEQ)
        x_rest = X0 + 3 * R_W + 3 * SEQ
        state = at(x_rest, R_W)
        lnx = at(x_rest + R_W, 2, R_W)
        tmp = at(x_rest + 3 * R_W, R_W)
        n4 = 4 * P
        spots = [X0 + i * n4 for i in range(7)] + [x_rest + 3 * R_W + i * n4 for i in range(3)]
        spots += [zs + i * n4 for i in range(26 - len(spots))]
        scr = [at(spot, 4, P) for spot in spots]
        assert X0 + 7 * n4 <= x_rest and spots[9] + n4 <= X0 + 2 * XN

        z = Z + 3 * TILES * R_W
        qiT = at(z, TILES, I_HEADS // 2, P); z += SEQ * I_HEADS // 2
        qT = at(z, TILES, A_HEADS, P); z += SEQ * A_HEADS
        score = at(z, TILES, SEQ); z += TILES * SEQ
        left = at(z, SEQ); z += SEQ
        unsel = at(z, TILES, SEQ); z += TILES * SEQ
        prob = at(z, 3, 2 * CTX); z += 6 * CTX
        probT = at(z, 2, 4 * P); z += 8 * P
        assert z <= TOTAL, z
        cqT = at(Z + 2 * TILES * R_W, C_HEADS, SEQ)
        co = at(Z + 2 * TILES * R_W + C_HEADS * SEQ, TILES, C_W)
        rel = at(X0, 4, 2, SEQ)
        kiT = at(x_rest + R_W - 3 * SEQ, SEQ)
        assert X0 + 8 * SEQ * 2 <= x_rest + R_W - 3 * SEQ
        kT = at(x_rest + R_W - 2 * SEQ, A_KV, SEQ)
        y_sq = tmp
        z = TOTAL - 4 * (A_HEADS + A_KV) * 16 - TILES * P
        rot = at(z, 4, (A_HEADS + A_KV) * 16); z += 4 * (A_HEADS + A_KV) * 16
        keyI = at(z, TILES, P)
        assert max(spots) + n4 <= TOTAL - 4 * (A_HEADS + A_KV) * 16 - TILES * P
        HALF = FF // P // 2
        hidT = (part_at(base, HALF, SEQ), part_at(base + HALF * SEQ, HALF, SEQ))
        z = base + 18144
        hmeta_xn = at(z, D); z += D
        hmeta = at(z, D); z += D
        z = base + 22528
        relu_now, square_now = at(z, 4 * SEQ), at(z + 4 * SEQ, 4 * SEQ); z += 8 * SEQ
        final_gain = at(base + 24624, D)
        head_gains = small[:, 389:391]
        fbias = small[:, 391:392]
        eps_col = small[:, 392:393]
        nmax = small[:, 367:373].rearrange("p (b j) -> p b j", j=2)
        psums = small[:, 373:381].rearrange("p (b j) -> p b j", j=2)
        pinv = small[:, 381:389].rearrange("p (b j) -> p b j", j=2)
        z = base
        sqT = at(z, HEADS2, SEQ); z += HEADS2 * SEQ
        skT = at(z, HEADS2, CTX); z += HEADS2 * CTX
        sv = at(z, TILES, W2); z += TILES * W2
        sv_meta = at(z, W2); z += W2
        fqT = at(z, HEADS2, SEQ); z += HEADS2 * SEQ
        fkT = at(z, HEADS2, CTX); z += HEADS2 * CTX
        fv = at(z, TILES, W2); z += TILES * W2
        fv_meta = at(z, W2); z += W2
        fgate = at(z, TILES, W2); z += TILES * W2
        vT = at(z, HEADS2, CTX); z += HEADS2 * CTX
        merged = at(z, TILES, D); z += TILES * D
        xn2 = merged
        ones = at(z, P); z += P
        prob2 = at(z, 3, CTX); z += 3 * CTX
        probT2 = at(z, 2, 3 * P); z += 6 * P
        stick = at(z, 3, 3, CTX); z += 9 * CTX
        seen = at(z, TILES, CTX); z += TILES * CTX
        pick = at(z, HEADS2, P); z += HEADS2 * P
        w_logit = at(z, SLABS, HEADS2); z += SLABS * HEADS2
        logf = at(z, 3, CTX); z += 3 * CTX
        cumf = at(z, TILES, HEADS2); z += TILES * HEADS2
        assert z <= TOTAL, z
        FOX_ROUNDS = [(x.rearrange("p h c -> p (h c)")[:, a:b], b - a, sq) for x, a, b, sq in (
            (fqT, 0, D, merged[:, 0]), (fkT, 0, D, merged[:, 1]), (fkT, D, HEADS2 * CTX, merged[:, 0]))]
        fox_root = stick.rearrange("p a b c -> p (a b c)")[:, 0:D]
        z = base
        hb = at(z, TILES, D); z += TILES * D
        gain_row = at(z, D); z += D
        pqT = at(z, 2 * E_HEADS, SEQ); z += 2 * E_HEADS * SEQ
        subk = at(z, 2 * E_HEADS, P); z += 2 * E_HEADS * P
        subkT = at(z, 2 * E_HEADS, P); z += 2 * E_HEADS * P
        xn3 = at(z, TILES, D); z += TILES * D
        scores = at(z, TILES, 2 * E_HEADS * N_KEYS); z += TILES * 2 * E_HEADS * N_KEYS
        bufs_z = z
        best1 = at(z, 2 * E_HEADS, E_TOP); z += 2 * E_HEADS * E_TOP
        bestf = at(z, 2 * E_HEADS, E_TOP); z += 2 * E_HEADS * E_TOP
        work1 = at(z, 256); z += 256
        best2 = at(z, TILES, E_HEADS, E_TOP); z += TILES * E_HEADS * E_TOP
        hot = at(z, E_HEADS * E_TOP, E_TOP); z += E_HEADS * E_TOP * E_TOP
        picked = at(z, 3, E_HEADS * E_TOP); z += 3 * E_HEADS * E_TOP
        iota16 = at(z, E_TOP); z += E_TOP
        experts = at(z, TILES, P + 4).bitcast(U32); z += TILES * (P + 4)
        expert_now = at(z, 32).bitcast(U32); z += 32
        dots_now = at(z, 16); z += 16
        coef_now = at(z, 16); z += 16
        dots = at(z, TILES, P); z += TILES * P
        coef = at(z, TILES, P); z += TILES * P
        esum = at(z, TILES, E_HEADS); z += TILES * E_HEADS
        assert z <= TOTAL, z
        spots = [n * D for n in range(4)] + [base + (3 + n) * D for n in range(4)] + [X0 + n * D for n in range(4)]
        spots += [base + 2 * D, base + 7 * D, base + 8 * D, z]
        assert z + D <= TOTAL
        rows_buf = [at(spot, D) for spot in spots]
        junk = scores[:, 0]

        G = {}
        w = lambda n: A[n][0]
        for g in (
            Product("in0", w("w_in"), D, 0, [CHUNK] * 2, True, 2),
            Product("cross_k", w("w_kv_cross"), D, 0, [CHUNK], False, 1, 0, SEQ),
            Product("cross_v", w("w_kv_cross"), D, C_W, [CHUNK], True, 1, 0, SEQ),
            Product("in", w("w_in"), D, 2 * CHUNK, [CHUNK] * 8, True, 2),
            Product("in_end", w("w_in"), D, 10 * CHUNK, [CHUNK, IN_COLS - 11 * CHUNK], True, 2),
            Product("mix", w("w_mix_out"), D, 0, [CHUNK] * 4, True, 2),
            Product("cross_q", w("w_q_cross"), D, 0, [CHUNK], False, 1),
            Product("cross_o", w("w_o_cross"), C_W, 0, [CHUNK] * 4, True, 4),
            Product("up0", w("w_up"), D, 0, [CHUNK] * (FF // CHUNK // 2), False, 2),
            Product("down0", w("w_down"), FF // 2, 0, [CHUNK] * 4, True, 2, 0, SEQ),
            Product("up1", w("w_up"), D, FF // 2, [CHUNK] * (FF // CHUNK // 2), False, 2),
            Product("down1", w("w_down"), FF // 2, 0, [CHUNK] * 4, True, 4, 0, SEQ, FF // 2),
            Product("sb_q", w("w_in_2"), D, 0, [CHUNK] * 2, False, 2),
            Product("sb_kv", w("w_in_2"), D, W2, [CHUNK] * 4, False, 4, 0),
            Product("fox_q", w("w_in_2"), D, 3 * W2, [CHUNK] * 2, False, 2),
            Product("fox_kv", w("w_in_2"), D, 4 * W2, [CHUNK] * 4, False, 4, 0),
            Product("fox_gate", w("w_in_2"), D, 6 * W2, [CHUNK] * 2, True, 2),
            Product("out2", w("w_out_2"), D, 0, [CHUNK] * 4, True, 4),
            Product("query", w("peer_w_query_2"), D, 0, [CHUNK] * 4, False, 4),
        ):
            G[g.name] = g
        lay_out(list(G.values()))
        following = dict(zip(list(G)[:-1], list(G)[1:]))
        tile_full = [sem(f"tile_full{i}") for i in range(SLOTS)]
        hi_ready, lo_ready = sem("hi_ready"), sem("lo_ready")
        slab_used = sem("slab_used")
        acc_free = [sem(f"acc_free{i}") for i in range(8)]

        def chunk_done(eng, g, c, i=0):
            eng.wait_ge(slab_used, g.slab(i, c, g.slabs - 1) + PARTS + 1)

        n_groups = {"x": 8, "mem": 8, "mixed": 8, "cross": 8, "o": 2, "mlp": 8, "meta": 4, "mix2": 8, "merged": 8, "ffn": 8}
        g0, n0 = {}, 0
        for name in n_groups:
            g0[name] = n0
            n0 += n_groups[name]
        norm_tiles = {"x": 2, "mem": 2, "cross": 2, "mlp": 2, "meta": 1, "final": 2, "mix2": 2, "heads2": 4, "ffn": 2}
        norm_no = {name: n for n, name in enumerate(norm_tiles)}
        sums0, xn0, xd0 = {}, {}, {}
        n0 = n1 = n2 = 0
        for name, k in norm_tiles.items():
            sums0[name], xn0[name], xd0[name] = n0, n1, n2
            n0 += k
            n1 += name not in ("final", "heads2")
            n2 += k == 2 and name != "final"
        s_ss, s_var, s_sd, s_rstd, s_xn = (sem(n) for n in (
            "squares_summed", "variance_ready", "deviation_ready", "scale_ready", "normed_ready"))
        s_xd = sem("normed_second_ready")
        s_tr, s_xh, s_xT = sem("transposed"), sem("x_hi_ready"), sem("xT_ready")
        s_const, s_vec, s_act, s_pool = sem("const_ready"), sem("vector_step"), sem("scalar_step"), sem("pool_step")
        s_gain, s_x, s_mem = sem("gains_loaded"), sem("x_loaded"), sem("mem_loaded")

        STAGES = [("turned", 1, 1), ("pairs", 1, 0), ("square", 1, 1), ("fourth", 1, 1), ("eighth", 1, 1),
                  ("inverse", 1, 0), ("solve0", 1, 1), ("solve1", 1, 0), ("solve2", 1, 0), ("solve3", 1, 0),
                  ("w_turned", 0, 1), ("sa0", 1, 0), ("state0", 1, 0), ("sa1", 1, 0), ("state1", 1, 0), ("y", 0, 1)]
        stage_no = {s[0]: n for n, s in enumerate(STAGES)}
        g_pe, g_ve, g_ac = sem("group_products"), sem("group_vector"), sem("group_scalar")

        def g_count(pair, name, u, who):
            n = stage_no[name]
            inside = n if who == 0 else sum(s[who] for s in STAGES[:n])
            whole = len(STAGES) if who == 0 else sum(s[who] for s in STAGES)
            return (pair * whole + inside) * 2 + u + 1

        def g_wait(eng, pair, name, u, who):
            if who == 0 or STAGES[stage_no[name]][who]:
                eng.wait_ge((g_pe, g_ve, g_ac)[who], g_count(pair, name, u, who))

        PAIRS = [(t, q) for t in range(TILES) for q in (0, 2)]
        (sAT, sBT, sKT, sRT, sD, sL, sDT, sAK, sRB, sRK, sX, sR, sY0) = range(13)

        def S_(u, n):
            return scr[u * 13 + n]

        def loop(eng, n, body):
            if n == 1:
                body(0)
            else:
                with eng.Fori(0, n) as i:
                    body(i)

        s_shift, s_mixed, s_par, s_lora = sem("shifted_loaded"), sem("mixed"), sem("params_loaded"), sem("lora_loaded")
        s_tanh, s_sig, s_lt, s_lT = sem("tanh_done"), sem("gate_sigmoid"), sem("lora_turned"), sem("loraT_ready")
        s_zd, s_ad, s_gd, s_cd = sem("z_done"), sem("a_done"), sem("g_done"), sem("c_done")
        s_zv, s_av, s_ze, s_ae, s_ld, s_kss, s_ksd = (sem(n) for n in (
            "z_biased", "a_biased", "z_exp", "a_exp", "logd_ready", "kk_summed", "kk_root"))
        s_cp, s_ea, s_en, s_kd, s_ep, s_el, s_gate = (sem(n) for n in (
            "c_before", "exp_before", "exp_minus", "key_scaled", "exp_plus", "elementwise", "gate_copied"))
        s_eg = sem("lora_exp")
        s_yr0, s_lnx, s_yv, s_ysd, s_yr, s_out = (sem(n) for n in (
            "y_rooted", "lnx_loaded", "y_var", "y_sd", "y_rwkv", "out_written"))
        a_S, a_sm, a_pr, a_T, a_PT, a_O, a_done = (sem(n) for n in (
            "scores_done", "max_ready", "prob_ready", "prob_turned", "probT_ready", "output_done", "output_read"))
        M_DSA, M_CROSS, M_TWO = 0, 8, 12
        s_ang, s_trig, s_rope, s_kturn, s_kT2 = (sem(n) for n in ("angle_ready", "sines_ready", "rotated", "keys_turned", "keyT_ready"))
        s_qturn, s_qT2, s_ix, s_rel, s_acc2, s_sel = (sem(n) for n in (
            "queries_turned", "queryT_ready", "index_product", "relu_ready", "index_added", "selected"))
        s_meta, s_c2, s_vt, s_vr, s_lg, s_lf0, s_lf1, s_lf2, s_ct, s_cc = (sem(n) for n in (
            "meta_loaded", "const2_ready", "values_turned", "values_read", "logits_done", "logits_biased", "logits_log",
            "cum_ready", "cum_turned", "cum_column"))
        s_fs, s_fp, s_fr, s_fn, s_l, s_mg, s_erow = (sem(n) for n in (
            "fox_squares", "fox_sums", "fox_roots", "fox_normed", "stick_log", "merged_ready", "expert_rows_loaded"))
        s_sk, s_skT, s_sp, s_sc, s_bs, s_be, s_ix0, s_dot, s_gelu, s_hb = (sem(n) for n in (
            "subkeys_turned", "subkeysT_ready", "key_scores_done", "key_scores_read", "best_shifted", "best_exp",
            "experts_numbered", "dots_ready", "gelu_done", "hb_ready"))
        s_now = sem("experts_staged")
        rows_full = [sem(f"rows_full{n}") for n in range(4)]
        rows_used = [sem(f"rows_used{n}") for n in range(4)]
        s_hm, s_hid, s_fin, s_fgain = sem("meta_rows_loaded"), sem("hidden_ready"), sem("final_norm"), sem("final_gain_loaded")
        block = ctx.enter_context(nc.Block())

        @block.sync
        def _(sp):
            def stream(g):
                rows = g.w.rearrange("(s p) n -> p s n", p=P)

                def body(i):
                    for c in range(g.per_body):
                        width = g.widths[c]
                        for j in range(g.tiles):
                            slot = g.tile(i, c, j)[0]
                            if g.slab0 or c or j >= SLOTS:
                                sp.wait_ge(lo_ready, g.slab(i, c, SLOT_SLABS * (j + 1 - SLOTS)))
                            cols = bass.ds(i * (g.per_body * CHUNK) + g.col0 + c * CHUNK, width)
                            r0 = g.row0 // P + SLOT_SLABS * j
                            sp.dma_start(ring[:, slot, :, 0:width], rows[:, r0:r0 + SLOT_SLABS, cols]
                                         ).then_inc(tile_full[slot], 16)
                loop(sp, g.bodies, body)

            for t in range(TILES):
                sp.dma_start(h[:, t], A["x"][0, t * P:(t + 1) * P, :]).then_inc(s_x, 16)
            for g in G.values():
                stream(g)
            for t in range(TILES):
                for k in range(4):
                    sp.wait_ge(rows_used[k], 2 * TILES * P // 16 + 1)
                sp.dma_start(out[0, t * P:(t + 1) * P, :], h[:, t]).then_inc(s_out, 16)
            sp.wait_ge(s_out, 16 * TILES)

        @block.gpsimd
        def _(pool):
            step = Chain(pool, s_pool)

            def keep(m, pattern, base, cm, cmp=ALU.is_ge, fill=0.0):
                return step(pool.affine_select(out=m, in_=m, pattern=pattern, base=base,
                                               channel_multiplier=cm, compare_op=cmp, fill=fill))

            def block_diagonal(m, b):
                v = m.rearrange("p (n b) -> p n b", b=b)
                keep(v, [[-b, P // b], [0, b]], 0, 1)
                keep(v, [[b, P // b], [0, b]], b - 1, -1)

            def rests(*names):
                for name in names:
                    g = G[name]

                    def body(i):
                        for c in range(g.per_body):
                            width = g.widths[c]
                            for s in range(g.slabs):
                                slot, k = g.tile(i, c, s // SLOT_SLABS)[0], s % PARTS
                                pool.wait_ge(hi_ready, g.slab(i, c, s) + 1)
                                pool.tensor_tensor(w_lo[:, k, 0:width], ring[:, slot, s % SLOT_SLABS, 0:width],
                                                   w_hi[:, k, 0:width].bitcast(FP32), ALU.subtract).then_inc(lo_ready, 1)
                    loop(pool, g.bodies, body)

            step(pool.memset(ident, 0.0))
            keep(ident, [[-1, P]], 0, 1, ALU.not_equal, 1.0)
            for m in (tri, upper, upper16):
                step(pool.memset(m, 1.0))
                keep(m, [[1, P]], 0 if m is tri else -1, -1)
                block_diagonal(m, 16 if m is upper16 else 64)
            for m, b in ((lower16, 16), (lower_rest, 64)):
                step(pool.memset(m, 1.0))
                keep(m, [[-1, P]], -1, 1)
                block_diagonal(m, b)
            step(pool.tensor_tensor(lower_rest, lower_rest, lower16, ALU.subtract))
            step(pool.memset(halves, 1.0))
            keep(halves, [[-64, 2]], 0, 1)
            keep(halves, [[64, 2]], 63, -1)
            for m, off in ((causal, 0), (strict, -1)):
                step(pool.memset(m, 0.0))
                for t in range(TILES):
                    keep(m[:, t, META:CTX], [[-1, SEQ]], t * P + off, 1, fill=NEG)
            pool.memset(zero_row, 0.0).then_inc(s_const, 1)

            step(pool.memset(eps_col, 1e-6))
            rests("in0", "cross_k", "cross_v", "in", "in_end")
            pool.wait_ge(s_mixed, TILES)
            pool.dma_start(w0, A["w_decay0"][0].partition_broadcast(P)).then_inc(s_par, 16)
            for n, name in enumerate(("a0", "k_k", "k_a")):
                pool.dma_start(params[:, n], A[name][0].partition_broadcast(P)).then_inc(s_par, 16)
            pool.dma_start(params[:, 3], A["r_k"][0].rearrange("h n -> (h n)").partition_broadcast(P)).then_inc(s_par, 16)
            TT = pool.tensor_tensor
            heads = lambda x: x.rearrange("p (h n) -> p h n", n=R_HEAD)

            def head_sums(dst, x, tmp):
                part, n = heads(tmp), R_HEAD // 2
                while n > 1:
                    step(TT(part[:, :, 0:n], x[:, :, 0:n], x[:, :, n:2 * n], ALU.add))
                    x, n = part, n // 2
                return TT(dst, part[:, :, 0], part[:, :, 1], ALU.add)

            pool.wait_ge(s_par, 16 * 5)
            for t in range(TILES):
                step(TT(key_t[:, t], p[:, t, R_W:2 * R_W], params[:, 1], ALU.mult))
                step(TT(kk_sq, key_t[:, t], key_t[:, t], ALU.mult))
                head_sums(kss[:, t], heads(kk_sq), kk_sq).then_inc(s_kss, 1)
                if t + 1 < TILES:
                    pool.wait_ge(s_kss, t + 1)
            pool.wait_ge(s_trig, 1)
            for k in range(4):
                pool.wait_ge(acc_free[k], G["mix"].used0[k] + 1)
            for t in range(TILES):
                for col, heads_n, width, half, stride in ((Q0, A_HEADS + A_KV, A_HEAD, 16, 1), (QI0, I_HEADS + 1, I_HEAD, 8, 2)):
                    x = p[:, t, col:col + heads_n * width].rearrange("p (h d) -> p h d", h=heads_n)
                    x1, x2 = x[:, :, 0:half], x[:, :, half:2 * half]
                    sn, cs = (sincos[:, k, t, 0:16:stride].unsqueeze(1).to_broadcast([P, heads_n, half]) for k in range(2))
                    r = [rot[:, k, 0:heads_n * half].rearrange("p (h d) -> p h d", h=heads_n) for k in range(4)]
                    TT(r[0], x1, cs, ALU.mult)
                    TT(r[1], x2, sn, ALU.mult)
                    TT(r[2], x2, cs, ALU.mult)
                    step(TT(r[3], x1, sn, ALU.mult))
                    TT(x1, r[0], r[1], ALU.subtract)
                    step(TT(x2, r[2], r[3], ALU.add))
                step(pool.tensor_scalar(p[:, t, WI0:WI0 + I_HEADS], p[:, t, WI0:WI0 + I_HEADS], (I_HEADS * I_HEAD) ** -0.5, None, ALU.mult))
                pool.tensor_copy(keyI[:, t].rearrange("p (a d) -> p a d", a=2),
                                 p[:, t, KI0:KI0 + I_HEAD].unsqueeze(1).to_broadcast([P, 2, I_HEAD])).then_inc(s_rope, 1)
            for u in range(2):
                g_wait(pool, len(PAIRS) - 1, "y", u, 2)
            pool.wait_ge(s_lnx, 32)
            bc = lambda x: x.unsqueeze(2).to_broadcast([P, R_HEADS, R_HEAD])

            for t in range(TILES):
                y = key_t[:, t]
                step(head_sums(yst[:, 0, t], heads(y), y_sq))
                step(pool.tensor_scalar(yst[:, 0, t], yst[:, 0, t], 1.0 / R_HEAD, None, ALU.mult))
                step(TT(heads(y), heads(y), bc(yst[:, 0, t]), ALU.subtract))
                step(TT(y_sq, y, y, ALU.mult))
                step(head_sums(yst[:, 1, t], heads(y_sq), y_sq))
                pool.tensor_scalar(yst[:, 1, t], yst[:, 1, t], 1.0 / R_HEAD, 64e-5, ALU.mult, ALU.add).then_inc(s_yv, 1)
            pool.wait_ge(s_ysd, 1)
            for t in range(TILES):
                y = key_t[:, t]
                step(TT(heads(y), heads(y), bc(yst[:, 1, t]), ALU.mult))
                step(TT(y, y, lnx[:, 0], ALU.mult))
                step(TT(y, y, lnx[:, 1], ALU.add))
                step(TT(heads(y_sq), heads(p[:, t, 2 * R_W:3 * R_W]), bc(bonus[:, t]), ALU.mult))
                step(TT(y, y, y_sq, ALU.add))
                TT(y, y, gate[:, t], ALU.mult).then_inc(s_yr, 1)

            rests("mix", "cross_q", "cross_o", "up0", "down0", "up1", "down1")
            for k in range(8):
                pool.wait_ge(acc_free[k], G["sb_q"].used0[k] + 1)
            pool.dma_start(w_logit, A["w_in_2"][0].rearrange("(s p) n -> p s n", p=P)[:, :, 7 * W2:C_IN]).then_inc(s_meta, 16)
            step(pool.memset(pick[0:HEADS2], 0.0))
            keep(pick[0:HEADS2], [[-1, HEADS2], [0, P]], 0, 1, ALU.not_equal, 1.0)
            pool.memset(ones, 1.0).then_inc(s_c2, 1)
            rests("sb_q", "sb_kv", "fox_q", "fox_kv", "fox_gate", "out2", "query")
            zero4 = zero_row.bitcast(U32).to_broadcast([P, 4])
            now = lambda n: expert_now[:, 4 * (n % 8):4 * (n % 8) + 4]
            for k in range(4):
                pool.sem_inc(rows_used[k], 1)
            pool.wait_ge(s_sp, 4)
            per, rounds, staged = P // 32, 0, 0
            for phase, table in enumerate((A["peer_u_2"][0], A["peer_v_2"][0])):
                for t in range(TILES):
                    pool.wait_ge(s_ix0, 5 * t + 1)
                    if staged:
                        pool.wait_ge(s_now, staged)
                    pool.tensor_tensor(now(0), experts[:, t, 0:4], zero4, ALU.add).then_inc(s_now, 1)
                    with pool.Fori(0, per) as i:
                        for n in range(8):
                            pool.wait_ge(rows_used[n % 4], i * 2 + (rounds + n // 4 + 1))
                            pool.wait_ge(s_now, i * 8 + (staged + n + 1))
                            if n == 7:
                                pool.wait_ge(s_ix0, i + (5 * t + 2))
                            pool.tensor_tensor(now(n + 1), experts[:, t, bass.ds(i * 32 + 4 * (n + 1), 4)], zero4, ALU.add
                                               ).then_inc(s_now, 1)
                            for j in range(4):
                                pool.indirect_dma_start(
                                    out=rows_buf[4 * (n % 4) + j], out_offset=None, in_=table,
                                    in_offset=bass.IndirectOffsetOnAxis(ap=now(n)[:, j:j + 1], axis=0)
                                ).then_inc(rows_full[n % 4], 16)
                    rounds, staged = rounds + 2 * per, staged + 8 * per + 1

        @block.scalar
        def _(act):
            step = Chain(act, s_act)
            for dst, name in [(gains[:, 0], "norm_mem"), (gains[:, 1], "norm_mix"), (gains[:, 2], "norm_cross"),
                              (gains[:, 3], "norm_mlp"), (gains[:, 4], "norm_mix_2"), (gains[:, 5, 0:8], "sb_out_gain_2"),
                              (gains[:, 5, 8:16], "fox_out_gain_2"), (gains[:, 6], "norm_ffn_2"),
                              (head_gains[:, 0:1], "fox_q_gain_2"), (head_gains[:, 1:2], "fox_k_gain_2")]:
                act.dma_start(dst, A[name][0].rearrange("(s p) -> p s", p=P), allow_slow_non_contiguous=True).then_inc(s_gain, 16)
            act.dma_start(fbias[0:HEADS2], A["b_forget_2"].rearrange("l h -> h l"), allow_slow_non_contiguous=True).then_inc(s_gain, 16)
            act.dma_start(posi, A["positions"][0].rearrange("(t p) -> p t", p=P), allow_slow_non_contiguous=True).then_inc(s_gain, 16)

            def norm_start(name, src, rows=P, xn=xn):
                act.activation(xn[0:rows, 0], src(0), ACT.Square, accum_out=ssum[0:rows, 0:1]).then_inc(s_ss, 1)

            def norm_finish(name, src, rows=P, xn=xn):
                tiles = norm_tiles[name]
                act.wait_ge(s_var, norm_no[name] + 1)
                act.activation(rstd[0:rows, 0:tiles], var[0:rows, 0:tiles], ACT.Sqrt).then_inc(s_sd, 1)
                act.wait_ge(s_rstd, norm_no[name] + 1)
                if name != "final":
                    act.activation(xn[0:rows, 0], src(0), ACT.Copy, scale=var[0:rows, 0:1]).then_inc(s_xn, 1)

            def norm_rows(*args):
                norm_start(*args)
                norm_finish(*args)

            def hi(g, i, c, s, width=None):
                width = width or g.widths[min(c, len(g.widths) - 1)]
                slot, turn = g.tile(i, c, s // SLOT_SLABS)
                if s % SLOT_SLABS == 0:
                    act.wait_ge(tile_full[slot], 16 * turn)
                act.wait_ge(slab_used, g.slab(i, c, s) + 1)
                act.activation(w_hi[:, s % PARTS, 0:width], ring[:, slot, s % SLOT_SLABS, 0:width], ACT.Copy).then_inc(hi_ready, 1)

            def round_and_read(g, read=lambda i, c: None, before_last=None, between={}):
                def chunk(i, c, last):
                    for s in range(AHEAD, g.slabs):
                        hi(g, i, c, s)
                        if (c, s) in between:
                            between[c, s]()
                    if last and g.name in following:
                        for s in range(AHEAD):
                            hi(G[following[g.name]], 0, 0, s)
                    elif not last:
                        for s in range(AHEAD):
                            hi(g, i, c + 1, s)
                    read(i, c)

                def body(i):
                    for c in range(g.per_body):
                        chunk(i, c, False)
                if g.bodies > 1:
                    loop(act, g.bodies - 1, body)
                if before_last:
                    before_last()
                for c in range(g.per_body):
                    chunk(g.bodies - 1, c, c == g.per_body - 1)

            def round_turned(name, dst, gain, rows=P, tiles=TILES, slabs=SLABS, off=META, some=None):
                for t in some or range(tiles):
                    for k in range(slabs // 4):
                        group = g0[name] + t * (slabs // 4) + k
                        act.wait_ge(s_tr, group + 1)
                        src = bank(4 + group % 4)[:, 0:4 * rows].rearrange("p (s c) -> p s c", s=4)
                        cols = slice(off + t * P, off + t * P + rows)
                        if gain is None:
                            act.activation(dst[:, 4 * k:4 * k + 4, cols], src, ACT.Copy).then_inc(s_xh, 1)
                            continue
                        for j in range(4):
                            last = act.activation(dst[:, 4 * k + j, cols], src[:, j], ACT.Copy,
                                                  scale=gains[:, gain, 4 * k + j:4 * k + j + 1])
                        last.then_inc(s_xh, 1)

            def reader(g, put):
                def read(i, c):
                    chunk_done(act, g, c, i)
                    for t in range(TILES):
                        k = 2 * (c % 2) + t
                        put(t, i, c, bank(k)[:, 0:g.widths[c]]).then_inc(acc_free[k], 1)
                return read

            act.wait_ge(s_x, 16 * TILES)
            norm_rows("x", lambda t: h[:, t])
            act.wait_ge(s_gain, 16 * 12)
            for s in range(AHEAD):
                hi(G["in0"], 0, 0, s)
            round_turned("x", xT[0], 1)
            for t in range(TILES):
                act.dma_start(mem[:, t], A["mem"][0, t * P:(t + 1) * P, :]).then_inc(s_mem, 16)

            def start_mem():
                act.wait_ge(s_mem, 16 * TILES)
                norm_start("mem", lambda t: mem[:, t], P, mem_sq)
            round_and_read(G["in0"], reader(G["in0"], lambda t, i, c, src: act.activation(
                p[:, t, c * CHUNK:(c + 1) * CHUNK], src, ACT.Copy)), between={
                    (0, 8): start_mem, (0, 13): lambda: norm_finish("mem", lambda t: mem[:, t], P, mem),
                    (1, 5): lambda: round_turned("mem", memT[0], 0, off=0, some=(0,)),
                    (1, 10): lambda: round_turned("mem", memT[0], 0, off=0, some=(1,))})

            def read_ck(i, c):
                chunk_done(act, G["cross_k"], 0)
                for f in range(4):
                    act.activation(ckT[:, f], bank(f)[:, 0:SEQ], ACT.Copy).then_inc(acc_free[f], 1)
            round_and_read(G["cross_k"], read_ck)
            round_and_read(G["cross_v"], reader(G["cross_v"], lambda t, i, c, src: act.activation(cv[:, t], src, ACT.Copy)))
            g = G["in"]

            def shift():
                act.wait_ge(s_ang, 1)
                act.activation(sincos[:, 0], ang, ACT.Sin)
                act.wait_ge(s_ang, 2)
                act.activation(sincos[:, 1], turns_f, ACT.Sin).then_inc(s_trig, 1)
                act.dma_start(mu, A["rwkv_mu"][0].partition_broadcast(P)).then_inc(s_shift, 16)
                for k in range(4):
                    act.wait_ge(acc_free[k], g.used0[k] + g.bodies)
                for t in range(TILES):
                    act.dma_start(prev[1:P, t], p[0:P - 1, t, 0:RWKV_COLS]).then_inc(s_shift, 16)
                act.dma_start(prev[0:1, 1], p[P - 1:P, 0, 0:RWKV_COLS]).then_inc(s_shift, 16)
            round_and_read(g, reader(g, lambda t, i, c, src: act.activation(
                p[:, t, bass.ds(i * (2 * CHUNK) + (2 + c) * CHUNK, CHUNK)], src, ACT.Copy)), shift)
            g = G["in_end"]
            round_and_read(g, reader(g, lambda t, i, c, src: act.activation(
                p[:, t, G["in_end"].col0 + c * CHUNK:G["in_end"].col0 + c * CHUNK + G["in_end"].widths[c]], src, ACT.Copy)))
            act.dma_start(lora_up[0:LORA_W, 0], A["w_decay_up"][0]).then_inc(s_lora, 16)
            act.dma_start(lora_up[LORA_W:P, 0], A["a_up"][0]).then_inc(s_lora, 16)
            act.dma_start(lora_up[:, 1], A["g_up"][0, 0:P]).then_inc(s_lora, 16)
            act.dma_start(lora_up[0:LORA_G - P, 2], A["g_up"][0, P:LORA_G]).then_inc(s_lora, 16)
            act.dma_start(lnx[:, 0], A["lnx_w"][0].partition_broadcast(P)).then_inc(s_lnx, 16)
            act.dma_start(lnx[:, 1], A["lnx_b"][0].partition_broadcast(P)).then_inc(s_lnx, 16)

            act.wait_ge(s_mixed, TILES)
            for t in range(TILES):
                xw = p[:, t, XW0:XW0 + LORA_W]
                xg = p[:, t, XG0:XG0 + LORA_G]
                act.activation(xw, xw, ACT.Tanh).then_inc(s_tanh, 1)
                act.activation(xg, xg, ACT.Exp, scale=-1.0).then_inc(s_eg, 1)
            for t in range(TILES):
                act.wait_ge(s_zv, t + 1)
                act.activation(tmp, tmp, ACT.Exp, scale=-1.0).then_inc(s_ze, 1)
                act.wait_ge(s_av, t + 1)
                act.activation(beta_t[:, t], beta_t[:, t], ACT.Exp, scale=-1.0).then_inc(s_ae, 1)
                act.wait_ge(s_gd, t + 1)
                act.activation(gate[:, t], acc[:, 0:2].rearrange("p a b -> p (a b)"), ACT.Copy).then_inc(s_gate, 1)
                act.wait_ge(s_kss, t + 1)
                act.activation(kss[:, t], kss[:, t], ACT.Sqrt).then_inc(s_ksd, 1)
                act.wait_ge(s_cp, t + 1)
                act.activation(tmp, tmp, ACT.Exp).then_inc(s_ea, 1)
                c_all = acc[:, 2:4].rearrange("p a b -> p (a b)")
                act.activation(logd, c_all, ACT.Exp, scale=-1.0).then_inc(s_en, 1)
                act.activation(decayC[0:R_HEAD, t], bank(6)[0:R_HEAD, 0:2 * R_HEADS].rearrange("p (h c) -> p h c", c=2),
                               ACT.Exp)
                act.wait_ge(s_kd, t + 1)
                act.activation(tmp, c_all, ACT.Exp).then_inc(s_ep, 1)

            for n, (t, q) in enumerate(PAIRS):
                def copy(u, dst, b):
                    return act.activation(dst, b, ACT.Copy)
                for u in range(2):
                    g_wait(act, n, "turned", u, 0)
                    B = 4 * u
                    copy(u, S_(u, sKT)[0:64], bank(B + 2)[0:64].rearrange("p (j c) -> p j c", j=4))
                    copy(u, S_(u, sRT)[0:64], bank(B + 3)[0:64].rearrange("p (j c) -> p j c", j=4)).then_inc(g_ac, 1)
                b4 = lambda k: bank(k).rearrange("p (j c) -> p j c", j=4)
                for u in range(2):
                    B = 4 * u
                    g_wait(act, n, "square", u, 0)
                    copy(u, S_(u, sKT), b4(B + 1))
                    copy(u, S_(u, sBT), b4(B + 2))
                    cols = slice((q + u) * 256, (q + u) * 256 + 256)
                    copy(u, S_(u, sR)[:, :, 0:64], key_t[:, t, cols].rearrange("p (j c) -> p j c", j=4))
                    copy(u, S_(u, sR)[:, :, 64:128], b4(B + 3)[:, :, 0:64]).then_inc(g_ac, 1)
                for u in range(2):
                    B = 4 * u
                    g_wait(act, n, "fourth", u, 0)
                    copy(u, S_(u, sD), b4(B + 1))
                    copy(u, S_(u, sDT), b4(B + 2)).then_inc(g_ac, 1)
                for u in range(2):
                    g_wait(act, n, "eighth", u, 0)
                    copy(u, S_(u, sKT), b4(4 * u + 1)).then_inc(g_ac, 1)
                for u in range(2):
                    g_wait(act, n, "solve0", u, 0)
                    copy(u, S_(u, sY0), b4(4 * u + 1)).then_inc(g_ac, 1)
                for u in range(2):
                    g_wait(act, n, "w_turned", u, 0)
                    copy(u, S_(u, sAT)[0:64], b4(4 * u)[0:64]).then_inc(g_ac, 1)
                for u in range(2):
                    g_wait(act, n, "y", u, 0)
                    cols = slice((q + u) * 256, (q + u) * 256 + 256)
                    copy(u, key_t[:, t, cols].rearrange("p (j c) -> p j c", j=4), b4(4 * u + 1)[:, :, 0:64]).then_inc(g_ac, 1)
            act.wait_ge(s_kturn, 1)
            act.activation(kiT, bank(0)[:, 0:SEQ], ACT.Copy)
            act.activation(kT, bank(1).rearrange("p (k s) -> p k s", k=A_KV), ACT.Copy).then_inc(s_kT2, 1)
            for t in range(TILES):
                act.wait_ge(s_qturn, t + 1)
                act.activation(qiT[:, t], acc[:, 2:4].rearrange("p a (j c) -> p (a j) c", c=P), ACT.Copy)
                act.activation(qT[:, t], acc[:, 4:6].rearrange("p a (j c) -> p (a j) c", c=P), ACT.Copy,
                               scale=A_HEAD ** -0.5).then_inc(s_qT2, 1)
                nk = (t + 1) * P
                for i in range(I_HEADS // 2):
                    m = t * (I_HEADS // 2) + i
                    if m == 14:
                        act.wait_ge(s_yv, TILES)
                        act.activation(yst[:, 1], yst[:, 1], ACT.Sqrt).then_inc(s_yr0, 1)
                    act.wait_ge(s_ix, m + 1)
                    if m >= 4:
                        act.wait_ge(s_acc2, m - 3)
                    act.activation(rel[:, m % 4, :, 0:nk], acc[:, 6 * (m % 2):6 * (m % 2) + 2, 0:nk],
                                   ACT.Relu).then_inc(s_rel, 1)


            def attend(m0, n, exps, blocks, pre=None):
                for m in range(m0, m0 + n + 2):
                    if pre and m < m0 + n:
                        pre(m)
                    if m0 <= m - 1 < m0 + n:
                        act.wait_ge(a_sm, m)
                        if m - 1 >= 4:
                            act.wait_ge(a_done, m - 4)
                        if m - 1 >= 3:
                            act.wait_ge(a_T, m - 3)
                        exps(m - 1)
                    if m0 <= m - 2:
                        act.wait_ge(a_T, m - 1)
                        if m - 2 >= 2:
                            act.wait_ge(a_O, m - 3)
                        blocks(m - 2)

            def exps_of(src, nk):
                def go(m):
                    for j in range(2):
                        last = act.activation(prob[:, m % 3, j * nk(m):(j + 1) * nk(m)], src(m, j), ACT.Exp,
                                              bias=nmax[:, m % 3, j:j + 1], accum_out=psums[:, m % 4, j:j + 1])
                    last.then_inc(a_pr, 1)
                return go

            def blocks_of(nb):
                def go(m):
                    n = 2 * nb(m) * P
                    act.activation(probT[:, m % 2, 0:n], bank(3 + m % 2)[:, 0:n], ACT.Copy).then_inc(a_PT, 1)
                return go

            tile_of = lambda m: (m - M_DSA) // 4
            nk1 = lambda m: (tile_of(m) + 1) * P
            attend(M_DSA, 8, exps_of(lambda m, j: prob[:, m % 3, j * nk1(m):(j + 1) * nk1(m)], nk1),
                   blocks_of(lambda m: tile_of(m) + 1))

            round_turned("mixed", xT[0], None)
            round_and_read(G["mix"])
            for k in range(8):
                act.wait_ge(acc_free[k], G["cross_q"].used0[k] + 1)
            norm_rows("cross", lambda t: h[:, t])
            round_turned("cross", xT[0], 2)

            def read_cq(i, c):
                chunk_done(act, G["cross_q"], 0)
                for f in range(4):
                    act.activation(cqT[:, f], bank(f)[:, 0:SEQ], ACT.Copy, scale=C_HEAD ** -0.5).then_inc(acc_free[f], 1)
            round_and_read(G["cross_q"], read_cq)
            sc = lambda m, j: bank(m % 3)[:, j * SEQ:(j + 1) * SEQ]
            attend(M_CROSS, 4, exps_of(sc, lambda m: SEQ), blocks_of(lambda m: 2))
            round_turned("o", xT[0], None, slabs=C_W // P)
            round_and_read(G["cross_o"])
            for k in range(8):
                act.wait_ge(acc_free[k], G["up0"].used0[k] + 1)
            norm_rows("mlp", lambda t: h[:, t])
            act.dma_start(final_gain, A["norm_final"].partition_broadcast(P)).then_inc(s_fgain, 16)
            act.dma_start(hmeta[0:META], A["meta_tokens_2"]).then_inc(s_hm, 16)
            round_turned("mlp", xT[0], 3)
            meta_norm = ("meta", lambda t: hmeta[0:META], META, hmeta_xn.unsqueeze(1))
            round_and_read(G["up0"])
            round_and_read(G["down0"])
            round_and_read(G["up1"])
            act.wait_ge(s_hm, 16)
            round_and_read(G["down1"], between={
                (0, 6): lambda: norm_start(*meta_norm), (0, 14): lambda: norm_finish(*meta_norm),
                (1, 12): lambda: round_turned("meta", xT[0], 4, META, 1, off=0)})
            for k in range(8):
                act.wait_ge(acc_free[k], G["sb_q"].used0[k] + 1)
            norm_rows("final", lambda t: h[:, t], P, at(base, TILES, D))

            act.wait_ge(s_fin, 1)
            norm_rows("mix2", lambda t: h[:, t], P, xn2)
            round_turned("mix2", xT[0], 4)

            def reader_T(name, dsts, width, scale=1.0):
                g = G[name]

                def read(i, c):
                    chunk_done(act, g, c, i)
                    flat = dsts[c // 2].rearrange("p h c -> p (h c)")
                    for f in range(4):
                        at_, b = i * (8 * width) + (c % 2 * 4 + f) * width, 4 * (c % 2) + f
                        act.activation(flat[:, bass.ds(at_, width)], bank(b)[:, 0:width],
                                       ACT.Copy, scale=scale).then_inc(acc_free[b], 1)
                return read

            def read_values(v, v_meta, n0):
                two = lambda k, rows: acc[0:rows, k:k + 2].rearrange("p a c -> p (a c)")
                for t in range(TILES):
                    act.wait_ge(s_vt, n0 + t + 1)
                    act.activation(v[:, t], two(4 + 2 * t, P), ACT.Copy).then_inc(s_vr, 1)
                act.wait_ge(s_vt, n0 + 3)
                act.activation(v_meta[0:META], two(4, META), ACT.Copy).then_inc(s_vr, 1)

            round_and_read(G["sb_q"], reader_T("sb_q", (sqT,), SEQ, HEAD2 ** -0.5))
            round_and_read(G["sb_kv"], reader_T("sb_kv", (skT, vT), CTX))
            round_and_read(G["fox_q"], reader_T("fox_q", (fqT,), SEQ))
            read_values(sv, sv_meta, 0)
            round_and_read(G["fox_kv"], reader_T("fox_kv", (fkT, vT), CTX))
            def log_gates():
                act.wait_ge(s_lg, 1)
                act.activation(logf[0:HEADS2, 0], bank(3)[0:HEADS2, 0:CTX], ACT.Identity, bias=fbias[0:HEADS2]).then_inc(s_lf0, 1)
                act.wait_ge(s_lf0, 1)
                step(act.activation(logf[0:HEADS2, 1], logf[0:HEADS2, 0], ACT.Abs))
                step(act.activation(logf[0:HEADS2, 1], logf[0:HEADS2, 1], ACT.Exp, scale=-1.0))
                act.activation(logf[0:HEADS2, 1], logf[0:HEADS2, 1], ACT.Ln, bias=1.0).then_inc(s_lf1, 1)

            def fox_roots(r):
                n = FOX_ROUNDS[r][1]
                act.wait_ge(s_fp, r + 1)
                if r:
                    act.wait_ge(s_fn, r)
                act.activation(fox_root[:, 0:n], acc[:, 4:8].rearrange("p a c -> p (a c)")[:, 0:n], ACT.Sqrt,
                               scale=1.0 / HEAD2, bias=eps_col).then_inc(s_fr, 1)

            round_and_read(G["fox_gate"], reader(G["fox_gate"], lambda t, i, c, src: act.activation(
                fgate[:, t, c * CHUNK:(c + 1) * CHUNK], src, ACT.Exp, scale=-1.0)),
                between={(0, 6): log_gates, (0, 11): lambda: fox_roots(0), (1, 8): lambda: fox_roots(1)})
            fox_roots(2)
            read_values(fv, fv_meta, 3)

            of = lambda m: ((m - M_TWO) // 16, (m - M_TWO) % 2, (m - M_TWO) % 16 // 2)
            nk2 = lambda m: META + ((m - M_TWO) // 16 + 1) * P

            def stick_log(m):
                t, fox, hd = of(m)
                if fox:
                    return
                act.wait_ge(a_S, m + 1)
                act.wait_ge(a_sm, m - 2)
                x = stick[:, m % 3, 0, 0:nk2(m)]
                step(act.activation(x, bank(m % 3)[:, 0:nk2(m)], ACT.Abs))
                step(act.activation(x, x, ACT.Exp, scale=-1.0))
                act.activation(x, x, ACT.Ln, bias=1.0).then_inc(s_l, 1)

            def two_exps(m):
                t, fox, hd = of(m)
                pr = prob2[:, m % 3, 0:nk2(m)]
                if fox:
                    act.activation(pr, pr, ACT.Exp, bias=nmax[:, m % 3, 0:1], accum_out=psums[:, m % 4, 0:1]).then_inc(a_pr, 1)
                else:
                    act.activation(pr, stick[:, m % 3, 1, 0:nk2(m)], ACT.Exp).then_inc(a_pr, 1)

            def two_blocks(m):
                n = ((m - M_TWO) // 16 + 1) * P
                src = bank(3 + m % 2)
                act.activation(probT2[0:META, m % 2, 0:P], src[0:META, 0:P], ACT.Copy)
                act.activation(probT2[:, m % 2, P:P + n], src[:, P:P + n], ACT.Copy).then_inc(a_PT, 1)

            attend(M_TWO, 32, two_exps, two_blocks, stick_log)
            act.wait_ge(a_done, M_TWO + 32)
            act.dma_start(gain_row, A["norm_ffn_2"][0].partition_broadcast(P)).then_inc(s_erow, 16)
            act.dma_start(subk, A["peer_sub_keys_2"][0].rearrange("h q n c -> n (h q) c")).then_inc(s_erow, 16)
            for t in range(TILES):
                for kind in range(2):
                    act.activation(at(base + (2 * t + kind) * W2, W2), merged[:, t, kind * W2:(kind + 1) * W2], ACT.Square,
                                   accum_out=ssum[:, 2 * t + kind:2 * t + kind + 1]).then_inc(s_ss, 1)
            act.wait_ge(s_var, norm_no["heads2"] + 1)
            act.activation(rstd[:, 0:4], var[:, 0:4], ACT.Sqrt).then_inc(s_sd, 1)
            round_turned("merged", xT[0], 5)

            def read_subkeys():
                for k in range(4):
                    act.wait_ge(s_sk, k + 1)
                    act.activation(subkT[:, 4 * k:4 * k + 4], bank(4 + k).rearrange("p (j c) -> p j c", j=4), ACT.Copy).then_inc(s_skT, 1)
            round_and_read(G["out2"], between={(1, 8): read_subkeys})
            for k in range(8):
                act.wait_ge(acc_free[k], G["query"].used0[k] + 1)
            norm_rows("ffn", lambda t: h[:, t], P, xn3)
            round_turned("ffn", xT[0], 6)
            def read_scores(c):
                act.wait_ge(s_sp, c + 1)
                b = 4 * (c % 2)
                act.activation(scores[:, :, c * CHUNK:(c + 1) * CHUNK], acc[:, b:b + TILES], ACT.Copy).then_inc(s_sc, 1)
            round_and_read(G["query"], reader_T("query", (pqT, pqT[:, 8:16]), SEQ),
                           between={(c + 1, 12): lambda c=c: read_scores(c) for c in range(3)})
            read_scores(3)
            for t in range(TILES):
                act.wait_ge(s_bs, t + 1)
                act.activation(coef[:, t], coef[:, t], ACT.Exp).then_inc(s_be, 1)
            act.wait_ge(s_dot, TILES)
            act.activation(dots, dots, ACT.Gelu).then_inc(s_gelu, 1)

        @block.vector
        def _(dve):
            step = Chain(dve, s_vec)
            TT, TS, STT, RED = dve.tensor_tensor, dve.tensor_scalar, dve.scalar_tensor_tensor, dve.tensor_reduce

            def norm_scale(name, eps, rows=P, width=D, src=None, xn=xn, normed=None):
                tiles = norm_tiles[name]
                if src:
                    dve.drain()
                    dve.tensor_tensor_reduce(out=xn[:, 1], in0=src(1), in1=src(1), scale=1.0, scalar=0.0, op0=ALU.mult,
                                             op1=ALU.add, accum_out=ssum[:, 1:2]).then_inc(s_ss, 1)
                dve.wait_ge(s_ss, sums0[name] + tiles)
                TS(var[0:rows, 0:tiles], ssum[0:rows, 0:tiles], 1.0 / width, eps, ALU.mult, ALU.add).then_inc(s_var, 1)
                dve.wait_ge(s_sd, norm_no[name] + 1)
                dve.reciprocal(var[0:rows, 0:tiles], rstd[0:rows, 0:tiles]).then_inc(s_rstd, 1)
                if src and name != "final":
                    dve.wait_ge(s_rstd, norm_no[name] + 1)
                    TS((xn if normed is None else normed)[:, 1], src(1), var[:, 1:2], None, ALU.mult).then_inc(s_xd, 1)

            def rest_turned(name, dst, gain, rows=P, tiles=TILES, slabs=SLABS, off=META):
                for t in range(tiles):
                    for k in range(slabs // 4):
                        group = g0[name] + t * (slabs // 4) + k
                        dve.wait_ge(s_xh, group + 1)
                        src = bank(4 + group % 4)[:, 0:4 * rows].rearrange("p (s c) -> p s c", s=4)
                        cols = slice(off + t * P, off + t * P + rows)
                        hi, lo = (x[:, 4 * k:4 * k + 4, cols] for x in dst)
                        if gain is None:
                            last = TT(lo, src, hi.bitcast(FP32), ALU.subtract)
                        else:
                            for j in range(4):
                                last = STT(lo[:, j], src[:, j], gains[:, gain, 4 * k + j:4 * k + j + 1],
                                           hi[:, j].bitcast(FP32), ALU.mult, ALU.subtract)
                        last.then_inc(s_xT, 1)

            rows_of_h = lambda t: h[:, t]
            dve.wait_ge(s_x, 16 * TILES)
            norm_scale("x", 1e-5, src=rows_of_h)
            dve.wait_ge(s_gain, 16 * 12)
            rest_turned("x", xT, 1)
            dve.wait_ge(s_mem, 16 * TILES)
            norm_scale("mem", 1e-5, src=lambda t: mem[:, t], xn=mem_sq, normed=mem)
            rest_turned("mem", memT, 0, off=0)
            def whole_turns(x, off):
                step(TS(turns_f, x, 1.0 / (2 * 3.141592653589793), off / (2 * 3.141592653589793), ALU.mult, ALU.add))
                step(dve.tensor_copy(turns_i, turns_f))
                step(dve.tensor_copy(turns_f, turns_i))
                step(STT(rot2, turns_f, -TWO_PI_HI, x, ALU.mult, ALU.add))
                step(STT(rot2, turns_f, -TWO_PI_LO, rot2, ALU.mult, ALU.add))
                step(dve.tensor_scalar_add(rot2, rot2, off))

            rot2, cos_ang = turn_tmp[:, 0], turn_tmp[:, 1]
            for j in range(16):
                dve.memset(invf[:, j:j + 1], float(np.float32(THETA) ** np.float32(-j / 16)))
            step(dve.tensor_copy(posf, posi))
            step(TT(ang, posf.unsqueeze(2).to_broadcast([P, TILES, 16]), invf.unsqueeze(1).to_broadcast([P, TILES, 16]), ALU.mult))
            whole_turns(ang, 3.141592653589793 / 2)
            step(TS(turns_f, rot2, -PI, PI, ALU.max, ALU.min))
            step(dve.tensor_copy(cos_ang, turns_f))
            whole_turns(ang, 0.0)
            TS(ang, rot2, -PI, PI, ALU.max, ALU.min).then_inc(s_ang, 1)
            dve.tensor_copy(turns_f, cos_ang).then_inc(s_ang, 1)
            chunk_done(dve, G["cross_v"], 0)
            step(dve.memset(prev[0:1, 0], 0.0))
            dve.wait_ge(s_shift, 16 * 4)
            for t in range(TILES):
                cur = p[:, t, 0:RWKV_COLS]
                step(TT(prev[:, t], prev[:, t], cur, ALU.subtract))
                step(TT(prev[:, t], prev[:, t], mu, ALU.mult))
                TT(cur, cur, prev[:, t], ALU.add).then_inc(s_mixed, 1)
            for t in range(TILES):
                xg = p[:, t, XG0:XG0 + LORA_G]
                dve.wait_ge(s_eg, t + 1)
                step(dve.tensor_scalar_add(xg, xg, 1.0))
                dve.reciprocal(xg, xg).then_inc(s_sig, 1)
            dve.wait_ge(s_lt, 1)
            step(dve.tensor_copy(loraT[:, 0:2], acc[:, 4:6, 0:SEQ]))
            dve.tensor_copy(loraT[0:LORA_G - P, 2], bank(6)[0:LORA_G - P, 0:SEQ]).then_inc(s_lT, 1)
            step(dve.memset(state[0:R_HEAD], 0.0))
            dve.wait_ge(s_par, 16 * 5)
            heads = lambda x: x.rearrange("p (h n) -> p h n", n=R_HEAD)
            for t in range(TILES):
                r_, k_ = p[:, t, 0:R_W], p[:, t, R_W:2 * R_W]
                a_, kk = beta_t[:, t], key_t[:, t]
                if t:
                    dve.wait_ge(s_el, t)
                dve.wait_ge(s_zd, t + 1)
                TT(tmp, acc[:, 4:6].rearrange("p a b -> p (a b)"), w0, ALU.add).then_inc(s_zv, 1)
                dve.wait_ge(s_ad, t + 1)
                TT(a_, acc[:, 6:8].rearrange("p a b -> p (a b)"), params[:, 0], ALU.add).then_inc(s_av, 1)
                dve.wait_ge(s_ze, t + 1)
                step(dve.tensor_scalar_add(tmp, tmp, 1.0))
                step(dve.reciprocal(logd, tmp))
                dve.tensor_scalar_mul(logd, logd, -E_HALF).then_inc(s_ld, 1)
                dve.wait_ge(s_ae, t + 1)
                step(dve.tensor_scalar_add(a_, a_, 1.0))
                step(dve.reciprocal(a_, a_))
                step(STT(tmp, a_, -1.0, params[:, 2], ALU.add, ALU.mult))
                dve.wait_ge(s_kss, t + 1)
                step(STT(k_, tmp, 1.0, k_, ALU.add, ALU.mult))
                step(TT(tmp, r_, k_, ALU.mult))
                step(TT(tmp, tmp, params[:, 3], ALU.mult))
                step(RED(bonus[:, t], heads(tmp), AX, ALU.add))
                dve.wait_ge(s_ksd, t + 1)
                step(dve.tensor_scalar_max(kss[:, t], kss[:, t], 1e-12))
                step(dve.reciprocal(kss[:, t], kss[:, t]))
                step(TT(heads(kk), heads(kk), kss[:, t].unsqueeze(2).to_broadcast([P, R_HEADS, R_HEAD]), ALU.mult))
                step(TT(a_, a_, kk, ALU.mult))
                dve.wait_ge(s_cd, t + 1)
                TT(tmp, acc[:, 2:4].rearrange("p a b -> p (a b)"), logd, ALU.subtract).then_inc(s_cp, 1)
                dve.wait_ge(s_en, t + 1)
                STT(kk, kk, -1.0, tmp, ALU.mult, ALU.mult).then_inc(s_kd, 1)
                TT(a_, a_, logd, ALU.mult)
                TT(k_, k_, logd, ALU.mult)
                dve.wait_ge(s_ep, t + 1)
                TT(r_, r_, tmp, ALU.mult).then_inc(s_el, 1)

            b4 = lambda k: bank(k).rearrange("p (j c) -> p j c", j=4)
            m4 = lambda m: m.unsqueeze(1).to_broadcast([P, 4, P])
            for n, (t, q) in enumerate(PAIRS):
                for u in range(2):
                    B = 4 * u
                    g_wait(dve, n, "turned", u, 0)
                    dve.tensor_copy(S_(u, sAT)[0:64], b4(B)[0:64])
                    dve.tensor_copy(S_(u, sBT)[0:64], b4(B + 1)[0:64]).then_inc(g_ve, 1)
                for u in range(2):
                    B = 4 * u
                    g_wait(dve, n, "pairs", u, 0)
                    TT(S_(u, sD), b4(B), m4(lower16), ALU.mult)
                    TT(S_(u, sL), b4(B), m4(lower_rest), ALU.mult)
                    step(TT(S_(u, sDT), b4(B + 1), m4(upper16), ALU.mult))
                    TT(S_(u, sX), S_(u, sDT), m4(ident), ALU.add)
                    TT(S_(u, sAK), b4(B + 2), m4(upper), ALU.mult)
                    TT(S_(u, sRB), b4(B + 3), m4(tri), ALU.mult).then_inc(g_ve, 1)
                for u in range(2):
                    g_wait(dve, n, "square", u, 0)
                    TT(S_(u, sRK), b4(4 * u), m4(tri), ALU.mult).then_inc(g_ve, 1)
                for name in ("fourth", "eighth", "inverse"):
                    for u in range(2):
                        g_wait(dve, n, name, u, 0)
                        TT(S_(u, sX), b4(4 * u), S_(u, sX), ALU.add).then_inc(g_ve, 1)
                for u in range(2):
                    g_wait(dve, n, "solve0", u, 0)
                    dve.tensor_copy(S_(u, sDT), b4(4 * u + 2)).then_inc(g_ve, 1)
                for name in ("solve1", "solve2", "solve3"):
                    for u in range(2):
                        g_wait(dve, n, name, u, 0)
                        g_wait(dve, n, "solve0", u, 2)
                        TT(S_(u, sR), b4(4 * u + 3), S_(u, sY0), ALU.add).then_inc(g_ve, 1)
                for c in range(2):
                    rows = slice(64 * c, 64 * c + 64)
                    for u in range(2):
                        g_wait(dve, n, f"sa{c}", u, 0)
                        TT(S_(u, sKT)[rows, :, 0:64], b4(4 * u + 2)[rows, :, 0:64], S_(u, sR)[rows, :, 64:128],
                           ALU.add).then_inc(g_ve, 1)
                    for u in range(2):
                        g_wait(dve, n, f"state{c}", u, 0)
                        st = state[0:64, (q + u) * 256:(q + u + 1) * 256].rearrange("p (j v) -> p j v", j=4)
                        step(TT(st, st, b4(4 * u + 3)[0:64, :, 0:64], ALU.add))
                        dec = decayC[0:64, t, 4 * (q + u):4 * (q + u) + 4, c:c + 1].to_broadcast([64, 4, 64])
                        TT(st, st, dec, ALU.mult).then_inc(g_ve, 1)
            for t in range(TILES):
                nk = (t + 1) * P
                sc = score[:, t, 0:nk]
                step(dve.tensor_copy(sc, causal[:, t, META:META + nk]))
                for i in range(I_HEADS // 2):
                    m = t * (I_HEADS // 2) + i
                    dve.wait_ge(s_rel, m + 1)
                    for j in range(2):
                        last = STT(sc, rel[:, m % 4, j, 0:nk], p[:, t, WI0 + 2 * i + j:WI0 + 2 * i + j + 1], sc,
                                   ALU.mult, ALU.add)
                        if j == 0:
                            step(last)
                    last.then_inc(s_acc2, 1)
                    dve.wait_ge(s_acc2, m + 1)
                if t == TILES - 1:
                    dve.wait_ge(s_yr0, 1)
                    dve.reciprocal(yst[:, 1], yst[:, 1]).then_inc(s_ysd, 1)
                src = sc
                for r in range(TOPK // 8):
                    step(dve.max(m8, src))
                    step(dve.match_replace(left[:, 0:nk], m8, src, TAKEN))
                    src = left[:, 0:nk]
                un = unsel[:, t, 0:nk]
                step(TS(un, left[:, 0:nk], TAKEN / 2, NEG, ALU.is_gt, ALU.mult))
                step(TT(un, un, causal[:, t, META:META + nk], ALU.add))

            def attend(m0, n, prepare, finish):
                for m in range(m0, m0 + n + 3):
                    if m < m0 + n:
                        dve.wait_ge(a_S, m + 1)
                        if m >= 3:
                            dve.wait_ge(a_T, m - 2)
                            dve.wait_ge(a_pr, m - 2)
                        prepare(m)
                    if m0 <= m - 3:
                        dve.wait_ge(a_O, m - 2)
                        finish(m - 3)

            def finish_of(dst):
                def go(m):
                    step(dve.reciprocal(pinv[:, m % 4], psums[:, m % 4]))
                    TT(dst(m), bank(5 + m % 2)[:, 0:2 * P].rearrange("p (j d) -> p j d", j=2),
                       pinv[:, m % 4].unsqueeze(2).to_broadcast([P, 2, P]), ALU.mult).then_inc(a_done, 1)
                return go

            def dsa_prepare(m):
                t = (m - M_DSA) // 4
                nk = (t + 1) * P
                pr = prob[:, m % 3, 0:2 * nk].rearrange("p (j s) -> p j s", j=2)
                step(TT(pr, bank(m % 3)[:, 0:2 * nk].rearrange("p (j s) -> p j s", j=2),
                        unsel[:, t, 0:nk].unsqueeze(1).to_broadcast([P, 2, nk]), ALU.add))
                RED(nmax[:, m % 3], pr, AX, ALU.max, negate=True).then_inc(a_sm, 1)

            def dsa_out(m):
                t, i = (m - M_DSA) // 4, (m - M_DSA) % 4
                return p[:, t, Q0 + 2 * i * P:Q0 + 2 * (i + 1) * P].rearrange("p (j d) -> p j d", j=2)
            attend(M_DSA, 8, dsa_prepare, finish_of(dsa_out))


            def add_to_h(g, after={}):
                def body(i):
                    for c in range(g.per_body):
                        chunk_done(dve, g, c, i)
                        for t in range(TILES):
                            k = 2 * (c % 2) + t
                            cols = h[:, t, bass.ds(i * (g.per_body * CHUNK) + c * CHUNK, CHUNK)]
                            TT(cols, bank(k), cols, ALU.add).then_inc(acc_free[k], 1)
                        if c in after:
                            after[c]()
                loop(dve, g.bodies, body)

            rest_turned("mixed", xT, None)
            add_to_h(G["mix"])
            norm_scale("cross", 1e-5, src=rows_of_h)
            rest_turned("cross", xT, 2)

            def cross_prepare(m):
                RED(nmax[:, m % 3], bank(m % 3).rearrange("p (j s) -> p j s", j=2), AX, ALU.max, negate=True
                    ).then_inc(a_sm, 1)

            def cross_out(m):
                t, i = (m - M_CROSS) // 2, (m - M_CROSS) % 2
                return co[:, t, 2 * i * P:2 * (i + 1) * P].rearrange("p (j d) -> p j d", j=2)
            attend(M_CROSS, 4, cross_prepare, finish_of(cross_out))
            rest_turned("o", xT, None, slabs=C_W // P)
            add_to_h(G["cross_o"])
            norm_scale("mlp", 1e-5, src=rows_of_h)
            rest_turned("mlp", xT, 3)
            hid_hi, hid_lo = (x.rearrange("p s c -> p (s c)") for x in hidT)
            for half in range(2):
                g = G[f"up{half}"]

                def body(i):
                    for c in range(g.per_body):
                        chunk_done(dve, g, c, i)
                        for f in range(4):
                            b = 4 * (c % 2) + f
                            dve.tensor_scalar_max(relu_now[:, f * SEQ:(f + 1) * SEQ], bank(b)[:, 0:SEQ], 0.0
                                                  ).then_inc(acc_free[b], 1)
                        dve.drain()
                        TT(square_now, relu_now, relu_now, ALU.mult)
                        dve.drain()
                        cols = bass.ds(i * (8 * SEQ) + c * (4 * SEQ), 4 * SEQ)
                        dve.tensor_copy(hid_hi[:, cols], square_now)
                        dve.drain()
                        TT(hid_lo[:, cols], square_now, hid_hi[:, cols].bitcast(FP32), ALU.subtract).then_inc(s_hid, 1)
                        dve.drain()
                loop(dve, g.bodies, body)
                if half == 0:
                    add_to_h(G["down0"])
            norm_scale("meta", 1e-6, META)
            add_to_h(G["down1"], {0: lambda: rest_turned("meta", xT, 4, META, 1, off=0)})
            norm_scale("final", 1e-5, src=rows_of_h, xn=at(base, TILES, D))
            dve.wait_ge(s_fgain, 16)
            dve.wait_ge(s_rstd, norm_no["final"] + 1)
            for t in range(TILES):
                STT(h[:, t], h[:, t], var[:, t:t + 1], final_gain, ALU.mult, ALU.mult).then_inc(s_fin, 1)

            norm_scale("mix2", 1e-6, src=rows_of_h, xn=xn2)
            rest_turned("mix2", xT, 4)
            dve.wait_ge(s_c2, 1)
            step(TS(seen, strict, NEG / 2, None, ALU.is_gt))
            step(dve.tensor_scalar_mul(head_gains[:, 0:1], head_gains[:, 0:1], HEAD2 ** -0.5))
            for r, (x, n, sq) in enumerate(FOX_ROUNDS):
                for k in range(8):
                    if r < 2:
                        dve.wait_ge(acc_free[k], G["fox_kv"].used0[k] + r + 1)
                if r == 2:
                    dve.wait_ge(s_fp, 1)
                TT(sq[:, 0:n], x, x, ALU.mult).then_inc(s_fs, 1)

            def fox_norm(r):
                x, n, sq = FOX_ROUNDS[r]
                dve.wait_ge(s_fr, r + 1)
                step(dve.reciprocal(fox_root[:, 0:n], fox_root[:, 0:n]))
                STT(x, x, head_gains[:, min(r, 1):min(r, 1) + 1], fox_root[:, 0:n], ALU.mult, ALU.mult).then_inc(s_fn, 1)

            dve.wait_ge(s_lf1, 1)
            lf = logf[0:HEADS2]
            step(STT(lf[:, 2], lf[:, 0], 0.0, lf[:, 1], ALU.min, ALU.subtract))
            step(dve.tensor_tensor_scan(lf[:, 0], lf[:, 2], lf[:, 2], 0.0, ALU.add, ALU.bypass))
            dve.tensor_scalar_mul(lf[:, 1], lf[:, 0], -1.0).then_inc(s_lf2, 1)
            for r in range(3):
                fox_norm(r)
            dve.wait_ge(s_ct, 1)
            dve.tensor_copy(cumf, bank(5)[:, 0:TILES * HEADS2].rearrange("p (t h) -> p t h", t=TILES)).then_inc(s_cc, 1)

            of = lambda m: ((m - M_TWO) // 16, (m - M_TWO) % 2, (m - M_TWO) % 16 // 2)
            nk2 = lambda m: META + ((m - M_TWO) // 16 + 1) * P

            def two_prepare(m):
                t, fox, hd = of(m)
                z = bank(m % 3)[:, 0:nk2(m)]
                if fox:
                    pr = prob2[:, m % 3, 0:nk2(m)]
                    step(STT(pr, z, cumf[:, t, hd:hd + 1], causal[:, t, 0:nk2(m)], ALU.add, ALU.add))
                    RED(nmax[:, m % 3, 0:1], pr, AX, ALU.max, negate=True).then_inc(a_sm, 1)
                    return
                a, b, c = (stick[:, m % 3, k, 0:nk2(m)] for k in range(3))
                dve.wait_ge(s_l, (m - M_TWO) // 2 + 1)
                step(STT(b, z, 0.0, a, ALU.max, ALU.add))
                step(dve.tensor_tensor_scan(c[:, ::-1], b[:, ::-1], seen[:, t, 0:nk2(m)][:, ::-1], 0.0, ALU.add, ALU.mult))
                step(TT(b, z, c, ALU.subtract))
                TT(b, b, strict[:, t, 0:nk2(m)], ALU.add).then_inc(a_sm, 1)

            def two_finish(m):
                t, fox, hd = of(m)
                dst = merged[:, t, fox * W2 + hd * P:fox * W2 + (hd + 1) * P]
                src = bank(5 + m % 2)[:, 0:P]
                if m in (M_TWO + 8, M_TWO + 12):
                    gates = fgate[:, (m - M_TWO) // 4 - 2]
                    step(dve.tensor_scalar_add(gates, gates, 1.0))
                    step(dve.reciprocal(gates, gates))
                if fox:
                    step(dve.reciprocal(pinv[:, m % 4, 0:1], psums[:, m % 4, 0:1]))
                    TS(dst, src, pinv[:, m % 4, 0:1], None, ALU.mult).then_inc(a_done, 1)
                else:
                    dve.tensor_copy(dst, src).then_inc(a_done, 1)

            attend(M_TWO, 32, two_prepare, two_finish)
            norm_scale("heads2", 1e-6, P, W2)
            dve.wait_ge(s_rstd, norm_no["heads2"] + 1)
            for t in range(TILES):
                TS(merged[:, t, 0:W2], merged[:, t, 0:W2], var[:, 2 * t:2 * t + 1], None, ALU.mult).then_inc(s_mg, 1)
                STT(merged[:, t, W2:D], merged[:, t, W2:D], var[:, 2 * t + 1:2 * t + 2], fgate[:, t], ALU.mult, ALU.mult
                    ).then_inc(s_mg, 1)
            rest_turned("merged", xT, 5)
            add_to_h(G["out2"])
            norm_scale("ffn", 1e-6, src=rows_of_h, xn=xn3)
            rest_turned("ffn", xT, 6)
            dve.wait_ge(s_erow, 32)
            dve.wait_ge(s_xn, xn0["ffn"] + 1)
            dve.wait_ge(s_xd, xd0["ffn"] + 1)
            for t in range(TILES):
                TT(hb[:, t], xn3[:, t], gain_row, ALU.mult).then_inc(s_hb, 1)
            b1 = best1.bitcast(FP32)
            i1 = bestf.bitcast(U32)
            jn = picked[:, 0].bitcast(U32)
            hi, lo = picked[:, 1].bitcast(U32), picked[:, 2].bitcast(U32)
            step(dve.memset(iota16[:, 0:1], 0.0))
            for k in range(1, E_TOP):
                step(dve.memset(iota16[:, k:k + 1], float(k)))

            def best16(val, idx, src):
                step(dve.max(val[:, 0:8], src))
                step(dve.max_index(idx[:, 0:8], val[:, 0:8], src))
                w = work1[:, 0:src.shape[-1]]
                step(dve.match_replace(w, val[:, 0:8], src, TAKEN))
                step(dve.max(val[:, 8:16], w))
                step(dve.max_index(idx[:, 8:16], val[:, 8:16], w))

            cw = lambda t: coef[:, t].rearrange("p (h k) -> p h k", h=E_HEADS)
            pair = best1.rearrange("p (h q) a -> p h q a", q=2)
            lists = bestf.rearrange("p (h q) a -> p h q a", q=2)

            def choose(t, c):
                hs, ks, js = slice(2 * c, 2 * c + 2), slice(4 * c, 4 * c + 4), slice(2 * c * E_TOP, 2 * (c + 1) * E_TOP)
                shape = [P, 2, E_TOP, E_TOP]
                rows = hot[:, js]
                cand = rows.rearrange("p (h a) b -> p h a b", h=2)
                flat = rows.rearrange("p a b -> p (a b)")
                for k in range(4 * c, 4 * c + 4):
                    best16(best1[:, k], i1[:, k], scores[:, t, k * N_KEYS:(k + 1) * N_KEYS])
                step(TT(cand, pair[:, hs, 0].unsqueeze(3).to_broadcast(shape), pair[:, hs, 1].unsqueeze(2).to_broadcast(shape), ALU.add))
                for e in range(2):
                    j = (2 * c + e) * E_TOP
                    best16(best2[:, t, 2 * c + e], jn[:, j:j + E_TOP], flat[:, e * 256:(e + 1) * 256])
                ins = TT(cw(t)[:, hs], best2[:, t, hs], best2[:, t, hs, 0:1].to_broadcast([P, 2, E_TOP]), ALU.subtract)
                if c == 3:
                    ins.then_inc(s_bs, 1)
                TS(hi[:, js], jn[:, js], 4, None, ALU.logical_shift_right)
                TS(lo[:, js], jn[:, js], 15, None, ALU.bitwise_and)
                step(dve.tensor_copy(bestf[:, ks], i1[:, ks]))
                step(dve.tensor_copy(picked[:, 1:3, js], picked[:, 1:3, js].bitcast(U32)))
                for q_ in range(2):
                    at_ = picked[:, 1 + q_, js].rearrange("p (h k) -> p h k", h=2).unsqueeze(3).to_broadcast(shape)
                    step(TT(cand, at_, iota16.unsqueeze(1).unsqueeze(1).to_broadcast(shape), ALU.is_equal))
                    step(TT(cand, cand, lists[:, hs, q_].unsqueeze(2).to_broadcast(shape), ALU.mult))
                    step(RED(picked[:, 1 + q_, js], rows, AX, ALU.add))
                STT(experts[:, t, js], picked[:, 1, js], float(N_KEYS), picked[:, 2, js], ALU.mult, ALU.add).then_inc(s_ix0, 1)
                dve.wait_ge(s_ix0, 5 * t + c + 1)
                if c == 3:
                    dve.tensor_copy(experts[:, t, P:P + 4], experts[:, t, 0:4]).then_inc(s_ix0, 1)

            per = P // 16

            def dot_products(t, i):
                for n in range(4):
                    dve.wait_ge(rows_full[n], i * 64 + (t * per + 1) * 64)
                    for j in range(4):
                        last = dve.tensor_tensor_reduce(out=junk, in0=rows_buf[4 * n + j], in1=hb[:, t], scale=1.0, scalar=0.0,
                                                        op0=ALU.mult, op1=ALU.add, accum_out=dots_now[:, 4 * n + j:4 * n + j + 1])
                        if j == 3:
                            last.then_inc(rows_used[n], 1)
                        dve.drain()
                dve.tensor_copy(dots[:, t, bass.ds(i * 16, 16)], dots_now)
                dve.drain()

            for c in range(4):
                dve.wait_ge(s_sc, c + 1)
                choose(0, c)
            assert per == 8
            for i in range(per):
                if i % 2 == 0:
                    choose(1, i // 2)
                dot_products(0, i)
            dve.nop().then_inc(s_dot, 1)
            for t in range(TILES):
                dve.wait_ge(s_be, t + 1)
                step(RED(esum[:, t], cw(t), AX, ALU.add))
                step(dve.reciprocal(esum[:, t], esum[:, t]))
                step(TT(cw(t), cw(t), esum[:, t].unsqueeze(2).to_broadcast([P, E_HEADS, E_TOP]), ALU.mult))
            with dve.Fori(0, per) as i:
                dot_products(1, i)
            dve.nop().then_inc(s_dot, 1)
            dve.wait_ge(s_gelu, 1)
            step(TT(coef, coef, dots, ALU.mult))
            for t in range(TILES):
                with dve.Fori(0, per) as i:
                    dve.tensor_copy(coef_now, coef[:, t, bass.ds(i * 16, 16)])
                    dve.drain()
                    for n in range(4):
                        dve.wait_ge(rows_full[n], i * 64 + ((TILES + t) * per + 1) * 64)
                        for j in range(4):
                            last = STT(h[:, t], rows_buf[4 * n + j], coef_now[:, 4 * n + j:4 * n + j + 1], h[:, t],
                                       ALU.mult, ALU.add)
                            if j == 3:
                                last.then_inc(rows_used[n], 1)
                            dve.drain()

        @block.tensor
        def _(pe):
            for k in range(8):
                pe.sem_inc(acc_free[k], 1)
            pe.sem_inc(slab_used, PARTS)

            def product(g, x, before={}):
                def body(i):
                    for c in range(g.per_body):
                        width = g.widths[c]
                        banks = range(2 * (c % 2), 2 * (c % 2) + 2) if g.tok else range(4 * (c % 2), 4 * (c % 2) + 4)
                        if (c, 0) in before:
                            before[c, 0]()
                        for b in banks:
                            n = sum(1 for d in range(c) if d % 2 == c % 2)
                            pe.wait_ge(acc_free[b], i * g.uses(b) + g.used0[b] + n + 1)
                        for s in range(g.slabs):
                            if s and (c, s) in before:
                                before[c, s]()
                            pe.wait_ge(lo_ready, g.slab(i, c, s) + 1)
                            k = s % PARTS
                            for n, (wp, xp) in enumerate(((w_hi, x[0]), (w_hi, x[1]), (w_lo, x[0]))):
                                kw = dict(start=s == 0 and n == 0, stop=s == g.slabs - 1 and n == 2)
                                if g.tok:
                                    for t in range(TILES):
                                        last = pe.matmul(bank(banks[t])[:, 0:width],
                                                         xp[:, s, g.lo + t * P:g.lo + (t + 1) * P],
                                                         wp[:, k, 0:width], **kw)
                                else:
                                    for f in range(4):
                                        last = pe.matmul(bank(banks[f])[:, 0:g.hi - g.lo], wp[:, k, f * P:(f + 1) * P],
                                                         xp[:, s, g.lo:g.hi], **kw)
                            last.then_inc(slab_used, 1)
                loop(pe, g.bodies, body)

            def turn(name, is_norm, block_of, rows=P, tiles=TILES, slabs=SLABS, some=None):
                for t in some or range(tiles):
                    group = g0[name] + t * (slabs // 4)
                    if is_norm:
                        if t == 0:
                            pe.wait_ge(s_xn, xn0[name] + 1)
                        else:
                            pe.wait_ge(s_xd, xd0[name] + 1)
                    for k in range(slabs // 4):
                        if group >= 4:
                            pe.wait_ge(s_xT, group - 3)
                        for j in range(4):
                            last = pe.transpose(bank(4 + group % 4)[:, j * rows:(j + 1) * rows],
                                                block_of(t, 4 * k + j), ident[0:rows, 0:rows])
                        last.then_inc(s_tr, 1)
                        group += 1

            xn_block = lambda t, s: xn[:, t, s * P:(s + 1) * P]
            pe.wait_ge(s_const, 1)
            turn("x", True, xn_block)
            pe.wait_ge(s_xT, 8)
            mem_block = lambda t, s: mem[:, t, s * P:(s + 1) * P]
            product(G["in0"], xT, {(1, 2): lambda: turn("mem", True, mem_block, some=(0,)),
                                   (1, 7): lambda: turn("mem", True, mem_block, some=(1,))})
            pe.wait_ge(s_xT, 16)
            product(G["cross_k"], memT)
            product(G["cross_v"], memT)
            product(G["in"], xT)
            product(G["in_end"], xT)

            for k in range(4):
                pe.wait_ge(acc_free[k], G["mix"].used0[k] + 1)
            for t in range(TILES):
                pe.wait_ge(s_tanh, t + 1)
                pe.transpose(bank(4)[:, t * P:(t + 1) * P], p[:, t, XW0:XW0 + P], ident)
                pe.wait_ge(s_sig, t + 1)
                pe.transpose(bank(5)[:, t * P:(t + 1) * P], p[:, t, XG0:XG0 + P], ident)
                last = pe.transpose(bank(6)[0:LORA_G - P, t * P:(t + 1) * P], p[:, t, XG0 + P:XG0 + LORA_G], ident)
            last.then_inc(s_lt, 1)
            pe.wait_ge(s_lT, 1)
            pe.wait_ge(s_lora, 64)
            for t in range(TILES):
                tok = slice(t * P, (t + 1) * P)
                if t:
                    pe.wait_ge(s_ep, t)
                for c in range(2):
                    cols = slice(c * CHUNK, (c + 1) * CHUNK)
                    last = pe.matmul(bank(4 + c), loraT[0:LORA_W, 0, tok], lora_up[0:LORA_W, 0, cols], start=True, stop=True)
                last.then_inc(s_zd, 1)
                for c in range(2):
                    cols = slice(c * CHUNK, (c + 1) * CHUNK)
                    last = pe.matmul(bank(6 + c), loraT[LORA_W:P, 0, tok], lora_up[LORA_W:P, 0, cols], start=True, stop=True)
                last.then_inc(s_ad, 1)
                if t:
                    pe.wait_ge(s_gate, t)
                for c in range(2):
                    cols = slice(c * CHUNK, (c + 1) * CHUNK)
                    pe.matmul(bank(c), loraT[:, 1, tok], lora_up[:, 1, cols], start=True, stop=False)
                    last = pe.matmul(bank(c), loraT[0:LORA_G - P, 2, tok], lora_up[0:LORA_G - P, 2, cols], start=False, stop=True)
                last.then_inc(s_gd, 1)
                pe.wait_ge(s_ld, t + 1)
                for c in range(2):
                    pe.matmul(bank(2 + c), tri, logd[:, c * CHUNK:(c + 1) * CHUNK], start=True, stop=True)
                for hd in range(R_HEADS):
                    last = pe.matmul(bank(6)[0:R_HEAD, 2 * hd:2 * hd + 2], logd[:, hd * R_HEAD:(hd + 1) * R_HEAD], halves,
                                     start=hd == 0, stop=True, skip_group_check=True)
                last.then_inc(s_cd, 1)
            pe.wait_ge(s_el, TILES)
            for n, (t, q) in enumerate(PAIRS):
                b4 = lambda k: bank(k).rearrange("p (j c) -> p j c", j=4)
                V = lambda u, j: p[:, t, 2 * R_W + (q + u) * 256 + j * 64:2 * R_W + (q + u) * 256 + (j + 1) * 64]
                K = lambda u, j: p[:, t, R_W + (q + u) * 256 + j * 64:R_W + (q + u) * 256 + (j + 1) * 64]
                R = lambda u, j: p[:, t, (q + u) * 256 + j * 64:(q + u) * 256 + (j + 1) * 64]
                AK_ = lambda u, j: key_t[:, t, (q + u) * 256 + j * 64:(q + u) * 256 + (j + 1) * 64]
                BT_ = lambda u, j: beta_t[:, t, (q + u) * 256 + j * 64:(q + u) * 256 + (j + 1) * 64]
                S0 = lambda u, j: state[0:64, (q + u) * 256 + j * 64:(q + u) * 256 + (j + 1) * 64]

                def mm(b, j, lhsT, rhs, start=True, stop=True, rows=slice(0, P), width=P, check=False):
                    return pe.matmul(b4(b)[rows, j, 0:width], lhsT, rhs, start=start, stop=stop, skip_group_check=check)

                def after(prev_stage, u):
                    g_wait(pe, n, prev_stage, u, 1)
                    g_wait(pe, n, prev_stage, u, 2)

                for u in range(2):
                    if n:
                        g_wait(pe, n - 1, "state1", u, 1)
                        g_wait(pe, n - 1, "y", u, 2)
                    for b, src in enumerate((AK_, BT_, K, R)):
                        for j in range(4):
                            last = pe.transpose(b4(4 * u + b)[0:64, j], src(u, j), ident)
                    last.then_inc(g_pe, 1)
                for u in range(2):
                    after("turned", u)
                    at_, bt, kt, rt = (S_(u, x) for x in (sAT, sBT, sKT, sRT))
                    for j in range(4):
                        mm(4 * u, j, at_[0:64, j], bt[0:64, j])
                        mm(4 * u + 1, j, bt[0:64, j], at_[0:64, j])
                        mm(4 * u + 2, j, kt[0:64, j], at_[0:64, j])
                        last = mm(4 * u + 3, j, bt[0:64, j], rt[0:64, j])
                    last.then_inc(g_pe, 1)
                for u in range(2):
                    after("pairs", u)
                    for j in range(4):
                        mm(4 * u, j, S_(u, sKT)[0:64, j], S_(u, sRT)[0:64, j])
                        mm(4 * u + 1, j, S_(u, sDT)[:, j], S_(u, sD)[:, j])
                        mm(4 * u + 2, j, S_(u, sD)[:, j], S_(u, sDT)[:, j])
                        last = mm(4 * u + 3, j, S_(u, sAK)[:, j], V(u, j), width=64)
                    last.then_inc(g_pe, 1)
                for u in range(2):
                    after("square", u)
                    for j in range(4):
                        mm(4 * u, j, S_(u, sKT)[:, j], S_(u, sX)[:, j])
                        mm(4 * u + 1, j, S_(u, sBT)[:, j], S_(u, sKT)[:, j])
                        last = mm(4 * u + 2, j, S_(u, sKT)[:, j], S_(u, sBT)[:, j])
                    last.then_inc(g_pe, 1)
                for u in range(2):
                    after("fourth", u)
                    for j in range(4):
                        mm(4 * u, j, S_(u, sD)[:, j], S_(u, sX)[:, j])
                        last = mm(4 * u + 1, j, S_(u, sDT)[:, j], S_(u, sD)[:, j])
                    last.then_inc(g_pe, 1)
                for u in range(2):
                    after("eighth", u)
                    for j in range(4):
                        last = mm(4 * u, j, S_(u, sKT)[:, j], S_(u, sX)[:, j])
                    last.then_inc(g_pe, 1)
                for u in range(2):
                    after("inverse", u)
                    for j in range(4):
                        mm(4 * u + 1, j, S_(u, sX)[:, j], S_(u, sR)[:, j])
                        last = mm(4 * u + 2, j, S_(u, sL)[:, j], S_(u, sX)[:, j])
                    last.then_inc(g_pe, 1)
                for a, b in (("solve0", "solve1"), ("solve1", "solve2"), ("solve2", "solve3")):
                    for u in range(2):
                        after(a, u)
                        y = S_(u, sY0) if a == "solve0" else S_(u, sR)
                        for j in range(4):
                            last = mm(4 * u + 3, j, S_(u, sDT)[:, j], y[:, j])
                        last.then_inc(g_pe, 1)
                for u in range(2):
                    after("solve3", u)
                    for j in range(4):
                        last = pe.transpose(b4(4 * u)[0:64, j], S_(u, sR)[:, j, 0:64], ident)
                    last.then_inc(g_pe, 1)
                for c in range(2):
                    rows = slice(64 * c, 64 * c + 64)
                    for u in range(2):
                        if c == 0:
                            after("w_turned", u)
                            for j in range(4):
                                mm(4 * u + 1, j, S_(u, sRK)[:, j], V(u, j), start=j == 0, stop=False, width=64, check=True)
                        else:
                            after("state0", u)
                        for j in range(4):
                            last = mm(4 * u + 2, j, S_(u, sAT)[0:64, j, rows], S0(u, j), rows=rows, width=64)
                        last.then_inc(g_pe, 1)
                    for u in range(2):
                        for j in range(4):
                            mm(4 * u + 1, j, S_(u, sRT)[0:64, j, rows], S0(u, j), start=False, stop=False, rows=rows,
                               width=64, check=True)
                        after(f"sa{c}", u)
                        for j in range(4):
                            mm(4 * u + 3, j, BT_(u, j)[rows], S_(u, sKT)[rows, j, 0:64], start=True, stop=False,
                               rows=slice(0, 64), width=64)
                            last = mm(4 * u + 3, j, K(u, j)[rows], V(u, j)[rows], start=False, stop=True,
                                      rows=slice(0, 64), width=64)
                        last.then_inc(g_pe, 1)
                for u in range(2):
                    for j in range(4):
                        last = mm(4 * u + 1, j, S_(u, sRB)[:, j], S_(u, sKT)[:, j, 0:64], start=False, stop=j == 3,
                                  width=64, check=True)
                    last.then_inc(g_pe, 1)

            for u in range(2):
                g_wait(pe, len(PAIRS) - 1, "state1", u, 1)
                g_wait(pe, len(PAIRS) - 1, "y", u, 2)
            pe.wait_ge(s_rope, TILES)
            for t in range(TILES):
                pe.transpose(bank(0)[:, t * P:(t + 1) * P], keyI[:, t], ident)
                for k in range(A_KV):
                    last = pe.transpose(bank(1)[:, k * SEQ + t * P:k * SEQ + (t + 1) * P],
                                        p[:, t, K0 + k * P:K0 + (k + 1) * P], ident)
            last.then_inc(s_kturn, 1)
            for t in range(TILES):
                if t:
                    pe.wait_ge(s_qT2, t)
                for k, col in ((2, QI0), (4, Q0)):
                    for i in range(8):
                        last = pe.transpose(bank(k + i // 4)[:, (i % 4) * P:(i % 4 + 1) * P],
                                            p[:, t, col + i * P:col + (i + 1) * P], ident)
                last.then_inc(s_qturn, 1)
                pe.wait_ge(s_kT2, 1)
                pe.wait_ge(s_qT2, t + 1)
                nk = (t + 1) * P
                for i in range(I_HEADS // 2):
                    m = t * (I_HEADS // 2) + i
                    if m >= 2:
                        pe.wait_ge(s_rel, m - 1)
                    for j in range(2):
                        half = slice(j * I_HEAD, (j + 1) * I_HEAD)
                        last = pe.matmul(bank(6 * (m % 2) + j)[:, 0:nk], qiT[half, t, i], kiT[half, 0:nk],
                                         start=True, stop=True)
                    last.then_inc(s_ix, 1)

            def attend(m0, n, heads_n, scores_of, blocks, values, pr_of, pT_of):
                for m in range(m0, m0 + n + 3):
                    if m < m0 + n:
                        if m >= 3:
                            pe.wait_ge(a_pr, m - 2)
                        scores_of(m).then_inc(a_S, 1)
                    if m0 <= m - 2 < m0 + n:
                        k = m - 2
                        pe.wait_ge(a_pr, k + 1)
                        if k >= 2:
                            pe.wait_ge(a_PT, k - 1)
                        slot = 0
                        for j in range(heads_n):
                            for off, size in blocks(k):
                                last = pe.transpose(bank(3 + k % 2)[0:size, slot * P:(slot + 1) * P],
                                                    pr_of(k, j)[:, off:off + size], ident)
                                slot += 1
                        last.then_inc(a_T, 1)
                    if m0 <= m - 3:
                        k = m - 3
                        pe.wait_ge(a_PT, k + 1)
                        if k >= 2:
                            pe.wait_ge(a_done, k - 1)
                        nb = len(blocks(k))
                        for j in range(heads_n):
                            for n_, (off, size) in enumerate(blocks(k)):
                                slot = j * nb + n_
                                last = pe.matmul(bank(5 + k % 2)[:, j * P:(j + 1) * P],
                                                 pT_of(k)[0:size, slot * P:(slot + 1) * P], values(k, j, n_),
                                                 start=n_ == 0, stop=n_ == nb - 1)
                        last.then_inc(a_O, 1)

            def dsa_scores(m):
                t, i = (m - M_DSA) // 4, (m - M_DSA) % 4
                nk = (t + 1) * P
                for j in range(2):
                    hd = 2 * i + j
                    last = pe.matmul(bank(m % 3)[:, j * nk:(j + 1) * nk], qT[:, t, hd], kT[:, hd // (A_HEADS // A_KV), 0:nk],
                                     start=True, stop=True)
                return last

            def dsa_values(m, j, n_):
                kv = (2 * ((m - M_DSA) % 4) + j) // (A_HEADS // A_KV)
                return p[:, n_, V0 + kv * P:V0 + (kv + 1) * P]

            nk1 = lambda m: ((m - M_DSA) // 4 + 1) * P
            pe.wait_ge(s_rel, I_HEADS)
            attend(M_DSA, 8, 2, dsa_scores, lambda m: [(b * P, P) for b in range((m - M_DSA) // 4 + 1)], dsa_values,
                   lambda m, j: prob[:, m % 3, j * nk1(m):(j + 1) * nk1(m)], lambda m: probT[:, m % 2])
            pe.wait_ge(a_done, M_DSA + 8)
            pe.wait_ge(s_yr, TILES)
            turn("mixed", False, lambda t, s: key_t[:, t, s * P:(s + 1) * P] if s < R_W // P else
                 p[:, t, Q0 + (s - R_W // P) * P:Q0 + (s - R_W // P + 1) * P])
            pe.wait_ge(s_xT, g0["mixed"] + 8)
            product(G["mix"], xT)
            turn("cross", True, xn_block)
            pe.wait_ge(s_xT, g0["cross"] + 8)
            product(G["cross_q"], xT)
            for k in range(4):
                pe.wait_ge(acc_free[k], G["cross_o"].used0[k] + 1)

            def cross_scores(m):
                t, i = (m - M_CROSS) // 2, (m - M_CROSS) % 2
                for j in range(2):
                    last = pe.matmul(bank(m % 3)[:, j * SEQ:(j + 1) * SEQ], cqT[:, 2 * i + j, t * P:(t + 1) * P],
                                     ckT[:, 2 * i + j], start=True, stop=True)
                return last
            attend(M_CROSS, 4, 2, cross_scores, lambda m: [(0, P), (P, P)],
                   lambda m, j, n_: cv[:, n_, (2 * ((m - M_CROSS) % 2) + j) * P:(2 * ((m - M_CROSS) % 2) + j + 1) * P],
                   lambda m, j: prob[:, m % 3, j * SEQ:(j + 1) * SEQ], lambda m: probT[:, m % 2])
            pe.wait_ge(a_done, M_CROSS + 4)
            turn("o", False, lambda t, s: co[:, t, s * P:(s + 1) * P], slabs=C_W // P)
            pe.wait_ge(s_xT, g0["o"] + 2)
            product(G["cross_o"], xT)
            turn("mlp", True, xn_block)
            pe.wait_ge(s_xT, g0["mlp"] + 8)
            for half in range(2):
                product(G[f"up{half}"], xT)
                pe.wait_ge(s_hid, (half + 1) * (FF // CHUNK // 2))
                product(G[f"down{half}"], hidT, {} if half == 0 else {
                    (1, 4): lambda: turn("meta", True, lambda t, s: hmeta_xn[0:META, s * P:(s + 1) * P], META, 1)})
            turn("mix2", True, lambda t, s: xn2[:, t, s * P:(s + 1) * P])
            pe.wait_ge(s_xT, g0["mix2"] + 8)

            def turn_values(v0, v_free):
                for k in range(8):
                    pe.wait_ge(acc_free[k], v_free.used0[k] + 1)
                for n in range(3):
                    if n == 2:
                        pe.wait_ge(s_vr, v0 + 1)
                    for hd in range(HEADS2):
                        b = (4, 6, 4)[n] + hd // 4
                        src = vT[:, hd, META + n * P:META + (n + 1) * P] if n < 2 else vT[:, hd, 0:META]
                        last = pe.transpose(bank(b)[0:src.shape[-1], (hd % 4) * P:(hd % 4 + 1) * P], src, ident)
                    last.then_inc(s_vt, 1)

            product(G["sb_q"], xT)
            product(G["sb_kv"], xT)
            product(G["fox_q"], xT)
            turn_values(0, G["fox_kv"])
            product(G["fox_kv"], xT, {(1, 0): lambda: pe.wait_ge(s_vr, 3)})
            pe.wait_ge(s_meta, 16)
            pe.wait_ge(s_c2, 1)
            pe.wait_ge(acc_free[3], G["fox_gate"].used0[3] + 1)
            for n in range(2):
                for s_ in range(SLABS):
                    last = pe.matmul(bank(3)[0:HEADS2, 0:CTX], w_logit[:, s_], xT[n][:, s_].bitcast(FP32),
                                     start=n == 0 and s_ == 0, stop=n == 1 and s_ == SLABS - 1)
            last.then_inc(s_lg, 1)

            def fox_sums(r):
                x, n, sq = FOX_ROUNDS[r]
                pe.wait_ge(s_fs, r + 1)
                if r:
                    pe.wait_ge(s_fr, r)
                for c in range(0, n, CHUNK):
                    w_ = min(CHUNK, n - c)
                    last = pe.matmul(bank(4 + c // CHUNK)[:, 0:w_], ones, sq[:, c:c + w_], start=True, stop=True)
                last.then_inc(s_fp, 1)

            for k in range(4, 8):
                pe.wait_ge(acc_free[k], G["fox_gate"].used0[k] + 1)
            fox_sums(0)

            def keys_and_logits():
                pe.wait_ge(s_lf0, 1)
                fox_sums(1)
            product(G["fox_gate"], xT, {(1, 0): keys_and_logits})
            fox_sums(2)
            pe.wait_ge(s_lf2, 1)
            for t in range(TILES):
                last = pe.transpose(bank(5)[:, t * HEADS2:(t + 1) * HEADS2], logf[0:HEADS2, 0, META + t * P:META + (t + 1) * P],
                                    ident[0:HEADS2, 0:HEADS2])
            last.then_inc(s_ct, 1)
            pe.wait_ge(s_cc, 1)
            pe.wait_ge(s_fr, 3)
            turn_values(3, G["out2"])
            pe.wait_ge(s_vr, 6)
            for k in range(8):
                pe.wait_ge(acc_free[k], G["out2"].used0[k] + 1)
            pe.wait_ge(s_fn, 3)

            of = lambda m: ((m - M_TWO) // 16, (m - M_TWO) % 2, (m - M_TWO) % 16 // 2)

            def two_scores(m):
                t, fox, hd = of(m)
                nk = META + (t + 1) * P
                z, tok = bank(m % 3)[:, 0:nk], slice(t * P, (t + 1) * P)
                if not fox:
                    return pe.matmul(z, sqT[:, hd, tok], skT[:, hd, 0:nk], start=True, stop=True)
                pe.matmul(z, fqT[:, hd, tok], fkT[:, hd, 0:nk], start=True, stop=False)
                return pe.matmul(z, pick[0:HEADS2, hd], logf[0:HEADS2, 1, 0:nk], start=False, stop=True)

            def two_values(m, j, n_):
                t, fox, hd = of(m)
                cols = slice(hd * P, (hd + 1) * P)
                if n_ == 0:
                    return (fv_meta if fox else sv_meta)[0:META, cols]
                return (fv if fox else sv)[:, n_ - 1, cols]

            attend(M_TWO, 32, 1, two_scores,
                   lambda m: [(0, META)] + [(META + b * P, P) for b in range((m - M_TWO) // 16 + 1)], two_values,
                   lambda m, j: prob2[:, m % 3], lambda m: probT2[:, m % 2])
            pe.wait_ge(s_mg, 2 * TILES)
            turn("merged", False, lambda t, s: merged[:, t, s * P:(s + 1) * P])
            pe.wait_ge(s_xT, g0["merged"] + 8)

            def turn_subkeys():
                pe.wait_ge(s_erow, 32)
                for k in range(4):
                    for j in range(4):
                        last = pe.transpose(bank(4 + k)[:, j * P:(j + 1) * P], subk[:, 4 * k + j], ident)
                    last.then_inc(s_sk, 1)
            product(G["out2"], xT, {(1, 4): turn_subkeys})
            pe.wait_ge(s_skT, 4)
            turn("ffn", True, lambda t, s: xn3[:, t, s * P:(s + 1) * P])
            pe.wait_ge(s_xT, g0["ffn"] + 8)
            g = G["query"]

            def key_scores(c):
                for k in range(4 * (c % 2), 4 * (c % 2) + 4):
                    pe.wait_ge(acc_free[k], g.used0[k] + c // 2 + 2)
                for t in range(TILES):
                    for j in range(4):
                        last = pe.matmul(bank(4 * (c % 2) + t)[:, j * P:(j + 1) * P], pqT[:, 4 * c + j, t * P:(t + 1) * P],
                                         subkT[:, 4 * c + j], start=True, stop=True)
                last.then_inc(s_sp, 1)
            before = {(c + 1, 8): lambda c=c: key_scores(c) for c in range(3)}
            for c in (2, 3):
                before[c, 0] = lambda c=c: pe.wait_ge(s_sc, c - 1)
            product(g, xT, before)
            key_scores(3)


def kernel(**inputs):
    import concourse.bacc as bacc
    from concourse.bass_utils import run_bass_kernel_spmd

    nc = bacc.Bacc("TRN2", target_bir_lowering=False, num_devices=1)
    arrays, dram = {}, {}
    for name, value in inputs.items():
        value = np.ascontiguousarray(value)
        arrays["in_" + name] = value
        dram[name] = nc.dram_tensor("in_" + name, value.shape, mybir.dt.from_np(value.dtype), kind="ExternalInput").ap()
    out = nc.dram_tensor("out_x", (1, SEQ, D), FP32, kind="ExternalOutput").ap()
    build(nc, dram, out)
    result = run_bass_kernel_spmd(nc, [arrays], core_ids=[0])
    return result.results[0]["out_x"]
```
